# Optimizing a Trainium2 kernel written in Bass

```python
import jax, jax.numpy as jnp
from jax import lax
import numpy as np

D_MODEL = 1024
BATCH = 1
SEQ = 1024
DEPTH = 1
DEC_BATCH = 8
DEC_SEQ = 1
PAST_LEN = 256
PAGE_SIZE = 128

HEAD_DIM = 64
DIL_PAIRS = ((128, 1), (512, 4), (2048, 16))
N_DIL = 3
H_G = D_MODEL // 256
N_A_HEADS = N_DIL * H_G
H_B = D_MODEL // 128
A_W = N_A_HEADS * HEAD_DIM
B_W = H_B * HEAD_DIM
N_IN = 3 * A_W + 3 * B_W + 2 * D_MODEL
BLK = 128
Q_BLK = 128
ALIBI_MAX = 8.0
SB_BIAS_INIT = -6.0
N_GROUPS = 4
E_PER = 8
N_EXPERTS = N_GROUPS * E_PER
TOP_K = 2
D_EXPERT = D_MODEL // 2
PLE_DIM = 256
EPS = 1e-6

kernel_name = 'dilated_stickbreak_hmoe_decoder_step'

def rmsnorm(x, g):
    xf = x.astype(jnp.float32)
    y = xf * lax.rsqrt(jnp.mean(xf * xf, axis=-1, keepdims=True) + EPS)
    return (y * g.astype(jnp.float32)).astype(x.dtype)

def alibi_slopes():
    h = jnp.arange(N_A_HEADS, dtype=jnp.float32) + 1.0
    return jnp.exp2(-ALIBI_MAX * h / N_A_HEADS).reshape(N_DIL, H_G)

def project_in(x, g_mix, w_in):
    u = rmsnorm(x, g_mix)
    z = u @ w_in
    cuts = [int(c) for c in np.cumsum([A_W, A_W, A_W, B_W, B_W, B_W, D_MODEL])]
    qa, ka, va, qb, kb, vb, ga, gb = jnp.split(z, cuts, axis=-1)
    lead = x.shape[:2]
    ha = lambda t: t.reshape(*lead, N_DIL, H_G, HEAD_DIM)
    hb = lambda t: t.reshape(*lead, H_B, HEAD_DIM)
    return ha(qa), ha(ka), ha(va), hb(qb), hb(kb), hb(vb), ga, gb

def dilated_prompt(q, k, v, win, dil, slopes):
    B, S, H, hd = q.shape
    w_units = win // dil
    span = dil * BLK
    L = -(-S // span) * span
    NB = L // span
    blocks = lambda t: jnp.pad(t, ((0, 0), (0, L - S), (0, 0), (0, 0))).reshape(B, NB, BLK, dil, H, hd)
    qs, ks, vs = blocks(q), blocks(k), blocks(v)

    def with_prev(t):
        prev = jnp.pad(t[:, :-1], ((0, 0), (1, 0), (0, 0), (0, 0), (0, 0), (0, 0)))
        return jnp.concatenate([prev, t], axis=2)

    kk, vv = with_prev(ks), with_prev(vs)
    s = jnp.einsum('bnirhd,bnjrhd->bnrhij', qs, kk).astype(jnp.float32) * (hd ** -0.5)
    dist = jnp.arange(BLK)[:, None] + BLK - jnp.arange(2 * BLK)[None, :]
    key_unit = jnp.arange(NB)[:, None] * BLK - BLK + jnp.arange(2 * BLK)[None, :]
    valid = (dist >= 0)[None] & (dist <= w_units)[None] & (key_unit >= 0)[:, None, :]
    s = s - slopes[:, None, None] * (dil * dist).astype(jnp.float32)
    s = jnp.where(valid[None, :, None, None], s, -jnp.inf)
    lse = jax.nn.logsumexp(s, axis=-1)
    p = jnp.exp(s - lse[..., None])
    o = jnp.einsum('bnrhij,bnjrhd->bnirhd', p.astype(v.dtype), vv).reshape(B, L, H, hd)[:, :S]
    lse = lse.transpose(0, 1, 4, 2, 3).reshape(B, L, H)[:, :S]
    return o, lse

def dilated_sample(q, k, v, buf, win, dil, slopes):
    WB = buf.shape[1]
    DS = q.shape[1]
    w_units = win // dil
    kk = jnp.concatenate([buf[:, :, 0], k], axis=1)
    vv = jnp.concatenate([buf[:, :, 1], v], axis=1)
    j = jnp.arange(w_units + 1)
    idx = WB + jnp.arange(DS)[:, None] - dil * j[None, :]
    valid = idx >= 0
    idxc = jnp.maximum(idx, 0)
    kg, vg = kk[:, idxc], vv[:, idxc]
    s = jnp.einsum('bqhd,bqjhd->bhqj', q, kg).astype(jnp.float32) * (q.shape[-1] ** -0.5)
    s = s - slopes[:, None, None] * (dil * j).astype(jnp.float32)[None, None, :]
    s = jnp.where(valid[None, None], s, -jnp.inf)
    lse = jax.nn.logsumexp(s, axis=-1)
    p = jnp.exp(s - lse[..., None])
    o = jnp.einsum('bhqj,bqjhd->bqhd', p.astype(v.dtype), vg)
    return o, lse.transpose(0, 2, 1)

def combine_groups(outs):
    o = jnp.stack([r[0] for r in outs], axis=0)
    l = jnp.stack([r[1] for r in outs], axis=0)
    w = jax.nn.softmax(l, axis=0)
    return jnp.sum(w[..., None].astype(o.dtype) * o, axis=0)

def stick_breaking(q, k, v, q_pos, k_pos, bias):
    z = jnp.einsum('bqhd,bkhd->bhqk', q, k).astype(jnp.float32) * (q.shape[-1] ** -0.5)
    z = z + bias.astype(jnp.float32)[None, :, None, None]
    causal = k_pos[None, :] < q_pos[:, None]
    log_1mb = jnp.where(causal, -jax.nn.softplus(z), 0.0)
    suffix = lax.cumsum(log_1mb, axis=3, reverse=True)
    log_a = -jax.nn.softplus(-z) + suffix - log_1mb
    a = jnp.where(causal, jnp.exp(log_a), 0.0)
    return jnp.einsum('bhqk,bkhd->bqhd', a.astype(v.dtype), v)

def sb_prompt(q, k, v, bias):
    B, S, H, hd = q.shape
    nb = S // Q_BLK
    qb = q.reshape(B, nb, Q_BLK, H, hd).transpose(1, 0, 2, 3, 4)
    k_pos = jnp.arange(S)

    def one_block(args):
        qi, n = args
        return stick_breaking(qi, k, v, n * Q_BLK + jnp.arange(Q_BLK), k_pos, bias)

    ob = lax.map(one_block, (qb, jnp.arange(nb)))
    return ob.transpose(1, 0, 2, 3, 4).reshape(B, S, H, hd)

def sb_sample(q, k, v, k_past, v_past, bias):
    P = k_past.shape[1]
    DS = q.shape[1]
    kk = jnp.concatenate([k_past, k], axis=1)
    vv = jnp.concatenate([v_past, v], axis=1)
    return stick_breaking(q, kk, vv, P + jnp.arange(DS), jnp.arange(P + DS), bias)

def merge_out(x, oa, ob, ga, gb, w_oa, w_ob, w_out):
    lead = x.shape[:2]
    ya = oa.reshape(*lead, H_G * HEAD_DIM) @ w_oa
    yb = ob.reshape(*lead, B_W) @ w_ob
    return x + (jax.nn.sigmoid(ga) * ya + jax.nn.sigmoid(gb) * yb) @ w_out

def dispatch_experts(x, expert, weight, w_up, w_gate, w_down):
    n_tok = x.shape[0]
    n_asg = n_tok * TOP_K
    e = expert.reshape(-1)
    tok = jnp.repeat(jnp.arange(n_tok, dtype=jnp.int32), TOP_K)
    w = weight.reshape(-1)
    order = jnp.argsort(e)
    e_s, tok_s, w_s = e[order], tok[order], w[order]
    counts = jnp.bincount(e, length=N_EXPERTS)
    padded = (counts + BLK - 1) // BLK * BLK
    start = jnp.cumsum(counts) - counts
    pstart = jnp.cumsum(padded) - padded
    dest = pstart[e_s] + jnp.arange(n_asg) - start[e_s]
    n_blocks = -(-n_asg // BLK) + N_EXPERTS
    n_rows = n_blocks * BLK
    row_tok = jnp.full((n_rows,), n_tok, jnp.int32).at[dest].set(tok_s)
    row_w = jnp.zeros((n_rows,), x.dtype).at[dest].set(w_s)
    blk_e = jnp.minimum(jnp.searchsorted(pstart + padded, jnp.arange(n_blocks) * BLK, side='right'), N_EXPERTS - 1)
    x_pad = jnp.concatenate([x, jnp.zeros((1, D_MODEL), x.dtype)], axis=0)
    xb = x_pad[row_tok].reshape(n_blocks, BLK, D_MODEL)

    def expert_block(args):
        xi, ei = args
        return (jax.nn.silu(xi @ w_gate[ei]) * (xi @ w_up[ei])) @ w_down[ei]

    yb = lax.map(expert_block, (xb, blk_e)).reshape(n_rows, D_MODEL) * row_w[:, None]
    return jnp.zeros((n_tok + 1, D_MODEL), x.dtype).at[row_tok].add(yb)[:n_tok]

def hier_moe(u, w_rg, b_rg, w_re, b_re, w_up, w_gate, w_down):
    lead = u.shape[:-1]
    x = u.reshape(-1, D_MODEL)
    n_tok = x.shape[0]
    g_logit = (x @ w_rg).astype(jnp.float32) + b_rg.astype(jnp.float32)
    g_idx = jnp.argmax(g_logit, axis=-1)
    g_prob = jnp.take_along_axis(jax.nn.softmax(g_logit, axis=-1), g_idx[:, None], axis=1)
    e_logit = ((x @ w_re).astype(jnp.float32) + b_re.astype(jnp.float32)).reshape(n_tok, N_GROUPS, E_PER)
    e_logit = jnp.take_along_axis(e_logit, g_idx[:, None, None], axis=1)[:, 0]
    top_v, top_i = lax.top_k(e_logit, TOP_K)
    weight = (jax.nn.softmax(top_v, axis=-1) * g_prob).astype(x.dtype)
    expert = g_idx[:, None] * E_PER + top_i
    return dispatch_experts(x, expert, weight, w_up, w_gate, w_down).reshape(*lead, D_MODEL)

def channel_and_ple(x, p, g_moe, w_rg, b_rg, w_re, b_re, w_up, w_gate, w_down, g_ple, w_pg, w_pp):
    x = x + hier_moe(rmsnorm(x, g_moe), w_rg, b_rg, w_re, b_re, w_up, w_gate, w_down)
    gate = jax.nn.sigmoid(rmsnorm(x, g_ple) @ w_pg)
    return x + gate * (p @ w_pp)

def setup_inputs(seed: int = 0) -> dict:
    key = jax.random.key(seed)
    ks = iter(jax.random.split(key, 40))
    nrm = lambda shape, scale: jax.random.normal(next(ks), shape, jnp.float32) * scale
    gain = lambda shape: 1.0 + nrm(shape, 0.02)
    n_pages = PAST_LEN // PAGE_SIZE
    used = DEC_BATCH * n_pages
    n_pool = used + max(1, used // 4)
    page_table = jax.random.permutation(next(ks), n_pool)[:used].reshape(DEC_BATCH, n_pages).astype(jnp.int32)
    return {
        'x_prompt': nrm((BATCH, SEQ, D_MODEL), 1.0),
        'x_sample': nrm((DEC_BATCH, DEC_SEQ, D_MODEL), 1.0),
        'cache_win1': nrm((DEPTH, DEC_BATCH, min(DIL_PAIRS[0][0], PAST_LEN), 2, H_G, HEAD_DIM), 1.0),
        'cache_win2': nrm((DEPTH, DEC_BATCH, min(DIL_PAIRS[1][0], PAST_LEN), 2, H_G, HEAD_DIM), 1.0),
        'cache_win3': nrm((DEPTH, DEC_BATCH, min(DIL_PAIRS[2][0], PAST_LEN), 2, H_G, HEAD_DIM), 1.0),
        'cache_sb': nrm((DEPTH, n_pool, PAGE_SIZE, 2, H_B, HEAD_DIM), 1.0),
        'page_table': page_table,
        'p_prompt': nrm((DEPTH, BATCH, SEQ, PLE_DIM), 1.0),
        'p_sample': nrm((DEPTH, DEC_BATCH, DEC_SEQ, PLE_DIM), 1.0),
        'g_mix': gain((DEPTH, D_MODEL)),
        'w_in': nrm((DEPTH, D_MODEL, N_IN), D_MODEL ** -0.5),
        'w_oa': nrm((DEPTH, H_G * HEAD_DIM, D_MODEL), (H_G * HEAD_DIM) ** -0.5),
        'w_ob': nrm((DEPTH, B_W, D_MODEL), B_W ** -0.5),
        'b_sb': SB_BIAS_INIT + nrm((DEPTH, H_B), 0.5),
        'w_out': nrm((DEPTH, D_MODEL, D_MODEL), D_MODEL ** -0.5),
        'g_moe': gain((DEPTH, D_MODEL)),
        'w_rg': nrm((DEPTH, D_MODEL, N_GROUPS), D_MODEL ** -0.5),
        'b_rg': nrm((DEPTH, N_GROUPS), 0.01),
        'w_re': nrm((DEPTH, D_MODEL, N_GROUPS * E_PER), D_MODEL ** -0.5),
        'b_re': nrm((DEPTH, N_GROUPS * E_PER), 0.01),
        'w_up': nrm((DEPTH, N_EXPERTS, D_MODEL, D_EXPERT), D_MODEL ** -0.5),
        'w_gate': nrm((DEPTH, N_EXPERTS, D_MODEL, D_EXPERT), D_MODEL ** -0.5),
        'w_down': nrm((DEPTH, N_EXPERTS, D_EXPERT, D_MODEL), D_EXPERT ** -0.5),
        'g_ple': gain((DEPTH, D_MODEL)),
        'w_pg': nrm((DEPTH, D_MODEL, D_MODEL), D_MODEL ** -0.5),
        'w_pp': nrm((DEPTH, PLE_DIM, D_MODEL), PLE_DIM ** -0.5),
        'g_final': gain((D_MODEL,)),
    }

def reference(x_prompt, x_sample, cache_win1, cache_win2, cache_win3, cache_sb, page_table, p_prompt, p_sample,
              g_mix, w_in, w_oa, w_ob, b_sb, w_out, g_moe, w_rg, b_rg, w_re, b_re, w_up, w_gate, w_down,
              g_ple, w_pg, w_pp, g_final):
    slopes = alibi_slopes()
    win_caches = (cache_win1, cache_win2, cache_win3)
    S = x_prompt.shape[1]
    DB = x_sample.shape[0]
    xp, xs = x_prompt, x_sample
    win_p = [[], [], []]
    win_s = [[], [], []]
    sb_p, sb_s = [], []
    for i in range(DEPTH):
        ffn_w = (g_moe[i], w_rg[i], b_rg[i], w_re[i], b_re[i], w_up[i], w_gate[i], w_down[i], g_ple[i], w_pg[i], w_pp[i])
        qa, ka, va, qb, kb, vb, ga, gb = project_in(xp, g_mix[i], w_in[i])
        oa = combine_groups([dilated_prompt(qa[:, :, g], ka[:, :, g], va[:, :, g], win, dil, slopes[g])
                             for g, (win, dil) in enumerate(DIL_PAIRS)])
        ob = sb_prompt(qb, kb, vb, b_sb[i])
        xp = merge_out(xp, oa, ob, ga, gb, w_oa[i], w_ob[i], w_out[i])
        xp = channel_and_ple(xp, p_prompt[i], *ffn_w)
        for g, (win, _) in enumerate(DIL_PAIRS):
            wb = min(win, S)
            win_p[g].append(jnp.stack([ka[:, S - wb:, g], va[:, S - wb:, g]], axis=2))
        sb_p.append(jnp.stack([kb, vb], axis=2))
        qa, ka, va, qb, kb, vb, ga, gb = project_in(xs, g_mix[i], w_in[i])
        oa = combine_groups([dilated_sample(qa[:, :, g], ka[:, :, g], va[:, :, g], win_caches[g][i], win, dil, slopes[g])
                             for g, (win, dil) in enumerate(DIL_PAIRS)])
        past = cache_sb[i][page_table]
        past = past.reshape(DB, -1, 2, H_B, HEAD_DIM)
        ob = sb_sample(qb, kb, vb, past[:, :, 0], past[:, :, 1], b_sb[i])
        xs = merge_out(xs, oa, ob, ga, gb, w_oa[i], w_ob[i], w_out[i])
        xs = channel_and_ple(xs, p_sample[i], *ffn_w)
        for g in range(N_DIL):
            win_s[g].append(jnp.stack([ka[:, :, g], va[:, :, g]], axis=2))
        sb_s.append(jnp.stack([kb, vb], axis=2))
    y_prompt = rmsnorm(xp, g_final)
    y_sample = rmsnorm(xs, g_final)
    win1_prompt, win1_sample = jnp.stack(win_p[0]), jnp.stack(win_s[0])
    win2_prompt, win2_sample = jnp.stack(win_p[1]), jnp.stack(win_s[1])
    win3_prompt, win3_sample = jnp.stack(win_p[2]), jnp.stack(win_s[2])
    sb_prompt_rows, sb_sample_rows = jnp.stack(sb_p), jnp.stack(sb_s)
    return (y_prompt, y_sample, win1_prompt, win1_sample, win2_prompt, win2_sample,
            win3_prompt, win3_sample, sb_prompt_rows, sb_sample_rows)


_drawn_inputs = setup_inputs


def setup_inputs(seed=0):
    import zlib

    import numpy as np

    out = dict(_drawn_inputs(seed))
    spreads = {}
    factors = {'g_mix': 2.838,
     'b_sb': 2.972,
     'b_rg': 24.183,
     'b_re': 13.815,
     'g_ple': 59.159,
     'g_final': 7.838,
     'cache_sb': 8.0,
     'g_moe': 3.97}
    for name, (base, spread) in spreads.items():
        noise = np.random.default_rng([zlib.crc32(name.encode()), seed]).standard_normal(out[name].shape)
        drawn = base * np.exp(spread * noise) if base else spread * noise
        out[name] = __import__('jax').numpy.asarray(drawn.astype(out[name].dtype))
    for name, factor in factors.items():
        out[name] = (out[name] * factor).astype(out[name].dtype)
    return out
```

```python
from contextlib import ExitStack

import concourse.bass as bass
from concourse import mybir

F32 = mybir.dt.float32
I32 = mybir.dt.int32
ALU = mybir.AluOpType
ACT = mybir.ActivationFunctionType
AX = mybir.AxisListType.X

P = 128
D = 1024
KD = D // P
SEQ = 1024
DEC = 8
NT = SEQ + DEC
QT = SEQ // P
TT = QT + 1
HD = 64
N_DIL, H_G, H_B = 3, 4, 8
DIL = ((128, 1), (512, 4), (2048, 16))
A_W = N_DIL * H_G * HD
B_W = H_B * HD
QKV = 3 * A_W + 3 * B_W
N_IN = QKV + 2 * D
CHUNKS = QKV // P
CA, CB = A_W // P, B_W // P
NSPLIT = 3
NS = NT // NSPLIT
PAST = 256
PAGE = 128
NG, EPG = 4, 8
NE = NG * EPG
NR = NG + NE
FE = D // 2
KF = FE // P
PLE = 256
EPS = 1e-6
ASG = 2 * NT
SLOTS = ASG + P
MAXBLK = (ASG + NE * (P - 1)) // P
NEG = -1.0e30
SCALE = HD ** -0.5
SLOPES = [2.0 ** (-8.0 * (h + 1) / (N_DIL * H_G)) for h in range(N_DIL * H_G)]


def need(eng, sem, value):
    if not isinstance(value, int) or value > 0:
        eng.wait_ge(sem, value)


def looped(eng, n, step):
    step(0)
    with eng.Fori(1, n) as it:
        step(it)


def clear(nc, low):
    with nc.Block() as block:
        @block.gpsimd
        def _(pool):
            pool.sem_clear(low)


def rows(t):
    return P if t < QT else DEC


def norm_in(nc, g, x_of):
    ctx = ExitStack()
    with ctx:
        sb = lambda n, s, d=F32: ctx.enter_context(nc.sbuf_tensor(n, s, d))
        sem = lambda n: ctx.enter_context(nc.semaphore(n))
        R = 3
        xt = sb("n_xt", [P, R, D])
        xn = sb("n_xn", [P, 2, D])
        sq = sb("n_sq", [P, D])
        ss = sb("n_ss", [P, TT])
        rt = sb("n_rt", [P, TT])
        rstd = sb("n_rstd", [P, TT])
        gm = sb("n_gm", [P, KD])
        tp = [ctx.enter_context(nc.psum_tensor(f"n_tp{j}", [P, KD, P], F32)) for j in range(2)]
        x_in = [sem(f"n_x_in{j}") for j in range(R)]
        gm_in, ssq, mean, root, inv, scaled, turned, stored = map(sem, (
            "n_gm_in", "n_ssq", "n_mean", "n_root", "n_inv", "n_scaled", "n_turned", "n_stored"))
        block = ctx.enter_context(nc.Block())

        @block.sync
        def _(sp):
            with nc.allow_non_contiguous_dma(reason="1024 gains, once"):
                sp.dma_start(gm[:, :], g["g_mix"].rearrange("a (k p) -> p (a k)", p=P)).then_inc(gm_in, 16)
            for t in range(TT):
                if t >= R:
                    sp.wait_ge(scaled, t - R + 1)
                sp.dma_start(xt[0:rows(t), t % R, :], x_of(t)).then_inc(x_in[t % R], 16)

        @block.scalar
        def _(act):
            for t in range(TT):
                r = rows(t)
                act.wait_ge(x_in[t % R], 16 * (t // R + 1))
                if t:
                    act.wait_ge(ssq, t)
                act.activation(sq[0:r, :], xt[0:r, t % R, :], ACT.Square,
                               accum_out=ss[0:r, t:t + 1]).then_inc(ssq, 1)
                act.wait_ge(mean, t + 1)
                act.activation(rt[0:r, t:t + 1], rt[0:r, t:t + 1], ACT.Sqrt).then_inc(root, 1)

        @block.vector
        def _(dve):
            dve.wait_ge(gm_in, 16)
            for t in range(TT + 1):
                if t < TT:
                    r = rows(t)
                    dve.wait_ge(ssq, t + 1)
                    dve.tensor_scalar(rt[0:r, t:t + 1], ss[0:r, t:t + 1], 1.0 / D, EPS, ALU.mult,
                                      ALU.add).then_inc(mean, 1)
                    dve.wait_ge(root, t + 1)
                    dve.reciprocal(rstd[0:r, t:t + 1], rt[0:r, t:t + 1]).then_inc(inv, 1)
                    dve.wait_ge(inv, t + 1)
                    if t >= 2:
                        dve.wait_ge(turned, t - 1)
                    dve.tensor_scalar(xn[0:r, t % 2, :], xt[0:r, t % R, :], rstd[0:r, t:t + 1], None,
                                      ALU.mult).then_inc(scaled, 1)
                if t >= 1:
                    u = t - 1
                    r = rows(u)
                    dve.wait_ge(turned, u + 1)
                    dve.tensor_tensor(g["uT"][:, :, u * P:u * P + r], tp[u % 2][:, :, 0:r],
                                      gm[:, :].unsqueeze(2).to_broadcast([P, KD, r]),
                                      ALU.mult).then_inc(stored, 1)

        @block.tensor
        def _(pe):
            pe.wait_ge(g["ident_set"], 2)
            for t in range(TT):
                r = rows(t)
                pe.wait_ge(scaled, t + 1)
                if t >= 2:
                    pe.wait_ge(stored, t - 1)
                for k in range(KD):
                    last = pe.transpose(tp[t % 2][:, k, 0:r], xn[0:r, t % 2, k * P:(k + 1) * P],
                                        g["ident"][0:r, 0:r])
                last.then_inc(turned, 1)

        @block.gpsimd
        def _(pool):
            pool.memset(g["ident"][:, :], 0.0).then_inc(g["ident_set"], 1)
            pool.wait_ge(g["ident_set"], 1)
            pool.affine_select(out=g["ident"][:, :], in_=g["ident"][:, :], compare_op=ALU.not_equal, fill=1.0,
                               base=0, pattern=[[-1, P]], channel_multiplier=1).then_inc(g["ident_set"], 1)


def project(nc, g):
    ctx = ExitStack()
    with ctx:
        sb = lambda n, s, d=F32: ctx.enter_context(nc.sbuf_tensor(n, s, d))
        sem = lambda n: ctx.enter_context(nc.semaphore(n))
        w = sb("p_w", [P, 2, KD, P])
        zc = sb("p_zc", [P, 2, NT])
        zk = sb("p_zk", [P, 2, TT, P])
        acc = [ctx.enter_context(nc.psum_tensor(f"p_acc{j}", [P, 512], F32)) for j in range(6)]
        tp = [ctx.enter_context(nc.psum_tensor(f"p_tp{j}", [P, 4, P], F32)) for j in range(2)]
        w_in = [sem(f"p_w_in{j}") for j in range(2)]
        z_out = [sem(f"p_z_out{j}") for j in range(2)]
        k_out = g["pool_dma"][0:2]
        acc_full, zc_full, tp_full, zk_full = map(sem, ("p_acc_full", "p_zc_full", "p_tp_full", "p_zk_full"))
        uT, ident, zT, ztok = g["uT"], g["ident"], g["zT"], g["ztok"]
        win_v = g["w_in"].rearrange("a (k p) n -> p (a k) n", p=P)
        zt_v = ztok[0:SEQ, :].rearrange("(t p) n -> p t n", p=P)
        block = ctx.enter_context(nc.Block())
        PASSES = CHUNKS // 2
        GROUPS = [(0, 4), (4, 4), (8, 1)]
        NG_ = len(GROUPS)

        @block.sync
        def _(sp):
            def load(it, b):
                sp.dma_start(w[:, b, :, :], win_v[:, :, bass.ds((it * 2 + b) * P, P)]).then_inc(w_in[b], 16)

            load(0, 0)
            load(0, 1)
            with sp.Fori(0, PASSES - 1) as it:
                for b in range(2):
                    sp.wait_ge(acc_full, it * 2 * NSPLIT + (b + 1) * NSPLIT)
                    load(it + 1, b)

        @block.tensor
        def _(pe):
            def step(it):
                need(pe, zc_full, it * 2 * NSPLIT)
                for b in range(2):
                    pe.wait_ge(w_in[b], it * 16 + 16)
                    for s in range(NSPLIT):
                        for k in range(KD):
                            last = pe.matmul(acc[b * NSPLIT + s][:, 0:NS], w[:, b, k, :],
                                             uT[:, k, s * NS:(s + 1) * NS], start=(k == 0), stop=(k == KD - 1))
                        last.then_inc(acc_full, 1)
                for b in range(2):
                    pe.wait_ge(zc_full, it * 2 * NSPLIT + (b + 1) * NSPLIT)
                    for n, (t0, m) in enumerate(GROUPS):
                        j = b * NG_ + n
                        need(pe, zk_full, it * 2 * NG_ + max(0, j - 1))
                        for t in range(t0, t0 + m):
                            last = pe.transpose(tp[j % 2][0:rows(t), t - t0, :],
                                                zc[:, b, t * P:t * P + rows(t)], ident[:, :])
                        last.then_inc(tp_full, 1)

            looped(pe, PASSES, step)

        @block.scalar
        def _(act):
            def step(it):
                for b in range(2):
                    need(act, tp_full, it * 2 * NG_)
                    need(act, z_out[b], it * 16)
                    for s in range(NSPLIT):
                        act.wait_ge(acc_full, it * 2 * NSPLIT + b * NSPLIT + s + 1)
                        act.activation(zc[:, b, s * NS:(s + 1) * NS], acc[b * NSPLIT + s][:, 0:NS],
                                       ACT.Copy).then_inc(zc_full, 1)
                for b in range(2):
                    act.wait_ge(zc_full, it * 2 * NSPLIT + (b + 1) * NSPLIT)
                    act.dma_start(zT[bass.ds(it * 2 + b, 1), :, :].rearrange("a p n -> (a p) n"),
                                  zc[:, b, :]).then_inc(z_out[b], 16)

            looped(act, PASSES, step)
            for b in range(2):
                act.wait_ge(z_out[b], PASSES * 16)

        @block.vector
        def _(dve):
            def step(it):
                for b in range(2):
                    need(dve, k_out[b], it * 32)
                    for n, (t0, m) in enumerate(GROUPS):
                        j = b * NG_ + n
                        dve.wait_ge(tp_full, it * 2 * NG_ + j + 1)
                        r = rows(t0)
                        dve.tensor_copy(zk[0:r, b, t0:t0 + m, :], tp[j % 2][0:r, 0:m, :]).then_inc(zk_full, 1)

            looped(dve, PASSES, step)

        @block.gpsimd
        def _(pool):
            def step(it):
                for b in range(2):
                    c = it * 2 + b
                    pool.wait_ge(zk_full, it * 2 * NG_ + (b + 1) * NG_)
                    pool.dma_start(zt_v[:, :, bass.ds(c * P, P)], zk[:, b, 0:QT, :]).then_inc(k_out[b], 16)
                    pool.dma_start(ztok[SEQ:NT, bass.ds(c * P, P)], zk[0:DEC, b, QT, :]).then_inc(k_out[b], 16)

            looped(pool, PASSES, step)
            for b in range(2):
                pool.wait_ge(k_out[b], PASSES * 32)


def turn_groups(n):
    return [(a, min(4, n - a)) for a in range(0, n, 4)]


def pipeline(n, size):
    def unit(it, j, lag):
        p_, x = (it, j - lag) if j >= lag else (it - 1, j - lag + size)
        return p_, x // QT, x % QT, it * size + (j - lag)

    def there(it, j, lag):
        return not isinstance(it, int) or 0 <= it * size + j - lag < n * size

    def passes(eng, step, lag):
        for j in range(size):
            step(0, j)
        with eng.Fori(1, n) as it:
            for j in range(size):
                step(it, j)
        for j in range(lag):
            step(n, j)

    return unit, passes, there


def stick(nc, g):
    ctx = ExitStack()
    with ctx:
        sb = lambda n, s, d=F32: ctx.enter_context(nc.sbuf_tensor(n, s, d))
        sem = lambda n: ctx.enter_context(nc.semaphore(n))
        ps = lambda n, s: ctx.enter_context(nc.psum_tensor(n, s, F32))
        PAIRS = H_B // 2
        U = 2 * QT
        BUF = 4
        q = sb("s_q", [HD, 2, SEQ])
        k = sb("s_k", [HD, 2, SEQ])
        v = sb("s_v", [P, 2, QT, HD])
        bias = sb("s_bias", [P, 2])
        causal = sb("s_causal", [P, P])
        const = sem("s_const")
        z = sb("s_z", [P, BUF, SEQ])
        w = sb("s_w", [P, 2, SEQ])
        r = sb("s_r", [P, 2, SEQ])
        cum = sb("s_cum", [P, 2, SEQ])
        a = sb("s_a", [P, BUF, SEQ])
        aT = sb("s_aT", [P, 2, SEQ])
        o = sb("s_o", [P, QT, P])
        S = [ps(f"s_S{j}", [P, SEQ]) for j in range(2)]
        tp = [ps(f"s_tp{j}", [P, 512]) for j in range(2)]
        oT = ps("s_oT", [P, 512])
        O = [ps("s_O", [P, HD]), oT[:, 0:HD]]
        s_full, z_full, masked, r_full, w_full, e_full, t_full, cum_full, al_full, a_full = map(sem, (
            "s_s_full", "s_z_full", "s_masked", "s_r_full", "s_w_full", "s_e_full", "s_t_full",
            "s_cum_full", "s_al_full", "s_a_full"))
        tp_full, aT_full, o_full, o_read, oT_full, oT_read = map(sem, (
            "s_tp_full", "s_aT_full", "s_o_full", "s_o_read", "s_oT_full", "s_oT_read"))
        qkv_in = [sem(f"s_qkv_in{b}") for b in range(2)]
        ident, zT, ztok, obT = g["ident"], g["zT"], g["ztok"], g["obT"]
        CQ, CK, COLV = 3 * CA, 3 * CA + CB, 3 * A_W + 2 * B_W
        BASE = [0]
        for i in range(QT):
            BASE.append(BASE[-1] + len(turn_groups(i + 1)))
        GH = BASE[QT]
        ztv = ztok[0:SEQ, :].rearrange("(t p) n -> p t n", p=P)
        block = ctx.enter_context(nc.Block())

        def group(it, b, i, n):
            return it * (2 * GH) + (b * GH + BASE[i] + n)

        unit, passes, there = pipeline(PAIRS, U)

        def late(x):
            p_, y = divmod(x, U)
            return p_ * 2 * GH + (y // QT) * GH + BASE[y % QT + 1]
        LATE = [late(j - 1 - BUF) for j in range(U)]

        @block.sync
        def _(sp):
            def load(it, b):
                half = b * HD
                need(sp, o_full, (it - 1) * U + (b + 1) * QT)
                sp.dma_start(q[:, b, :], zT[bass.ds(it + CQ, 1), half:half + HD, 0:SEQ]
                             .rearrange("a p n -> (a p) n")).then_inc(qkv_in[b], 16)
                sp.dma_start(k[:, b, :], zT[bass.ds(it + CK, 1), half:half + HD, 0:SEQ]
                             .rearrange("a p n -> (a p) n")).then_inc(qkv_in[b], 16)
                sp.dma_start(v[:, b, :, :], ztv[:, :, bass.ds(it * P + (COLV + half), HD)]).then_inc(qkv_in[b], 16)
                sp.dma_start(bias[:, b:b + 1], g["b_sb"][:, bass.ds(it * 2 + b, 1)].broadcast_to([P, 1]))\
                    .then_inc(qkv_in[b], 16)

            for b in range(2):
                load(0, b)
            with sp.Fori(1, PAIRS) as it:
                for b in range(2):
                    load(it, b)

        @block.tensor
        def _(pe):
            def scores(it, j):
                _, b, i, u = unit(it, j, 0)
                if i == 0:
                    pe.wait_ge(qkv_in[b], it * 64 + 64)
                need(pe, z_full, u - 1)
                for c in range(0, (i + 1) * P, 512):
                    n = min(512, (i + 1) * P - c)
                    last = pe.matmul(S[j % 2][:, c:c + n], q[:, b, i * P:(i + 1) * P], k[:, b, c:c + n],
                                     start=True, stop=True)
                last.then_inc(s_full, 1)

            def turn(it, j):
                p_, b, i, u = unit(it, j, 3)
                pe.wait_ge(a_full, u + 1)
                for n, (t0, m) in enumerate(turn_groups(i + 1)):
                    x = b * GH + BASE[i] + n
                    need(pe, aT_full, group(p_, b, i, n) - 1)
                    for t in range(m):
                        last = pe.transpose(tp[x % 2][:, t * P:(t + 1) * P],
                                            a[:, (j - 3) % BUF, (t0 + t) * P:(t0 + t + 1) * P], ident[:, :])
                    last.then_inc(tp_full, 1)

            def values(it, j):
                p_, b, i, u = unit(it, j, 4)
                pe.wait_ge(aT_full, group(p_, b, i, len(turn_groups(i + 1)) - 1) + 1)
                need(pe, o_read, u - 1)
                if j == 5:
                    need(pe, oT_read, it * 2)
                for t in range(i + 1):
                    last = pe.matmul(O[j % 2][:, :], aT[:, j % 2, t * P:(t + 1) * P], v[:, b, t, :],
                                     start=(t == 0), stop=(t == i))
                last.then_inc(o_full, 1)

            def out(it, j):
                pe.wait_ge(o_read, it * U)
                for h in range(2):
                    if h:
                        pe.wait_ge(oT_read, (it - 1) * 2 + h)
                    for t in range(4):
                        last = pe.transpose(oT[:, t * P:(t + 1) * P], o[:, h * 4 + t, :], ident[:, :])
                    last.then_inc(oT_full, 1)

            def step(it, j):
                if there(it, j, 0):
                    scores(it, j)
                if there(it, j, 3):
                    turn(it, j)
                if there(it, j, 4):
                    values(it, j)
                if j == 4 and (not isinstance(it, int) or it):
                    out(it, j)

            passes(pe, step, 6)

        @block.scalar
        def _(act):
            act.preload_act_table_set("natural_log_exp_and_others")

            def step(it, j):
                if there(it, j, 0):
                    _, b, i, u = unit(it, j, 0)
                    n = (i + 1) * P
                    act.wait_ge(s_full, u + 1)
                    need(act, al_full, u - BUF + 1)
                    act.activation(z[:, j % BUF, 0:n], S[j % 2][:, 0:n], ACT.Identity, scale=SCALE,
                                   bias=bias[:, b:b + 1]).then_inc(z_full, 1)
                if there(it, j, 1):
                    p_, b, i, u = unit(it, j, 1)
                    n = (i + 1) * P
                    x = (j - 1) % 2
                    act.wait_ge(w_full, u + 1)
                    act.activation(w[:, x, 0:n], w[:, x, 0:n], ACT.Exp, scale=-1.0).then_inc(e_full, 1)
                    act.wait_ge(e_full, u + 1)
                    act.activation(w[:, x, 0:n], w[:, x, 0:n], ACT.Ln, bias=1.0).then_inc(t_full, 1)
                if there(it, j, 2):
                    p_, b, i, u = unit(it, j, 2)
                    n = (i + 1) * P
                    act.wait_ge(al_full, u + 1)
                    act.activation(a[:, (j - 2) % BUF, 0:n], a[:, (j - 2) % BUF, 0:n], ACT.Exp).then_inc(a_full, 1)
                if there(it, j, 5):
                    p_, b, i, u = unit(it, j, 5)
                    act.wait_ge(o_full, u + 1)
                    if b == i == 0:
                        need(act, oT_full, p_ * 2)
                    act.activation(o[:, i, b * HD:(b + 1) * HD], O[(j - 1) % 2][:, :], ACT.Copy).then_inc(o_read, 1)

            passes(act, step, 5)

        @block.gpsimd
        def _(pool):
            pool.memset(causal[:, :], 0.0).then_inc(const, 1)
            pool.wait_ge(const, 1)
            pool.affine_select(out=causal[:, :], in_=causal[:, :], compare_op=ALU.is_gt, fill=NEG, base=0,
                               pattern=[[-1, P]], channel_multiplier=1).then_inc(const, 1)
            pool.wait_ge(const, 2)

            def step(it, j):
                if there(it, j, 0):
                    _, b, i, u = unit(it, j, 0)
                    pool.wait_ge(z_full, u + 1)
                    diag = z[:, j % BUF, i * P:(i + 1) * P]
                    pool.tensor_tensor(diag, diag, causal[:, :], ALU.add).then_inc(masked, 1)
                if there(it, j, 1):
                    p_, b, i, u = unit(it, j, 1)
                    n = (i + 1) * P
                    pool.wait_ge(cum_full, u + 1)
                    need(pool, tp_full, it * (2 * GH) + LATE[j])
                    pool.tensor_tensor(a[:, (j - 1) % BUF, 0:n], z[:, (j - 1) % BUF, 0:n], cum[:, j % 2, 0:n],
                                       ALU.subtract).then_inc(al_full, 1)

            passes(pool, step, 1)

        @block.vector
        def _(dve):
            def step(it, j):
                if there(it, j, 0):
                    _, b, i, u = unit(it, j, 0)
                    n = (i + 1) * P
                    dve.wait_ge(masked, u + 1)
                    dve.tensor_scalar(w[:, j % 2, 0:n].bitcast(I32), z[:, j % BUF, 0:n].bitcast(I32),
                                      0x7FFFFFFF, None, ALU.bitwise_and).then_inc(w_full, 1)
                    dve.tensor_scalar(r[:, j % 2, 0:n], z[:, j % BUF, 0:n], 0.0, None, ALU.max).then_inc(r_full, 1)
                if there(it, j, 1):
                    p_, b, i, u = unit(it, j, 1)
                    n = (i + 1) * P
                    x = (j - 1) % 2
                    dve.wait_ge(t_full, u + 1)
                    dve.wait_ge(r_full, u + 1)
                    need(dve, al_full, u - 1)
                    dve.tensor_tensor_scan(cum[:, j % 2, 0:n][:, ::-1], w[:, x, 0:n][:, ::-1],
                                           r[:, x, 0:n][:, ::-1], 0.0, ALU.add, ALU.add).then_inc(cum_full, 1)
                if there(it, j, 3):
                    p_, b, i, u = unit(it, j, 3)
                    need(dve, o_full, u - 1)
                    for n, (t0, m) in enumerate(turn_groups(i + 1)):
                        x = b * GH + BASE[i] + n
                        dve.wait_ge(tp_full, group(p_, b, i, n) + 1)
                        dve.tensor_copy(aT[:, (j - 3) % 2, t0 * P:(t0 + m) * P],
                                        tp[x % 2][:, 0:m * P]).then_inc(aT_full, 1)
                if j == 4 and (not isinstance(it, int) or it):
                    for h in range(2):
                        dve.wait_ge(oT_full, (it - 1) * 2 + h + 1)
                        dve.tensor_copy(obT[:, bass.ds(it - 1, 1), h * 512:(h + 1) * 512]
                                        .rearrange("p a n -> p (a n)"), oT[:, :]).then_inc(oT_read, 1)

            passes(dve, step, 6)


def dilated(nc, g):
    ctx = ExitStack()
    with ctx:
        sb = lambda n, s, d=F32: ctx.enter_context(nc.sbuf_tensor(n, s, d))
        sem = lambda n: ctx.enter_context(nc.semaphore(n))
        ps = lambda n, s: ctx.enter_context(nc.psum_tensor(n, s, F32))
        PAIRS = H_G // 2
        U = 2 * QT
        BUF = 4
        BACK = [min(QT - 1, win // P) for win, _ in DIL]
        W = [(n + 1) * P for n in BACK]
        SEGB = [0, 2 * P, 0]
        q = sb("d_q", [HD, 2, N_DIL, SEQ])
        k = sb("d_k", [HD, 2, N_DIL, SEQ])
        v = sb("d_v", [P, 2, N_DIL, QT, HD])
        md = [sb(f"d_md{x}", [P, W[x]]) for x in range(N_DIL)]
        slope = sb("d_slope", [P, N_DIL * H_G])
        row = sb("d_row", [P, BUF, sum(W)])
        pT = sb("d_pT", [P, 2, sum(W)])
        mx = sb("d_mx", [P, BUF])
        nmx = sb("d_nmx", [P, BUF])
        den = sb("d_den", [P, BUF])
        rden = sb("d_rden", [P, BUF])
        o = sb("d_o", [P, QT, P])
        S = [ps(f"d_S{j}", [P, SEQ]) for j in range(2)]
        tp = [ps(f"d_tp{j}", [P, 512]) for j in range(2)]
        oT = ps("d_oT", [P, 512])
        O = [ps("d_O", [P, HD]), oT[:, 0:HD]]
        const, dist_set, md_set, s01_full, s2_full, biased, mx_full, nmx_full, p_full, rden_full = map(sem, (
            "d_const", "d_dist_set", "d_md_set", "d_s01_full", "d_s2_full", "d_biased", "d_mx_full",
            "d_nmx_full", "d_p_full", "d_rden_full"))
        masked = sem("d_masked")
        tp_full, pT_full, o_full, o_read, oT_full, oT_read = map(sem, (
            "d_tp_full", "d_pT_full", "d_o_full", "d_o_read", "d_oT_full", "d_oT_read"))
        qkv_in = [sem(f"d_qkv_in{b}") for b in range(2)]
        ident, zT, ztok, oaT = g["ident"], g["zT"], g["ztok"], g["oaT"]
        unit, passes, there = pipeline(PAIRS, U)

        def keys(i):
            return [(x, t) for x in range(N_DIL) for t in range(max(0, i - BACK[x]), i + 1)]

        def span(i, x):
            m = [n for n, (y, _) in enumerate(keys(i)) if y == x]
            return m[0] * P, max(0, i - BACK[x]), len(m)

        BASE = [0]
        for i in range(QT):
            BASE.append(BASE[-1] + len(turn_groups(len(keys(i)))))
        GH = BASE[QT]

        def group(it, b, i, n):
            return it * (2 * GH) + (b * GH + BASE[i] + n)

        def late(x):
            p_, y = divmod(x, U)
            return p_ * 2 * GH + (y // QT) * GH + BASE[y % QT + 1]

        ztv = ztok[0:SEQ, :].rearrange("(t p) n -> p t n", p=P)
        block = ctx.enter_context(nc.Block())

        @block.sync
        def _(sp):
            def load(it, b):
                half = b * HD
                need(sp, o_full, (it - 1) * U + (b + 1) * QT)
                for x in range(N_DIL):
                    c = x * (H_G // 2) + it
                    sp.dma_start(q[:, b, x, :], zT[bass.ds(c, 1), half:half + HD, 0:SEQ]
                                 .rearrange("a p n -> (a p) n")).then_inc(qkv_in[b], 16)
                    sp.dma_start(k[:, b, x, :], zT[bass.ds(c + CA, 1), half:half + HD, 0:SEQ]
                                 .rearrange("a p n -> (a p) n")).then_inc(qkv_in[b], 16)
                    sp.dma_start(v[:, b, x, :, :], ztv[:, :, bass.ds(c * P + (2 * A_W + half), HD)])\
                        .then_inc(qkv_in[b], 16)

            for b in range(2):
                load(0, b)
            with sp.Fori(1, PAIRS) as it:
                for b in range(2):
                    load(it, b)

        @block.gpsimd
        def _(pool):
            for h in range(N_DIL * H_G):
                pool.memset(slope[:, h:h + 1], SLOPES[h]).then_inc(const, 1)
            for x in range(N_DIL):
                pool.iota(pT[:, 0, sum(W[:x]):sum(W[:x + 1])].bitcast(I32), pattern=[[-1, W[x]]],
                          base=BACK[x] * P, channel_multiplier=1).then_inc(dist_set, 1)
            for x, (win, _) in enumerate(DIL):
                pool.wait_ge(md_set, 2 * N_DIL)
                pool.affine_select(out=md[x][:, :], in_=md[x][:, :], compare_op=ALU.is_ge, fill=NEG,
                                   base=BACK[x] * P, pattern=[[-1, W[x]]], channel_multiplier=1).then_inc(const, 1)
                pool.wait_ge(const, N_DIL * H_G + 2 * x + 1)
                pool.affine_select(out=md[x][:, :], in_=md[x][:, :], compare_op=ALU.is_ge, fill=NEG,
                                   base=win - BACK[x] * P, pattern=[[1, W[x]]], channel_multiplier=-1)\
                    .then_inc(const, 1)

        @block.tensor
        def _(pe):
            def scores(it, j):
                _, b, i, u = unit(it, j, 0)
                if i == 0:
                    pe.wait_ge(qkv_in[b], it * (9 * 16) + 9 * 16)
                for x in range(N_DIL):
                    _, t0, m = span(i, x)
                    if x == 0:
                        need(pe, biased, u * 3 - 1)
                    if x == 2:
                        need(pe, biased, u * 3)
                    c = SEGB[x]
                    key, end = t0 * P, (t0 + m) * P
                    while key < end:
                        n = min(512 - c % 512, end - key)
                        last = pe.matmul(S[x // 2][:, c:c + n], q[:, b, x, i * P:(i + 1) * P],
                                         k[:, b, x, key:key + n], start=True, stop=True,
                                         skip_group_check=True)
                        key, c = key + n, c + n
                    if x:
                        last.then_inc(s01_full if x == 1 else s2_full, 1)

            def turn(it, j):
                p_, b, i, u = unit(it, j, 2)
                pe.wait_ge(p_full, u + 1)
                for n, (t0, m) in enumerate(turn_groups(len(keys(i)))):
                    x = b * GH + BASE[i] + n
                    need(pe, pT_full, group(p_, b, i, n) - 1)
                    for t in range(m):
                        last = pe.transpose(tp[x % 2][:, t * P:(t + 1) * P],
                                            row[:, (j - 2) % BUF, (t0 + t) * P:(t0 + t + 1) * P], ident[:, :])
                    last.then_inc(tp_full, 1)

            def values(it, j):
                p_, b, i, u = unit(it, j, 3)
                ks = keys(i)
                pe.wait_ge(pT_full, group(p_, b, i, len(turn_groups(len(ks))) - 1) + 1)
                need(pe, o_read, u - 1)
                if j == 4:
                    need(pe, oT_read, it * 2)
                for n, (x, t) in enumerate(ks):
                    last = pe.matmul(O[(j - 3) % 2][:, :], pT[:, (j - 3) % 2, n * P:(n + 1) * P], v[:, b, x, t, :],
                                     start=(n == 0), stop=(n == len(ks) - 1))
                last.then_inc(o_full, 1)

            def out(it, j):
                pe.wait_ge(o_read, it * U)
                for h in range(2):
                    if h:
                        pe.wait_ge(oT_read, (it - 1) * 2 + h)
                    for t in range(4):
                        last = pe.transpose(oT[:, t * P:(t + 1) * P], o[:, h * 4 + t, :], ident[:, :])
                    last.then_inc(oT_full, 1)

            def step(it, j):
                if there(it, j, 0):
                    scores(it, j)
                if there(it, j, 2):
                    turn(it, j)
                if there(it, j, 3):
                    values(it, j)
                if j == 3 and (not isinstance(it, int) or it):
                    out(it, j)

            passes(pe, step, 5)

        @block.scalar
        def _(act):
            def step(it, j):
                if there(it, j, 1):
                    p_, b, i, u = unit(it, j, 1)
                    n = len(keys(i)) * P
                    x = (j - 1) % BUF
                    act.wait_ge(nmx_full, u + 1)
                    need(act, rden_full, u - BUF + 1)
                    act.activation(row[:, x, 0:n], row[:, x, 0:n], ACT.Exp, scale=SCALE, bias=nmx[:, x:x + 1],
                                   accum_out=den[:, x:x + 1]).then_inc(p_full, 1)
                if there(it, j, 2):
                    p_, b, i, u = unit(it, j, 2)
                    need(act, o_full, u - 1)
                    for n, (t0, m) in enumerate(turn_groups(len(keys(i)))):
                        x = b * GH + BASE[i] + n
                        act.wait_ge(tp_full, group(p_, b, i, n) + 1)
                        act.activation(pT[:, (j - 2) % 2, t0 * P:(t0 + m) * P], tp[x % 2][:, 0:m * P],
                                       ACT.Copy).then_inc(pT_full, 1)
                if there(it, j, 4):
                    p_, b, i, u = unit(it, j, 4)
                    act.wait_ge(o_full, u + 1)
                    act.wait_ge(rden_full, u + 1)
                    if b == i == 0:
                        need(act, oT_full, p_ * 2)
                    act.activation(o[:, i, b * HD:(b + 1) * HD], O[(j - 4) % 2][:, :], ACT.Copy,
                                   scale=rden[:, (j - 4) % BUF:(j - 4) % BUF + 1]).then_inc(o_read, 1)

            passes(act, step, 4)

        @block.vector
        def _(dve):
            for x in range(N_DIL):
                dve.wait_ge(dist_set, N_DIL)
                d = pT[:, 0, sum(W[:x]):sum(W[:x + 1])].bitcast(I32)
                f = row[:, 0, sum(W[:x]):sum(W[:x + 1])]
                m = row[:, 1, sum(W[:x]):sum(W[:x + 1])].bitcast(I32)
                dve.tensor_scalar(m, d, DIL[x][1] - 1, None, ALU.bitwise_and).then_inc(md_set, 1)
                dve.wait_ge(md_set, 2 * x + 1)
                dve.tensor_scalar(f, m, 0.0, NEG, ALU.is_gt, ALU.mult).then_inc(masked, 1)
                dve.wait_ge(masked, x + 1)
                dve.scalar_tensor_tensor(out=md[x][:, :], in0=d, scalar=-8.0, in1=f, op0=ALU.mult,
                                         op1=ALU.add).then_inc(md_set, 1)
                dve.wait_ge(md_set, 2 * x + 2)
            dve.wait_ge(const, N_DIL * H_G + 2 * N_DIL)

            def step(it, j):
                if there(it, j, 0):
                    _, b, i, u = unit(it, j, 0)
                    r = row[:, j % BUF, :]
                    need(dve, tp_full, it * (2 * GH) + LATE[j])
                    for x in range(N_DIL):
                        c, t0, m = span(i, x)
                        dve.wait_ge(s01_full if x < 2 else s2_full, u + 1)
                        y = W[x] - m * P
                        if not isinstance(it, int):
                            h = bass.ds(it * 2 + (x * H_G + b), 1)
                        else:
                            h = slice(it * 2 + x * H_G + b, it * 2 + x * H_G + b + 1)
                        dve.scalar_tensor_tensor(out=r[:, c:c + m * P], in0=md[x][:, y:W[x]], scalar=slope[:, h],
                                                 in1=S[x // 2][:, SEGB[x]:SEGB[x] + m * P], op0=ALU.mult,
                                                 op1=ALU.add).then_inc(biased, 1)
                    dve.wait_ge(biased, u * 3 + 3)
                    y = slice(j % BUF, j % BUF + 1)
                    need(dve, p_full, u - BUF + 1)
                    dve.reduce_max(mx[:, y], r[:, 0:len(keys(i)) * P], AX).then_inc(mx_full, 1)
                    dve.wait_ge(mx_full, u + 1)
                    dve.tensor_scalar(nmx[:, y], mx[:, y], -SCALE, None, ALU.mult).then_inc(nmx_full, 1)
                if there(it, j, 1):
                    _, b, i, u = unit(it, j, 1)
                    y = slice((j - 1) % BUF, (j - 1) % BUF + 1)
                    dve.wait_ge(p_full, u + 1)
                    need(dve, o_read, u - BUF + 1)
                    dve.reciprocal(rden[:, y], den[:, y]).then_inc(rden_full, 1)
                if j == 3 and (not isinstance(it, int) or it):
                    for h in range(2):
                        dve.wait_ge(oT_full, (it - 1) * 2 + h + 1)
                        dve.tensor_copy(oaT[:, bass.ds(it - 1, 1), h * 512:(h + 1) * 512]
                                        .rearrange("p a n -> p (a n)"), oT[:, :]).then_inc(oT_read, 1)

            LATE = [late(j - BUF) for j in range(U)]
            passes(dve, step, 5)


def decode_dilated(nc, g):
    ctx = ExitStack()
    with ctx:
        sb = lambda n, s, d=F32: ctx.enter_context(nc.sbuf_tensor(n, s, d))
        sem = lambda n: ctx.enter_context(nc.semaphore(n))
        ps = lambda n, s: ctx.enter_context(nc.psum_tensor(n, s, F32))
        GW = H_G * HD
        BH = DEC * H_G
        N1, N2 = PAST // DIL[1][1], PAST // DIL[2][1]
        OWN = N1 + N2
        K = sb("c_k", [P, 2, DEC, GW])
        V = sb("c_v", [P, 2, DEC, GW])
        Q = sb("c_q", [P, 2, DEC, GW])
        dist = sb("c_dist", [P, 3])
        sl = sb("c_sl", [P, 2, H_G])
        bias = sb("c_bias", [P, 2, H_G])
        s = sb("c_s", [P, 2, BH])
        st = sb("c_st", [BH, 2, P])
        mx = sb("c_mx", [BH, 4])
        pT = sb("c_pT", [P, 2, BH])
        head = sb("c_head", [H_G, H_G, HD])
        ones = sb("c_ones", [H_G, 1])
        om = sb("c_om", [H_G, DEC, GW])
        s_ps = ps("c_s_ps", [BH, 2, P])
        pT_ps = ps("c_pT_ps", [P, 2, BH])
        o_ps = ps("c_o_ps", [H_G, DEC, GW])
        oT_ps = ps("c_oT_ps", [P, 2, DEC])
        cleared, kq_in, v_in, pool_step, bias_set, dve_step, s_full, sT_full, row_full, p_full, pn_full, pT_full, \
            pT_read, o_full, om_full, oT_full, done = map(sem, (
                "c_cleared", "c_kq_in", "c_v_in", "c_pool_step", "c_bias_set", "c_dve_step", "c_s_full", "c_sT_full",
                "c_row_full", "c_p_full", "c_pn_full", "c_pT_full", "c_pT_read", "c_o_full", "c_om_full",
                "c_oT_full", "c_done"))
        ident, ztok, oaT = g["ident"], g["ztok"], g["oaT"]
        tok = ztok[SEQ:NT, :]
        block = ctx.enter_context(nc.Block())

        def loads(eng, dst, which, cache_at, own_at, done_sem):
            for x, (p0, n, step) in enumerate(((0, P, 1), (0, N1, DIL[1][1]), (N1, N2, DIL[2][1]))):
                c = g[f"cache_win{x + 1}"]
                src = c[0, :, 0:n * step:step, cache_at, :, :].rearrange("b n h d -> n b (h d)")
                eng.dma_start(dst[p0:p0 + n, min(x, 1), :, :], src).then_inc(done_sem, 16)
            for x in range(N_DIL):
                eng.dma_start(dst[OWN + x:OWN + x + 1, 1, :, :],
                              tok[:, own_at + x * GW:own_at + (x + 1) * GW].unsqueeze(0)).then_inc(done_sem, 16)

        @block.sync
        def _(sp):
            sp.wait_ge(cleared, 3)
            loads(sp, K, "k", 0, A_W, kq_in)
            for x, (p0, n) in enumerate(((0, P), (0, N1), (N1, N2))):
                q = tok[:, x * GW:(x + 1) * GW].unsqueeze(0)
                sp.dma_start(Q[p0:p0 + n, min(x, 1), :, :], q.broadcast_to([n, DEC, GW])).then_inc(kq_in, 16)
                sp.dma_start(Q[OWN + x:OWN + x + 1, 1, :, :], q).then_inc(kq_in, 16)
            loads(sp, V, "v", 1, 2 * A_W, v_in)

        @block.gpsimd
        def _(pool):
            n = [0]

            def then(ins):
                n[0] += 1
                ins.then_inc(pool_step, 1)
                pool.wait_ge(pool_step, n[0])

            for t in (K, V, Q):
                pool.memset(t[:, 1, :, :], 0.0).then_inc(cleared, 1)
            nc_iota = dict(allow_small_or_imprecise_dtypes=True)
            then(pool.iota(dist[:, 0:1], pattern=[[0, 1]], base=P, channel_multiplier=-1, **nc_iota))
            then(pool.iota(dist[:, 1:2], pattern=[[0, 1]], base=PAST, channel_multiplier=-DIL[1][1], **nc_iota))
            then(pool.iota(dist[:, 2:3], pattern=[[0, 1]], base=PAST + N1 * DIL[2][1],
                           channel_multiplier=-DIL[2][1], **nc_iota))

            def keep(t, below, edge, fill):
                sign = -1 if below else 1
                then(pool.affine_select(out=t, in_=t, compare_op=ALU.is_ge, fill=fill,
                                        base=-sign * edge + (-1 if below else 0), pattern=[[0, 1]],
                                        channel_multiplier=sign))

            keep(dist[:, 1:2], True, N1, 0.0)
            keep(dist[:, 2:3], False, N1, 0.0)
            keep(dist[:, 2:3], True, OWN, 0.0)
            for h in range(H_G):
                then(pool.memset(sl[:, 0, h:h + 1], SLOPES[h]))
                then(pool.memset(sl[:, 1, h:h + 1], SLOPES[H_G + h]))
                keep(sl[:, 1, h:h + 1], True, N1, SLOPES[2 * H_G + h])
            then(pool.tensor_tensor(dist[:, 1:2], dist[:, 1:2], dist[:, 2:3], ALU.add))
            for x in range(2):
                then(pool.tensor_tensor(bias[:, x, :], sl[:, x, :], dist[:, x:x + 1].to_broadcast([P, H_G]),
                                        ALU.mult))
            for h in range(H_G):
                keep(bias[:, 1, h:h + 1], True, OWN + N_DIL, -NEG)
            then(pool.memset(ones[:, :], 1.0))
            then(pool.memset(head[:, :, :], 0.0))
            then(pool.affine_select(out=head[:, :, :], in_=head[:, :, :], compare_op=ALU.not_equal, fill=1.0,
                                    base=0, pattern=[[-1, H_G], [0, HD]], channel_multiplier=1))
            pool.memset(mx[:, :], 0.0).then_inc(bias_set, 1)

        @block.vector
        def _(dve):
            dve.wait_ge(kq_in, 12 * 16)
            for x in range(2):
                dve.tensor_tensor(K[:, x, :, :], K[:, x, :, :], Q[:, x, :, :], ALU.mult).then_inc(dve_step, 1)
            dve.wait_ge(dve_step, 2)
            for x in range(2):
                dve.tensor_reduce(s[:, x, :], K[:, x, :, :].rearrange("p b (h d) -> p (b h) d", d=HD), AX,
                                  ALU.add).then_inc(dve_step, 1)
            dve.wait_ge(dve_step, 4)
            dve.wait_ge(bias_set, 1)
            for x in range(2):
                sv = s[:, x, :].rearrange("p (b h) -> p b h", h=H_G)
                dve.scalar_tensor_tensor(out=sv, in0=sv, scalar=SCALE,
                                         in1=bias[:, x, :].unsqueeze(1).to_broadcast([P, DEC, H_G]),
                                         op0=ALU.mult, op1=ALU.subtract).then_inc(s_full, 1)
            dve.wait_ge(sT_full, 1)
            dve.tensor_copy(st[:, :, :], s_ps[:, :, :]).then_inc(dve_step, 1)
            dve.wait_ge(dve_step, 5)
            dve.reduce_max(mx[:, 0:1], st[:, :, :].rearrange("p a b -> p (a b)"), AX).then_inc(dve_step, 1)
            dve.wait_ge(dve_step, 6)
            dve.tensor_scalar(mx[:, 1:2], mx[:, 0:1], -1.0, None, ALU.mult).then_inc(row_full, 1)
            dve.wait_ge(p_full, 1)
            dve.reciprocal(mx[:, 3:4], mx[:, 2:3]).then_inc(dve_step, 1)
            dve.wait_ge(dve_step, 7)
            dve.tensor_scalar(st[:, :, :], st[:, :, :], mx[:, 3:4], None, ALU.mult).then_inc(pn_full, 1)
            dve.wait_ge(pT_full, 1)
            dve.tensor_copy(pT[:, :, :], pT_ps[:, :, :]).then_inc(pT_read, 1)
            dve.wait_ge(o_full, 1)
            dve.tensor_tensor(om[:, :, :], o_ps[:, :, :],
                              head[:, :, :].rearrange("p h d -> p (h d)").unsqueeze(1).to_broadcast([H_G, DEC, GW]),
                              ALU.mult).then_inc(om_full, 1)
            dve.wait_ge(oT_full, 1)
            dve.tensor_copy(oaT[:, :, SEQ:NT], oT_ps[:, :, :]).then_inc(done, 1)

        @block.scalar
        def _(act):
            act.wait_ge(row_full, 1)
            act.activation(st[:, :, :], st[:, :, :], ACT.Exp, bias=mx[:, 1:2], accum_out=mx[:, 2:3])\
                .then_inc(p_full, 1)

        @block.tensor
        def _(pe):
            pe.wait_ge(s_full, 2)
            for x in range(2):
                last = pe.transpose(s_ps[:, x, :], s[:, x, :], ident[:, :])
            last.then_inc(sT_full, 1)
            pe.wait_ge(pn_full, 1)
            for x in range(2):
                last = pe.transpose(pT_ps[:, x, :], st[:, x, :], ident[0:BH, 0:BH])
            last.then_inc(pT_full, 1)
            pe.wait_ge(pT_read, 1)
            pe.wait_ge(v_in, 6 * 16)
            for b in range(DEC):
                for x in range(2):
                    last = pe.matmul(o_ps[:, b, :], pT[:, x, b * H_G:(b + 1) * H_G], V[:, x, b, :],
                                     start=(x == 0), stop=(x == 1), skip_group_check=True)
            last.then_inc(o_full, 1)
            pe.wait_ge(om_full, 1)
            for b in range(DEC):
                for c in range(GW // P):
                    last = pe.matmul(oT_ps[:, c, b:b + 1], om[:, b, c * P:(c + 1) * P], ones[:, :],
                                     start=True, stop=True, skip_group_check=True)
            last.then_inc(oT_full, 1)


def decode_stick(nc, g):
    ctx = ExitStack()
    with ctx:
        sb = lambda n, s, d=F32: ctx.enter_context(nc.sbuf_tensor(n, s, d))
        sem = lambda n: ctx.enter_context(nc.semaphore(n))
        ps = lambda n, s: ctx.enter_context(nc.psum_tensor(n, s, F32))
        PG = PAST // PAGE
        BH = DEC * H_B
        KV = sb("e_kv", [P, DEC, PG, 2, B_W])
        Q = sb("e_q", [P, DEC, B_W])
        table = sb("e_table", [1, DEC * PG], I32)
        s = sb("e_s", [P, PG, DEC, H_B])
        bias = sb("e_bias", [BH, 1])
        z, w, r, cum = (sb("e_" + n, [BH, PAST]) for n in ("z", "w", "r", "cum"))
        aT = sb("e_aT", [P, PG, BH])
        head = sb("e_head", [H_B, H_B, HD])
        ones = sb("e_ones", [H_B, 1])
        om = sb("e_om", [H_B, DEC, B_W])
        s_ps = ps("e_s_ps", [BH, PG, P])
        aT_ps = ps("e_aT_ps", [P, PG, BH])
        o_ps = [ps(f"e_o_ps{j}", [H_B, B_W]) for j in range(4)]
        oT_ps = ps("e_oT_ps", [P, CB, DEC])
        table_in, kv_in, q_in, bias_in, dve_step, pool_step, head_set, s_full, sT_full, z_full, w_full, t_full, \
            al_full, a_full, aT_full, aT_read, o_full, om_full, oT_full, done = map(sem, (
                "e_table_in", "e_kv_in", "e_q_in", "e_bias_in", "e_dve_step", "e_pool_step", "e_head_set",
                "e_s_full", "e_sT_full", "e_z_full", "e_w_full", "e_t_full", "e_al_full", "e_a_full",
                "e_aT_full", "e_aT_read", "e_o_full", "e_om_full", "e_oT_full", "e_done"))
        ident, ztok, obT = g["ident"], g["ztok"], g["obT"]
        pages = g["cache_sb"].rearrange("a n k c h d -> (a n) k (c h d)")
        n_pool = pages.shape[0]
        block = ctx.enter_context(nc.Block())

        @block.sync
        def _(sp):
            sp.dma_start(table[:, :], g["page_table"].rearrange("(a b) p -> a (b p)", a=1)).then_inc(table_in, 16)
            sp.dma_start(Q[:, :, :], ztok[SEQ:NT, 3 * A_W:3 * A_W + B_W].unsqueeze(0)
                         .broadcast_to([P, DEC, B_W])).then_inc(q_in, 16)
            for b in range(DEC):
                sp.dma_start(bias[b * H_B:(b + 1) * H_B, :], g["b_sb"].rearrange("a (h x) -> (a h) x", x=1))\
                    .then_inc(bias_in, 16)
            sp.wait_ge(table_in, 16)
            for b in range(DEC):
                for x in range(PG):
                    page = sp.value_load(table[0:1, b * PG + x:b * PG + x + 1], min_val=0, max_val=n_pool - 1)
                    sp.dma_start(KV[:, b, x, :, :].rearrange("p c n -> p (c n)"),
                                 pages[bass.ds(page, 1), :, :].rearrange("a k n -> (a k) n")).then_inc(kv_in, 16)

        @block.gpsimd
        def _(pool):
            pool.memset(ones[:, :], 1.0).then_inc(pool_step, 1)
            pool.memset(head[:, :, :], 0.0).then_inc(pool_step, 1)
            pool.wait_ge(pool_step, 2)
            pool.affine_select(out=head[:, :, :], in_=head[:, :, :], compare_op=ALU.not_equal, fill=1.0, base=0,
                               pattern=[[-1, H_B], [0, HD]], channel_multiplier=1).then_inc(head_set, 1)

        @block.vector
        def _(dve):
            dve.wait_ge(q_in, 16)
            dve.wait_ge(kv_in, 16 * DEC * PG)
            for b in range(DEC):
                dve.tensor_tensor(KV[:, b, :, 0, :], KV[:, b, :, 0, :],
                                  Q[:, b, :].unsqueeze(1).to_broadcast([P, PG, B_W]), ALU.mult).then_inc(dve_step, 1)
            dve.wait_ge(dve_step, DEC)
            for b in range(DEC):
                for x in range(PG):
                    dve.tensor_reduce(s[:, x, b, :], KV[:, b, x, 0, :].rearrange("p (h d) -> p h d", d=HD), AX,
                                      ALU.add).then_inc(s_full, 1)
            dve.wait_ge(z_full, 1)
            dve.tensor_scalar(w[:, :].bitcast(I32), z[:, :].bitcast(I32), 0x7FFFFFFF, None, ALU.bitwise_and)\
                .then_inc(w_full, 1)
            dve.tensor_scalar(r[:, :], z[:, :], 0.0, None, ALU.max).then_inc(dve_step, 1)
            dve.wait_ge(dve_step, DEC + 1)
            dve.wait_ge(t_full, 2)
            dve.tensor_tensor_scan(cum[:, ::-1], w[:, ::-1], r[:, ::-1], 0.0, ALU.add, ALU.add).then_inc(dve_step, 1)
            dve.wait_ge(dve_step, DEC + 2)
            dve.tensor_tensor(z[:, :], z[:, :], cum[:, :], ALU.subtract).then_inc(al_full, 1)
            dve.wait_ge(aT_full, 1)
            dve.tensor_copy(aT[:, :, :], aT_ps[:, :, :]).then_inc(aT_read, 1)
            dve.wait_ge(head_set, 1)
            for b in range(DEC):
                dve.wait_ge(o_full, b + 1)
                dve.tensor_tensor(om[:, b, :], o_ps[b % 4][:, :], head[:, :, :].rearrange("p h d -> p (h d)"),
                                  ALU.mult).then_inc(om_full, 1)
            dve.wait_ge(oT_full, 1)
            dve.tensor_copy(obT[:, :, SEQ:NT], oT_ps[:, :, :]).then_inc(done, 1)

        @block.scalar
        def _(act):
            act.preload_act_table_set("natural_log_exp_and_others")
            act.wait_ge(sT_full, 1)
            act.wait_ge(bias_in, 16 * DEC)
            act.activation(z[:, :], s_ps[:, :, :].rearrange("p a b -> p (a b)"), ACT.Identity, scale=SCALE,
                           bias=bias[:, :]).then_inc(z_full, 1)
            act.wait_ge(w_full, 1)
            act.activation(w[:, :], w[:, :], ACT.Exp, scale=-1.0).then_inc(t_full, 1)
            act.wait_ge(t_full, 1)
            act.activation(w[:, :], w[:, :], ACT.Ln, bias=1.0).then_inc(t_full, 1)
            act.wait_ge(al_full, 1)
            act.activation(z[:, :], z[:, :], ACT.Exp).then_inc(a_full, 1)

        @block.tensor
        def _(pe):
            pe.wait_ge(s_full, DEC * PG)
            for x in range(PG):
                last = pe.transpose(s_ps[:, x, :], s[:, x, :, :].rearrange("p b h -> p (b h)"), ident[:, :])
            last.then_inc(sT_full, 1)
            pe.wait_ge(a_full, 1)
            for x in range(PG):
                last = pe.transpose(aT_ps[:, x, :], z[:, x * P:(x + 1) * P], ident[0:BH, 0:BH])
            last.then_inc(aT_full, 1)
            pe.wait_ge(aT_read, 1)
            for b in range(DEC):
                need(pe, om_full, b - 3)
                for x in range(PG):
                    last = pe.matmul(o_ps[b % 4][:, :], aT[:, x, b * H_B:(b + 1) * H_B], KV[:, b, x, 1, :],
                                     start=(x == 0), stop=(x == PG - 1))
                last.then_inc(o_full, 1)
            pe.wait_ge(om_full, DEC)
            for b in range(DEC):
                for c in range(CB):
                    last = pe.matmul(oT_ps[:, c, b:b + 1], om[:, b, c * P:(c + 1) * P], ones[:, :],
                                     start=True, stop=True, skip_group_check=True)
            last.then_inc(oT_full, 1)


def merge(nc, g):
    ctx = ExitStack()
    with ctx:
        sb = lambda n, s, d=F32: ctx.enter_context(nc.sbuf_tensor(n, s, d))
        sem = lambda n: ctx.enter_context(nc.semaphore(n))
        KA, KB = 2, CB
        PASSES = KD // 2
        U = 2 * NSPLIT
        wa = sb("m_wa", [P, 2, KD, P])
        wb = sb("m_wb", [P, 2, KD, P])
        woa = sb("m_woa", [P, 2, KA, P])
        wob = sb("m_wob", [P, 2, KB, P])
        sig = sb("m_sig", [P, 2, 2, NS])
        part = sb("m_part", [P, 2, 2, NS])
        bank = [[ctx.enter_context(nc.psum_tensor(f"m_{n}{j}", [P, 512], F32)) for n in ("ga", "ya", "gb", "yb")]
                for j in range(2)]
        w_in = [sem(f"m_w_in{j}") for j in range(2)]
        full, sig_full, part_full, merged = map(sem, ("m_full", "m_sig_full", "m_part_full", "m_merged"))
        uT, oaT, obT, mT = g["uT"], g["oaT"], g["obT"], g["mT"]
        kp = lambda t: g[t].rearrange("a (k p) n -> p (a k) n", p=P)
        block = ctx.enter_context(nc.Block())

        @block.sync
        def _(sp):
            def load(it, b):
                c = (it * 2 + b) * P
                need(sp, full, it * U + (b + 1) * NSPLIT - U)
                for dst, w, c0 in ((wa, "w_in", QKV), (wb, "w_in", QKV + D), (woa, "w_oa", 0), (wob, "w_ob", 0)):
                    sp.dma_start(dst[:, b, :, :], kp(w)[:, :, bass.ds(c + c0, P)]).then_inc(w_in[b], 16)

            for b in range(2):
                load(0, b)
            with sp.Fori(1, PASSES) as it:
                for b in range(2):
                    load(it, b)

        @block.tensor
        def _(pe):
            def step(it):
                for b in range(2):
                    pe.wait_ge(w_in[b], it * 64 + 64)
                    for s in range(NSPLIT):
                        j = b * NSPLIT + s
                        need(pe, part_full, it * (2 * U) + (2 * j - 2))
                        t = slice(s * NS, (s + 1) * NS)
                        for x, (w, act, n) in enumerate(((wa, uT, KD), (woa, oaT, KA), (wb, uT, KD), (wob, obT, KB))):
                            for k in range(n):
                                last = pe.matmul(bank[j % 2][x][:, 0:NS], w[:, b, k, :], act[:, k, t],
                                                 start=(k == 0), stop=(k == n - 1))
                        last.then_inc(full, 1)

            looped(pe, PASSES, step)

        @block.scalar
        def _(act):
            def step(it):
                for j in range(U):
                    u = it * U + j
                    act.wait_ge(full, u + 1)
                    need(act, part_full, it * (2 * U) + (2 * j - 2))
                    for x in range(2):
                        act.activation(sig[:, j % 2, x, :], bank[j % 2][2 * x][:, 0:NS], ACT.Sigmoid)\
                           .then_inc(sig_full, 1)

            looped(act, PASSES, step)

        @block.vector
        def _(dve):
            def step(it):
                for j in range(U):
                    need(dve, merged, it * U + (j - 1))
                    for x in range(2):
                        dve.wait_ge(sig_full, it * (2 * U) + (2 * j + x + 1))
                        dve.tensor_tensor(part[:, j % 2, x, :], sig[:, j % 2, x, :], bank[j % 2][2 * x + 1][:, 0:NS],
                                          ALU.mult).then_inc(part_full, 1)

            looped(dve, PASSES, step)

        @block.gpsimd
        def _(pool):
            def step(it):
                for j in range(U):
                    pool.wait_ge(part_full, it * (2 * U) + (2 * j + 2))
                    s = j % NSPLIT
                    pool.tensor_tensor(mT[:, bass.ds(it * 2 + j // NSPLIT, 1), s * NS:(s + 1) * NS]
                                       .rearrange("p a n -> p (a n)"), part[:, j % 2, 0, :], part[:, j % 2, 1, :],
                                       ALU.add).then_inc(merged, 1)

            looped(pool, PASSES, step)


def residual(nc, g, x_of):
    ctx = ExitStack()
    with ctx:
        sb = lambda n, s, d=F32: ctx.enter_context(nc.sbuf_tensor(n, s, d))
        sem = lambda n: ctx.enter_context(nc.semaphore(n))
        ps = lambda n, s: ctx.enter_context(nc.psum_tensor(n, s, F32))
        w = sb("r_w", [P, KD, D])
        wr = sb("r_wr", [P, KD, NR])
        br = sb("r_br", [P, NR])
        gm = sb("r_gm", [P, KD])
        xt = sb("r_xt", [P, 2, D])
        sq = sb("r_sq", [P, D])
        st = sb("r_st", [P, 3, TT])
        u2T = sb("r_u2T", [P, 2, KD, P])
        acc = [ps(f"r_acc{j}", [P, D]) for j in range(2)]
        tp = ps("r_tp", [P, KD, P])
        lg = ps("r_lg", [P, 64])
        w_in = [sem(f"r_w_in{j}") for j in range(2)]
        x_in = [sem(f"r_x_in{j}") for j in range(2)]
        small_in, acc_full, h_full, ssq, mean, root, inv, u2_full, tp_full, u2T_full, lg_full, lg_read, cleared = \
            map(sem, ("r_small_in", "r_acc_full", "r_h_full", "r_ssq", "r_mean", "r_root", "r_inv", "r_u2_full",
                      "r_tp_full", "r_u2T_full", "r_lg_full", "r_lg_read", "r_cleared"))
        h, u2, logit, mT, ident = g["h"], g["u2"], g["logit"], g["mT"], g["ident"]
        kp = lambda t: g[t].rearrange("a (k p) n -> p (a k) n", p=P)
        block = ctx.enter_context(nc.Block())

        @block.sync
        def _(sp):
            for c in range(2):
                sp.dma_start(w[:, :, c * 512:(c + 1) * 512], kp("w_out")[:, :, c * 512:(c + 1) * 512])\
                    .then_inc(w_in[c], 16)
            with nc.allow_non_contiguous_dma(reason="1024 gains, once"):
                sp.dma_start(gm[:, :], g["g_moe"].rearrange("a (k p) -> p (a k)", p=P)).then_inc(small_in, 16)
            sp.dma_start(wr[:, :, 0:NG], kp("w_rg")).then_inc(small_in, 16)
            sp.dma_start(wr[:, :, NG:NR], kp("w_re")).then_inc(small_in, 16)
            sp.dma_start(br[:, 0:NG], g["b_rg"].broadcast_to([P, NG])).then_inc(small_in, 16)
            sp.dma_start(br[:, NG:NR], g["b_re"].broadcast_to([P, NE])).then_inc(small_in, 16)
            for t in range(TT):
                need(sp, h_full, t - 1)
                sp.dma_start(xt[0:rows(t), t % 2, :], x_of(t)).then_inc(x_in[t % 2], 16)

        @block.tensor
        def _(pe):
            for t in range(TT + 2):
                if t < TT:
                    r = rows(t)
                    need(pe, h_full, t - 1)
                    for c in range(2):
                        if t == 0:
                            pe.wait_ge(w_in[c], 16)
                        for k in range(KD):
                            last = pe.matmul(acc[t % 2][0:r, c * 512:(c + 1) * 512], mT[:, k, t * P:t * P + r],
                                             w[:, k, c * 512:(c + 1) * 512], start=(k == 0), stop=(k == KD - 1))
                    last.then_inc(acc_full, 1)
                if 1 <= t <= TT:
                    v, r = t - 1, rows(t - 1)
                    pe.wait_ge(u2_full, v + 1)
                    need(pe, u2T_full, v)
                    for k in range(KD):
                        last = pe.transpose(tp[:, k, 0:r], u2[0:r, v, k * P:(k + 1) * P], ident[0:r, 0:r])
                    last.then_inc(tp_full, 1)
                if t >= 2:
                    v, r = t - 2, rows(t - 2)
                    if v == 0:
                        pe.wait_ge(small_in, 16 * 5)
                    pe.wait_ge(u2T_full, v + 1)
                    need(pe, lg_read, v)
                    for k in range(KD):
                        last = pe.matmul(lg[0:r, 0:NR], u2T[:, v % 2, k, 0:r], wr[:, k, :],
                                         start=(k == 0), stop=(k == KD - 1))
                    last.then_inc(lg_full, 1)

        @block.scalar
        def _(act):
            for t in range(TT):
                r = rows(t)
                act.wait_ge(h_full, t + 1)
                need(act, ssq, t)
                act.activation(sq[0:r, :], h[0:r, t, :], ACT.Square, accum_out=st[0:r, 0, t:t + 1]).then_inc(ssq, 1)
                act.wait_ge(mean, t + 1)
                act.activation(st[0:r, 1, t:t + 1], st[0:r, 1, t:t + 1], ACT.Sqrt).then_inc(root, 1)

        @block.vector
        def _(dve):
            dve.wait_ge(small_in, 16 * 5)
            dve.wait_ge(cleared, 1)
            for t in range(TT + 2):
                if t < TT:
                    r = rows(t)
                    dve.wait_ge(x_in[t % 2], 16 * (t // 2 + 1))
                    dve.wait_ge(acc_full, t + 1)
                    dve.tensor_tensor(h[0:r, t, :], xt[0:r, t % 2, :], acc[t % 2][0:r, :], ALU.add).then_inc(h_full, 1)
                    dve.wait_ge(ssq, t + 1)
                    dve.tensor_scalar(st[0:r, 1, t:t + 1], st[0:r, 0, t:t + 1], 1.0 / D, EPS, ALU.mult,
                                      ALU.add).then_inc(mean, 1)
                    dve.wait_ge(root, t + 1)
                    dve.reciprocal(st[0:r, 2, t:t + 1], st[0:r, 1, t:t + 1]).then_inc(inv, 1)
                    dve.wait_ge(inv, t + 1)
                    dve.tensor_scalar(u2[0:r, t, :], h[0:r, t, :], st[0:r, 2, t:t + 1], None, ALU.mult)\
                        .then_inc(u2_full, 1)
                if 1 <= t <= TT:
                    v, r = t - 1, rows(t - 1)
                    dve.wait_ge(tp_full, v + 1)
                    need(dve, lg_full, v - 1)
                    dve.tensor_tensor(u2T[:, v % 2, :, 0:r], tp[:, :, 0:r],
                                      gm[:, :].unsqueeze(2).to_broadcast([P, KD, r]), ALU.mult).then_inc(u2T_full, 1)
                if t >= 2:
                    v, r = t - 2, rows(t - 2)
                    dve.wait_ge(lg_full, v + 1)
                    dve.tensor_tensor(logit[0:r, v, :], lg[0:r, 0:NR], br[0:r, :], ALU.add).then_inc(lg_read, 1)

        @block.gpsimd
        def _(pool):
            pool.memset(logit[:, QT, :], 0.0).then_inc(cleared, 1)


def route(nc, g):
    ctx = ExitStack()
    with ctx:
        sb = lambda n, s, d=F32: ctx.enter_context(nc.sbuf_tensor("t_" + n, s, d))
        sem = lambda n: ctx.enter_context(nc.semaphore("t_" + n))
        T4, T32 = [P, TT, NG], [P, TT, NE]
        gmax, ghit, gden, gprob, m1, m2, hit, e2 = (sb(n, [P, TT]) for n in (
            "gmax", "ghit", "gden", "gprob", "m1", "m2", "hit", "e2"))
        a4, oh4 = sb("a4", T4), sb("oh4", T4)
        el, a32, oh1, oh2, both, pos = (sb(n, T32) for n in ("el", "a32", "oh1", "oh2", "both", "pos"))
        desc = sb("desc", [P, NE])
        real = sb("real", [P, TT])
        tri = sb("tri", [P, P])
        ones = sb("ones", [P, P])
        zero = sb("zero", [P, NE])
        run = sb("run", [P, TT + 1, NE])
        tot = sb("tot", T32)
        cnt, start, nblk, nbi, nbe, c32, o32 = (sb(n, [P, NE]) for n in (
            "cnt", "start", "nblk", "nbi", "nbe", "c32", "o32"))
        thr = sb("thr", [P, 64])
        cmp9 = sb("cmp9", [P, NE, TT])
        cmpm = sb("cmpm", [P, MAXBLK // 2 + 2])
        me = sb("me", [P, 1])
        metaf = sb("metaf", [P, 4])
        metai = sb("metai", [P, 4], I32)
        destf = sb("destf", [P, 2, TT])
        fill = sb("fill", [P, D])
        rank_ps = ctx.enter_context(nc.psum_tensor("t_rank_ps", [P, 512], F32))
        tot_ps = ctx.enter_context(nc.psum_tensor("t_tot_ps", [P, 512], F32))
        const, step_, gexp_in, gexp, eexp_in, eexp, both_full, sums, dest_set, meta_set, meta_out = map(sem, (
            "const", "step", "gexp_in", "gexp", "eexp_in", "eexp", "both_full", "sums", "dest_set", "meta_set",
            "meta_out"))
        moved = g["pool_dma"][2]
        logit, u2, dest, wt, xs, ys, meta, meta_row = (g[n] for n in (
            "logit", "u2", "dest", "wt", "xs", "ys", "meta", "meta_row"))
        block = ctx.enter_context(nc.Block())
        NTHR = max(TT, MAXBLK // 2 + 2)

        @block.gpsimd
        def _(pool):
            n = [0]

            def then(ins):
                n[0] += 1
                ins.then_inc(const, 1)
                pool.wait_ge(const, n[0])

            kw = dict(allow_small_or_imprecise_dtypes=True)
            then(pool.iota(desc[:, :], pattern=[[-1, NE]], base=NE, channel_multiplier=0, **kw))
            then(pool.iota(thr[:, 0:NTHR], pattern=[[P, NTHR]], base=0, channel_multiplier=0, **kw))
            then(pool.iota(me[:, :], pattern=[[0, 1]], base=0, channel_multiplier=1, **kw))
            then(pool.memset(zero[:, :], 0.0))
            then(pool.memset(real[:, :], 1.0))
            then(pool.affine_select(out=real[:, QT:TT], in_=real[:, QT:TT], compare_op=ALU.is_ge, fill=0.0,
                                    base=DEC - 1, pattern=[[0, 1]], channel_multiplier=-1))
            then(pool.memset(ones[:, :], 1.0))
            then(pool.memset(tri[:, :], 1.0))
            then(pool.affine_select(out=tri[:, :], in_=tri[:, :], compare_op=ALU.is_gt, fill=0.0, base=0,
                                    pattern=[[1, P]], channel_multiplier=-1))
            then(pool.memset(fill[:, :], 0.0))
            pool.dma_start(xs[ASG:SLOTS, :], fill[:, :]).then_inc(moved, 16)
            for b in range(2):
                pool.dma_start(ys[ASG + b * 64:ASG + b * 64 + 64, :], fill[0:64, :])\
                    .then_inc(g["pool_dma"][3 + b], 16)
            pool.wait_ge(dest_set, 2)
            for t in range(TT):
                for c in range(2):
                    pool.indirect_dma_start(xs[:, :], bass.IndirectOffsetOnAxis(ap=dest[0:rows(t), c, t:t + 1], axis=0),
                                            u2[0:rows(t), t, :], None).then_inc(moved, 16)
            pool.wait_ge(moved, 16 * (2 * TT + 1))
            for b in range(2):
                pool.wait_ge(g["pool_dma"][3 + b], 16)

        @block.sync
        def _(sp):
            sp.wait_ge(meta_set, 1)
            sp.dma_start(meta, metai[:, :]).then_inc(meta_out, 16)
            sp.wait_ge(meta_out, 16)
            sp.dma_start(meta_row[:, :], meta.rearrange("(a p) c -> a (p c)", a=1)).then_inc(meta_out, 16)
            sp.wait_ge(meta_out, 32)

        @block.scalar
        def _(act):
            act.wait_ge(gexp_in, 1)
            act.activation(a4[:, :, :], a4[:, :, :], ACT.Exp).then_inc(gexp, 1)
            act.wait_ge(eexp_in, 1)
            act.activation(e2[:, :], e2[:, :], ACT.Exp).then_inc(eexp, 1)

        @block.tensor
        def _(pe):
            pe.wait_ge(both_full, 1)
            b = both[:, :, :].rearrange("p t e -> p (t e)")
            pe.matmul(rank_ps[:, 0:TT * NE], tri[:, :], b, start=True, stop=True)
            pe.matmul(tot_ps[:, 0:TT * NE], ones[:, :], b, start=True, stop=True).then_inc(sums, 1)

        @block.vector
        def _(dve):
            n = [0]

            def then(ins):
                n[0] += 1
                ins.then_inc(step_, 1)
                dve.wait_ge(step_, n[0])

            wide = lambda t, w: t.unsqueeze(2).to_broadcast([P, TT, w])
            over_t = lambda t, w: t.unsqueeze(1).to_broadcast([P, TT, w])
            g4, e32 = logit[:, :, 0:NG], logit[:, :, NG:NR]

            def first_max(src, width, mx, tmp, out):
                then(dve.tensor_reduce(mx[:, :], src, AX, ALU.max))
                then(dve.tensor_tensor(tmp, src, wide(mx[:, :], width), ALU.is_equal))
                then(dve.tensor_tensor(tmp, tmp, over_t(desc[:, 0:width], width), ALU.mult))
                then(dve.tensor_reduce(hit[:, :], tmp, AX, ALU.max))
                then(dve.tensor_tensor(out, tmp, wide(hit[:, :], width), ALU.is_equal))

            dve.wait_ge(const, 10)
            first_max(g4, NG, gmax, a4[:, :, :], oh4[:, :, :])
            dve.tensor_tensor(a4[:, :, :], g4, wide(gmax[:, :], NG), ALU.subtract).then_inc(gexp_in, 1)
            ohe = oh4[:, :, :].unsqueeze(3).to_broadcast([P, TT, NG, EPG])
            four = lambda t: t.rearrange("p t (a b) -> p t a b", b=EPG)
            then(dve.tensor_copy(four(a32[:, :, :]), ohe))
            then(dve.tensor_tensor(el[:, :, :], e32, a32[:, :, :], ALU.mult))
            then(dve.tensor_scalar(a32[:, :, :], a32[:, :, :], -NEG, NEG, ALU.mult, ALU.add))
            then(dve.tensor_tensor(el[:, :, :], el[:, :, :], a32[:, :, :], ALU.add))
            first_max(el[:, :, :], NE, m1, a32[:, :, :], oh1[:, :, :])
            then(dve.scalar_tensor_tensor(out=el[:, :, :], in0=oh1[:, :, :], scalar=3 * NEG, in1=el[:, :, :],
                                          op0=ALU.mult, op1=ALU.add))
            first_max(el[:, :, :], NE, m2, a32[:, :, :], oh2[:, :, :])
            dve.tensor_tensor(e2[:, :], m2[:, :], m1[:, :], ALU.subtract).then_inc(eexp_in, 1)
            then(dve.tensor_tensor(both[:, :, :], oh1[:, :, :], oh2[:, :, :], ALU.add))
            dve.tensor_tensor(both[:, :, :], both[:, :, :], wide(real[:, :], NE), ALU.mult).then_inc(both_full, 1)
            dve.wait_ge(gexp, 1)
            then(dve.tensor_reduce(gden[:, :], a4[:, :, :], AX, ALU.add))
            dve.wait_ge(eexp, 1)
            then(dve.tensor_scalar(m1[:, :], e2[:, :], 1.0, None, ALU.add))
            then(dve.tensor_tensor(gden[:, :], gden[:, :], m1[:, :], ALU.mult))
            then(dve.reciprocal(wt[:, 0, :], gden[:, :]))
            then(dve.tensor_tensor(wt[:, 1, :], wt[:, 0, :], e2[:, :], ALU.mult))
            dve.wait_ge(sums, 1)
            flat = lambda t: t[:, :, :].rearrange("p t e -> p (t e)")
            then(dve.tensor_copy(flat(tot), tot_ps[:, 0:TT * NE]))
            then(dve.tensor_reduce(cnt[:, :], tot[:, :, :].rearrange("p t e -> p e t"), AX, ALU.add))
            then(dve.tensor_tensor_scan(start[:, :], cnt[:, :], zero[:, :], 0.0, ALU.add, ALU.add))
            then(dve.tensor_tensor(start[:, :], start[:, :], cnt[:, :], ALU.subtract))
            then(dve.tensor_copy(run[:, 0, :], start[:, :]))
            for t in range(TT):
                then(dve.tensor_tensor(run[:, t + 1, :], run[:, t, :], tot[:, t, :], ALU.add))
            then(dve.tensor_tensor(flat(pos), run[:, 0:TT, :].rearrange("p t e -> p (t e)"), rank_ps[:, 0:TT * NE],
                                   ALU.add))
            for c, oh in enumerate((oh1, oh2)):
                then(dve.tensor_tensor(a32[:, :, :], oh[:, :, :], pos[:, :, :], ALU.mult))
                then(dve.tensor_reduce(destf[:, c, :], a32[:, :, :], AX, ALU.add))
                dve.tensor_copy(dest[:, c, :], destf[:, c, :]).then_inc(dest_set, 1)
            then(dve.tensor_tensor(cmp9[:, :, :], cnt[:, :].unsqueeze(2).to_broadcast([P, NE, TT]),
                                   thr[:, 0:TT].unsqueeze(1).to_broadcast([P, NE, TT]), ALU.is_gt))
            then(dve.tensor_reduce(nblk[:, :], cmp9[:, :, :], AX, ALU.add))
            then(dve.tensor_tensor_scan(nbi[:, :], nblk[:, :], zero[:, :], 0.0, ALU.add, ALU.add))
            then(dve.tensor_tensor(nbe[:, :], nbi[:, :], nblk[:, :], ALU.subtract))
            then(dve.tensor_scalar(c32[:, :], nbi[:, :], me[:, :], None, ALU.is_le))
            then(dve.tensor_reduce(metaf[:, 0:1], c32[:, :], AX, ALU.add))
            then(dve.tensor_scalar(metaf[:, 0:1], metaf[:, 0:1], float(NE - 1), None, ALU.min))
            then(dve.tensor_scalar(o32[:, :], nbe[:, :], me[:, :], None, ALU.is_le))
            then(dve.tensor_tensor(o32[:, :], o32[:, :], c32[:, :], ALU.subtract))
            then(dve.scalar_tensor_tensor(out=c32[:, :], in0=nbe[:, :], scalar=-float(P), in1=start[:, :],
                                          op0=ALU.mult, op1=ALU.add))
            then(dve.tensor_tensor(c32[:, :], c32[:, :], o32[:, :], ALU.mult))
            then(dve.tensor_reduce(metaf[:, 1:2], c32[:, :], AX, ALU.add))
            then(dve.scalar_tensor_tensor(out=metaf[:, 1:2], in0=me[:, :], scalar=float(P), in1=metaf[:, 1:2],
                                          op0=ALU.mult, op1=ALU.add))
            then(dve.tensor_scalar(metaf[:, 1:2], metaf[:, 1:2], float(ASG), None, ALU.min))
            then(dve.tensor_scalar(metaf[:, 3:4], nbi[:, NE - 1:NE], float(P // 2), None, ALU.mult))
            then(dve.tensor_scalar(cmpm[:, :], thr[:, 0:MAXBLK // 2 + 2], metaf[:, 3:4], None, ALU.is_lt))
            then(dve.tensor_reduce(metaf[:, 2:3], cmpm[:, :], AX, ALU.add))
            then(dve.tensor_scalar(metaf[:, 2:3], metaf[:, 2:3], -1.0, None, ALU.add))
            dve.tensor_copy(metai[:, :], metaf[:, :]).then_inc(meta_set, 1)


def experts(nc, g):
    ctx = ExitStack()
    with ctx:
        sb = lambda n, s, d=F32: ctx.enter_context(nc.sbuf_tensor("x_" + n, s, d))
        sem = lambda n: ctx.enter_context(nc.semaphore("x_" + n))
        ps = lambda n, s: ctx.enter_context(nc.psum_tensor("x_" + n, s, F32))
        wg, wu = (sb(n, [P, 2, KD, FE]) for n in ("wg", "wu"))
        wd = sb("wd", [P, 2, KF, D])
        gm = sb("gm", [P, KD])
        x = sb("x", [P, 2, D])
        xT = sb("xT", [P, 2, KD, P])
        sg, gs, hm = (sb(n, [P, FE]) for n in ("sg", "gs", "hm"))
        hT = sb("hT", [P, KF, P])
        y = sb("y", [P, 2, D])
        tpx = [ps(f"tpx{j}", [P, 4, P]) for j in range(2)]
        G, U_ = ps("G", [P, FE]), ps("U", [P, FE])
        tph = ps("tph", [P, KF, P])
        Y = [ps(f"Y{j}", [P, 512]) for j in range(2)]
        x_in, gu_in, d_in = ([sem(f"{n}{b}") for b in range(2)] for n in ("x_in", "gu_in", "d_in"))
        y_out = g["pool_dma"][3:5]
        gm_in, tpx_full, xT_full, g_full, u_full, sg_full, gs_full, hm_full, tph_full, hT_full, y_full, y_read = map(
            sem, ("gm_in", "tpx_full", "xT_full", "g_full", "u_full", "sg_full", "gs_full", "hm_full", "tph_full",
                  "hT_full", "y_full", "y_read"))
        xs, ys, meta_row, ident = g["xs"], g["ys"], g["meta_row"], g["ident"]
        Wg = g["w_gate"].rearrange("a e (k p) f -> (a e) p k f", p=P)
        Wu = g["w_up"].rearrange("a e (k p) f -> (a e) p k f", p=P)
        Wd = g["w_down"].rearrange("a e (k p) f -> (a e) p k f", p=P)
        block = ctx.enter_context(nc.Block())

        def pairs(eng):
            return eng.value_load(meta_row[0:1, 2:3], min_val=(-(-ASG // P) + 1) // 2 - 1,
                                  max_val=(MAXBLK + 1) // 2 - 1) + 1

        def passes(eng, step, end):
            n = pairs(eng)
            for j in range(2):
                step(0, j)
            with eng.Fori(1, n) as it:
                for j in range(2):
                    step(it, j)
            if end:
                end(n)

        @block.sync
        def _(sp):
            with nc.allow_non_contiguous_dma(reason="1024 gains, once"):
                sp.dma_start(gm[:, :], g["g_moe"].rearrange("a (k p) -> p (a k)", p=P)).then_inc(gm_in, 16)

            def step(it, b):
                n = it * 2 + b
                col = n * 4
                e = sp.value_load(meta_row[0:1, bass.ds(col, 1)], min_val=0, max_val=NE - 1)
                row = sp.value_load(meta_row[0:1, bass.ds(col + 1, 1)], min_val=0, max_val=ASG)
                w = lambda W: W[bass.ds(e, 1), :, :, :].rearrange("a p k f -> (a p) k f")
                need(sp, tpx_full, it * 4 + (2 * b - 2))
                sp.dma_start(x[:, b, :], xs[bass.ds(row, P), :]).then_inc(x_in[b], 16)
                need(sp, u_full, it * 2 + (b - 1))
                sp.dma_start(wg[:, b, :, :], w(Wg)).then_inc(gu_in[b], 16)
                sp.dma_start(wu[:, b, :, :], w(Wu)).then_inc(gu_in[b], 16)
                need(sp, y_full, it * 4 + (2 * b - 2))
                sp.dma_start(wd[:, b, :, :], w(Wd)).then_inc(d_in[b], 16)

            passes(sp, step, None)

        @block.tensor
        def _(pe):
            def turn(it, b):
                pe.wait_ge(x_in[b], it * 16 + 16)
                for c in range(2):
                    need(pe, xT_full, it * 4 + (2 * b + c - 1))
                    for k in range(4):
                        last = pe.transpose(tpx[c][:, k, :], x[:, b, (c * 4 + k) * P:(c * 4 + k + 1) * P], ident[:, :])
                    last.then_inc(tpx_full, 1)

            def gate_up(p_, b, n):
                pe.wait_ge(gu_in[b], p_ * 32 + 32)
                pe.wait_ge(xT_full, n * 2 + 2)
                need(pe, hm_full, n)
                for bank, w, s in ((G, wg, g_full), (U_, wu, u_full)):
                    for k in range(KD):
                        last = pe.matmul(bank[:, :], xT[:, b, k, :], w[:, b, k, :], start=(k == 0),
                                         stop=(k == KD - 1))
                    last.then_inc(s, 1)

            def down(p_, b, n):
                pe.wait_ge(hm_full, n + 1)
                need(pe, hT_full, n)
                for k in range(KF):
                    last = pe.transpose(tph[:, k, :], hm[:, k * P:(k + 1) * P], ident[:, :])
                last.then_inc(tph_full, 1)
                pe.wait_ge(d_in[b], p_ * 16 + 16)
                pe.wait_ge(hT_full, n + 1)
                for c in range(2):
                    need(pe, y_read, n * 2 - 1 + c)
                    for k in range(KF):
                        last = pe.matmul(Y[c][:, :], hT[:, k, :], wd[:, b, k, c * 512:(c + 1) * 512],
                                         start=(k == 0), stop=(k == KF - 1))
                    last.then_inc(y_full, 1)

            def step(it, j):
                behind = j or not isinstance(it, int)
                p_, b, n = (it, 0, it * 2) if j else (it - 1, 1, it * 2 - 1)
                if behind:
                    gate_up(p_, b, n)
                turn(it, j)
                if behind:
                    down(p_, b, n)

            def end(np_):
                gate_up(np_ - 1, 1, np_ * 2 - 1)
                down(np_ - 1, 1, np_ * 2 - 1)

            passes(pe, step, end)

        @block.scalar
        def _(act):
            def late(p_, b, n):
                act.wait_ge(g_full, n + 1)
                need(act, gs_full, n)
                act.activation(sg[:, :], G[:, :], ACT.Sigmoid).then_inc(sg_full, 1)
                act.wait_ge(y_out[b], p_ * 16 + 16)
                for c in range(2):
                    act.wait_ge(y_full, n * 2 + c + 1)
                    act.activation(y[:, b, c * 512:(c + 1) * 512], Y[c][:, :], ACT.Copy).then_inc(y_read, 1)

            def step(it, j):
                if j or not isinstance(it, int):
                    late(*((it, 0, it * 2) if j else (it - 1, 1, it * 2 - 1)))

            passes(act, step, lambda n: late(n - 1, 1, n * 2 - 1))

        @block.vector
        def _(dve):
            dve.wait_ge(gm_in, 16)

            def turn(it, b):
                n = it * 2 + b
                need(dve, u_full, it * 2 + (b - 1))
                for c in range(2):
                    dve.wait_ge(tpx_full, n * 2 + c + 1)
                    dve.tensor_tensor(xT[:, b, c * 4:(c + 1) * 4, :], tpx[c][:, :, :],
                                      gm[:, c * 4:(c + 1) * 4].unsqueeze(2).to_broadcast([P, 4, P]),
                                      ALU.mult).then_inc(xT_full, 1)

            def hidden(n):
                dve.wait_ge(sg_full, n + 1)
                dve.tensor_tensor(gs[:, :], sg[:, :], G[:, :], ALU.mult).then_inc(gs_full, 1)
                dve.wait_ge(u_full, n + 1)
                dve.wait_ge(gs_full, n + 1)
                need(dve, tph_full, n)
                dve.tensor_tensor(hm[:, :], gs[:, :], U_[:, :], ALU.mult).then_inc(hm_full, 1)

            def hidden_T(n):
                dve.wait_ge(tph_full, n + 1)
                need(dve, y_full, n * 2)
                dve.tensor_copy(hT[:, :, :], tph[:, :, :]).then_inc(hT_full, 1)

            def step(it, j):
                behind = j or not isinstance(it, int)
                n = it * 2 - 1 + j
                if behind:
                    hidden(n)
                turn(it, j)
                if behind:
                    hidden_T(n)

            def end(np_):
                hidden(np_ * 2 - 1)
                hidden_T(np_ * 2 - 1)

            passes(dve, step, end)

        @block.gpsimd
        def _(pool):
            def step(it, b):
                n = it * 2 + b
                row = pool.value_load(meta_row[0:1, bass.ds(n * 4 + 1, 1)], min_val=0, max_val=ASG)
                pool.wait_ge(y_read, n * 2 + 2)
                if b:
                    pool.wait_ge(y_out[0], it * 16 + 32)
                else:
                    pool.wait_ge(y_out[1], it * 16 + 16)
                pool.dma_start(ys[bass.ds(row, P), :], y[:, b, :]).then_inc(y_out[b], 16)

            def end(np_):
                for b in range(2):
                    pool.wait_ge(y_out[b], np_ * 16 + 16)
                pool.wait_ge(gm_in, 16)

            passes(pool, step, end)


def finish(nc, g, p_of, y_of):
    ctx = ExitStack()
    with ctx:
        sb = lambda n, s, d=F32: ctx.enter_context(nc.sbuf_tensor("f_" + n, s, d))
        sem = lambda n: ctx.enter_context(nc.semaphore("f_" + n))
        ps = lambda n, s: ctx.enter_context(nc.psum_tensor("f_" + n, s, F32))
        KP = PLE // P
        wpg = sb("wpg", [P, KD, D])
        wpp = sb("wpp", [P, KP, D])
        gp = sb("gp", [P, KD])
        gf = sb("gf", [P, D])
        y2 = sb("y2", [P, 2, 2, D])
        pt = sb("pt", [P, 2, PLE])
        pT = sb("pT", [P, 2, KP, P])
        sq = sb("sq", [P, D])
        st = sb("st", [P, 6, TT])
        un = sb("un", [P, 2, D])
        uT = sb("uT", [P, 2, KD, P])
        sig = sb("sig", [P, D])
        yo = sb("yo", [P, 2, D])
        tp = ps("tp", [P, KD, P])
        gate = ps("gate", [P, D])
        pp = ps("pp", [P, D])
        tpp = ps("tpp", [P, KP, P])
        gp_in, gf_in, pg_in, pp_in, ssq, mean, root, inv, un_full, tp_full, uT_full, tpp_full, pT_full, \
            gate_full, pp_full, sig_full, mix, h_full, ssq2, mean2, root2, inv2, yo_full = map(sem, (
                "gp_in", "gf_in", "pg_in", "pp_in", "ssq", "mean", "root", "inv", "un_full", "tp_full", "uT_full",
                "tpp_full", "pT_full", "gate_full", "pp_full", "sig_full", "mix", "h_full", "ssq2", "mean2", "root2",
                "inv2", "yo_full"))
        p_in, y_out = ([sem(f"{n}{b}") for b in range(2)] for n in ("p_in", "y_out"))
        y_in = g["pool_dma"][5:7]
        h, wt, dest, ys, ident = (g[n] for n in ("h", "wt", "dest", "ys", "ident"))
        kp = lambda t: g[t].rearrange("a (k p) n -> p (a k) n", p=P)
        block = ctx.enter_context(nc.Block())

        @block.sync
        def _(sp):
            with nc.allow_non_contiguous_dma(reason="1024 gains, once"):
                sp.dma_start(gp[:, :], g["g_ple"].rearrange("a (k p) -> p (a k)", p=P)).then_inc(gp_in, 16)
            sp.dma_start(wpp[:, :, :], kp("w_pp")).then_inc(pp_in, 16)
            for t in range(2):
                sp.dma_start(pt[0:rows(t), t % 2, :], p_of(t)).then_inc(p_in[t % 2], 16)
            sp.dma_start(wpg[:, :, :], kp("w_pg")).then_inc(pg_in, 16)
            sp.dma_start(gf[:, :], g["g_final"].unsqueeze(0).broadcast_to([P, D])).then_inc(gf_in, 16)
            for t in range(2, TT + 2):
                if t < TT:
                    sp.wait_ge(tpp_full, t - 1)
                    sp.dma_start(pt[0:rows(t), t % 2, :], p_of(t)).then_inc(p_in[t % 2], 16)
                v = t - 2
                sp.wait_ge(yo_full, v + 1)
                sp.dma_start(y_of(v), yo[0:rows(v), v % 2, :]).then_inc(y_out[v % 2], 16)
            for b in range(2):
                sp.wait_ge(y_out[b], 16 * len(range(b, TT, 2)))

        @block.gpsimd
        def _(pool):
            for t in range(TT):
                need(pool, mix, 2 * (t - 1))
                for c in range(2):
                    pool.indirect_dma_start(y2[0:rows(t), t % 2, c, :], None, ys[:, :],
                                            bass.IndirectOffsetOnAxis(ap=dest[0:rows(t), c, t:t + 1], axis=0))\
                        .then_inc(y_in[t % 2], 16)

        @block.tensor
        def _(pe):
            for t in range(TT + 1):
                if t < TT:
                    r = rows(t)
                    pe.wait_ge(p_in[t % 2], 16 * (t // 2 + 1))
                    need(pe, pT_full, t)
                    for k in range(KP):
                        last = pe.transpose(tpp[:, k, 0:r], pt[0:r, t % 2, k * P:(k + 1) * P], ident[0:r, 0:r])
                    last.then_inc(tpp_full, 1)
                    pe.wait_ge(un_full, t + 1)
                    need(pe, uT_full, t)
                    for k in range(KD):
                        last = pe.transpose(tp[:, k, 0:r], un[0:r, t % 2, k * P:(k + 1) * P], ident[0:r, 0:r])
                    last.then_inc(tp_full, 1)
                if t >= 1:
                    v, r = t - 1, rows(t - 1)
                    pe.wait_ge(pT_full, v + 1)
                    pe.wait_ge(uT_full, v + 1)
                    if v == 0:
                        pe.wait_ge(pp_in, 16)
                        pe.wait_ge(pg_in, 16)
                    need(pe, sig_full, v)
                    for c in range(2):
                        for k in range(KD):
                            last = pe.matmul(gate[0:r, c * 512:(c + 1) * 512], uT[:, v % 2, k, 0:r],
                                             wpg[:, k, c * 512:(c + 1) * 512], start=(k == 0), stop=(k == KD - 1))
                    last.then_inc(gate_full, 1)
                    need(pe, h_full, 2 * v - 1)
                    for c in range(2):
                        for k in range(KP):
                            last = pe.matmul(pp[0:r, c * 512:(c + 1) * 512], pT[:, v % 2, k, 0:r],
                                             wpp[:, k, c * 512:(c + 1) * 512], start=(k == 0), stop=(k == KP - 1))
                    last.then_inc(pp_full, 1)

        @block.scalar
        def _(act):
            for t in range(TT + 1):
                if t < TT:
                    r = rows(t)
                    act.wait_ge(mix, 2 * t + 2)
                    act.activation(sq[0:r, :], h[0:r, t, :], ACT.Square, accum_out=st[0:r, 0, t:t + 1]).then_inc(ssq, 1)
                    act.wait_ge(mean, t + 1)
                    act.activation(st[0:r, 1, t:t + 1], st[0:r, 1, t:t + 1], ACT.Sqrt).then_inc(root, 1)
                if t >= 1:
                    v, r = t - 1, rows(t - 1)
                    act.wait_ge(gate_full, v + 1)
                    need(act, h_full, 2 * v - 1)
                    act.activation(sig[0:r, :], gate[0:r, :], ACT.Sigmoid).then_inc(sig_full, 1)
                    act.wait_ge(h_full, 2 * v + 2)
                    act.wait_ge(ssq, min(v + 2, TT))
                    act.activation(sq[0:r, :], h[0:r, v, :], ACT.Square, accum_out=st[0:r, 3, v:v + 1])\
                        .then_inc(ssq2, 1)
                    act.wait_ge(ssq2, v + 1)
                    act.wait_ge(mean2, v + 1)
                    act.activation(st[0:r, 4, v:v + 1], st[0:r, 4, v:v + 1], ACT.Sqrt).then_inc(root2, 1)

        @block.vector
        def _(dve):
            dve.wait_ge(gp_in, 16)
            dve.wait_ge(gf_in, 16)

            def head(t):
                r = rows(t)
                dve.wait_ge(y_in[t % 2], 32 * (t // 2 + 1))
                for c in range(2):
                    dve.scalar_tensor_tensor(out=h[0:r, t, :], in0=y2[0:r, t % 2, c, :], scalar=wt[0:r, c, t:t + 1],
                                             in1=h[0:r, t, :], op0=ALU.mult, op1=ALU.add).then_inc(mix, 1)
                    dve.wait_ge(mix, 2 * t + c + 1)
                dve.wait_ge(ssq, t + 1)
                dve.tensor_scalar(st[0:r, 1, t:t + 1], st[0:r, 0, t:t + 1], 1.0 / D, EPS, ALU.mult,
                                  ALU.add).then_inc(mean, 1)
                dve.wait_ge(root, t + 1)
                dve.reciprocal(st[0:r, 2, t:t + 1], st[0:r, 1, t:t + 1]).then_inc(inv, 1)
                dve.wait_ge(inv, t + 1)
                need(dve, tp_full, t - 1)
                dve.tensor_scalar(un[0:r, t % 2, :], h[0:r, t, :], st[0:r, 2, t:t + 1], None, ALU.mult)\
                    .then_inc(un_full, 1)
                need(dve, pp_full, t - 1)
                dve.wait_ge(tpp_full, t + 1)
                dve.tensor_copy(pT[:, t % 2, :, 0:r], tpp[:, :, 0:r]).then_inc(pT_full, 1)
                dve.wait_ge(tp_full, t + 1)
                dve.tensor_tensor(uT[:, t % 2, :, 0:r], tp[:, :, 0:r],
                                  gp[:, :].unsqueeze(2).to_broadcast([P, KD, r]), ALU.mult).then_inc(uT_full, 1)

            def tail(v):
                r = rows(v)
                dve.wait_ge(sig_full, v + 1)
                dve.wait_ge(pp_full, v + 1)
                need(dve, y_out[v % 2], 16 * (v // 2))
                dve.tensor_tensor(yo[0:r, v % 2, :], sig[0:r, :], pp[0:r, :], ALU.mult).then_inc(h_full, 1)
                dve.wait_ge(h_full, 2 * v + 1)
                dve.tensor_tensor(h[0:r, v, :], h[0:r, v, :], yo[0:r, v % 2, :], ALU.add).then_inc(h_full, 1)
                dve.wait_ge(ssq2, v + 1)
                dve.tensor_scalar(st[0:r, 4, v:v + 1], st[0:r, 3, v:v + 1], 1.0 / D, EPS, ALU.mult,
                                  ALU.add).then_inc(mean2, 1)
                dve.wait_ge(root2, v + 1)
                dve.reciprocal(st[0:r, 5, v:v + 1], st[0:r, 4, v:v + 1]).then_inc(inv2, 1)
                dve.wait_ge(inv2, v + 1)
                dve.scalar_tensor_tensor(out=yo[0:r, v % 2, :], in0=h[0:r, v, :], scalar=st[0:r, 5, v:v + 1],
                                         in1=gf[0:r, :], op0=ALU.mult, op1=ALU.mult).then_inc(yo_full, 1)

            for t in range(TT + 1):
                if t < TT:
                    head(t)
                if t >= 1:
                    tail(t - 1)


def window_rows(nc, g):
    ctx = ExitStack()
    with ctx:
        kept = ctx.enter_context(nc.semaphore("kept"))
        ztok = g["ztok"]
        block = ctx.enter_context(nc.Block())

        @block.sync
        def _(sp):
            n = 0
            GW = H_G * HD
            jobs = [(f"win{x + 1}", min(DIL[x][0], SEQ), A_W + x * GW, 2 * A_W + x * GW, GW) for x in range(N_DIL)]
            jobs.append(("sb", SEQ, 3 * A_W + B_W, 3 * A_W + 2 * B_W, B_W))
            for name, m, kc, vc, width in jobs:
                for group, lo, hi in (("prompt", SEQ - m, SEQ), ("sample", SEQ, NT)):
                    dst = g["out_" + name + "_" + group]
                    for x, c in enumerate((kc, vc)):
                        sp.dma_start(dst[:, x, :], ztok[lo:hi, c:c + width]).then_inc(kept, 16)
                        n += 16
            sp.wait_ge(kept, n)


def build(nc, g):
    ctx = ExitStack()
    with ctx:
        def dram(n, s, d=F32):
            return nc.dram_tensor(n, s, d, kind="Internal").ap()

        def sb(n, s, d=F32):
            return ctx.enter_context(nc.sbuf_tensor(n, s, d))

        g = dict(g)
        g["zT"] = dram("zT", (CHUNKS, P, NT))
        g["ztok"] = dram("ztok", (NT, QKV))
        g["xs"] = nc.dram_tensor("xs", (SLOTS, D), F32, kind="Internal").ap()
        g["ys"] = nc.dram_tensor("ys", (SLOTS, D), F32, kind="Internal").ap()
        g["meta"] = nc.dram_tensor("meta", (P, 4), I32, kind="Internal").ap()
        g["ident"] = sb("ident", [P, P])
        g["ident_set"] = ctx.enter_context(nc.semaphore("ident_set"))
        g["pool_dma"] = [ctx.enter_context(nc.semaphore("pool_dma_" + n)) for n in (
            "ztok_out0", "ztok_out1", "rows_moved", "y_out0", "y_out1", "y_in0", "y_in1")]
        g["h"] = sb("h", [P, TT, D])
        g["logit"] = sb("logit", [P, TT, NR])
        g["dest"] = sb("dest", [P, 2, TT], I32)
        g["wt"] = sb("wt", [P, 2, TT])
        g["meta_row"] = sb("meta_row", [1, 4 * P], I32)
        flat = g["h"][:, :, :].rearrange("p t d -> p (t d)")
        g["uT"] = flat[:, 0:KD * NT].rearrange("p (k n) -> p k n", k=KD)
        xp = g["x_prompt"].rearrange("b (t p) d -> (b t) p d", p=P)
        xs = g["x_sample"].rearrange("b s d -> (b s) d")
        x_of = lambda t: xp[t, :, :] if t < QT else xs
        pp = g["p_prompt"].rearrange("a b (t p) d -> (a b t) p d", p=P)
        psm = g["p_sample"].rearrange("a b s d -> (a b s) d")
        yp = g["out_y_prompt"].rearrange("b (t p) d -> (b t) p d", p=P)
        ysm = g["out_y_sample"].rearrange("b s d -> (b s) d")
        with nc.sbuf_tensor("u2", [P, TT, D], F32) as u2:
            g["u2"] = u2
            flat2 = u2[:, :, :].rearrange("p t d -> p (t d)")
            g["obT"] = flat2[:, 0:CB * NT].rearrange("p (k n) -> p k n", k=CB)
            g["oaT"] = flat2[:, CB * NT:(CB + 2) * NT].rearrange("p (k n) -> p k n", k=2)
            first = nc.free_semaphores[0]
            norm_in(nc, g, x_of)
            project(nc, g)
            window_rows(nc, g)
            stick(nc, g)
            clear(nc, range(first, nc.free_semaphores[0]))
            dilated(nc, g)
            decode_dilated(nc, g)
            decode_stick(nc, g)
            with nc.sbuf_tensor("mT", [P, KD, NT], F32) as mT:
                g["mT"] = mT
                merge(nc, g)
                residual(nc, g, x_of)
            route(nc, g)
        experts(nc, g)
        finish(nc, g, lambda t: pp[t, :, :] if t < QT else psm, lambda t: yp[t, :, :] if t < QT else ysm)


_OUT = (("y_prompt", (1, SEQ, D)), ("y_sample", (DEC, 1, D)),
        ("win1_prompt", (1, 1, 128, 2, H_G, HD)), ("win1_sample", (1, DEC, 1, 2, H_G, HD)),
        ("win2_prompt", (1, 1, 512, 2, H_G, HD)), ("win2_sample", (1, DEC, 1, 2, H_G, HD)),
        ("win3_prompt", (1, 1, SEQ, 2, H_G, HD)), ("win3_sample", (1, DEC, 1, 2, H_G, HD)),
        ("sb_prompt", (1, 1, SEQ, 2, H_B, HD)), ("sb_sample", (1, DEC, 1, 2, H_B, HD)))


def kernel(**inputs):
    import numpy as _np
    import concourse.bacc as _bacc
    from concourse.bass_utils import run_bass_kernel_spmd as _run

    nc = _bacc.Bacc("TRN2", target_bir_lowering=False, num_devices=1)
    arrays, g = {}, {}
    for name, a in inputs.items():
        a = _np.ascontiguousarray(a)
        arrays[f"in_{name}"] = a
        g[name] = nc.dram_tensor(f"in_{name}", a.shape, mybir.dt.from_np(a.dtype), kind="ExternalInput").ap()
    outputs(nc, g)
    build(nc, g)
    r = _run(nc, [arrays], core_ids=[0])
    return tuple(r.results[0][f"out_{n}"] for n, _ in _OUT)


def outputs(nc, g):
    for n, shape in _OUT:
        ap = nc.dram_tensor(f"out_{n}", shape, F32, kind="ExternalOutput").ap()
        if n[0] == "y":
            g[f"out_{n}"] = ap
        else:
            g[f"out_{n}"] = ap.rearrange("a b s c h d -> (a b s) c (h d)")
```

```python
from contextlib import ExitStack

import concourse.bass as bass
from concourse import mybir

F32 = mybir.dt.float32
F32R = mybir.dt.float32r
I32 = mybir.dt.int32
ALU = mybir.AluOpType
ACT = mybir.ActivationFunctionType
AX = mybir.AxisListType.X

P = 128
D = 1024
KD = D // P
SEQ = 1024
DEC = 8
NT = SEQ + DEC
QT = SEQ // P
TT = QT + 1
HD = 64
N_DIL, H_G, H_B = 3, 4, 8
DIL = ((128, 1), (512, 4), (2048, 16))
A_W = N_DIL * H_G * HD
B_W = H_B * HD
QKV = 3 * A_W + 3 * B_W
N_IN = QKV + 2 * D
CHUNKS = QKV // P
CA, CB = A_W // P, B_W // P
NSPLIT = 3
NS = NT // NSPLIT
PAST = 256
PAGE = 128
NG, EPG = 4, 8
NE = NG * EPG
NR = NG + NE
FE = D // 2
KF = FE // P
PLE = 256
EPS = 1e-6
ASG = 2 * NT
SLOTS = ASG + P
MAXBLK = (ASG + NE * (P - 1)) // P
NEG = -1.0e30
SCALE = HD ** -0.5
SLOPES = [2.0 ** (-8.0 * (h + 1) / (N_DIL * H_G)) for h in range(N_DIL * H_G)]


def need(eng, sem, value):
    if not isinstance(value, int) or value > 0:
        eng.wait_ge(sem, value)


def looped(eng, n, step):
    step(0)
    with eng.Fori(1, n) as it:
        step(it)


def clear(nc, low):
    with nc.Block() as block:
        @block.gpsimd
        def _(pool):
            pool.sem_clear(low)


def rows(t):
    return P if t < QT else DEC


def products(pe, out, w_high, w_low, m_high, m_low, first, last):
    pe.matmul(out, w_low, m_high, start=first, stop=False)
    pe.matmul(out, w_high, m_low, start=False, stop=False)
    return pe.matmul(out, w_high, m_high, start=False, stop=last)


def norm_in(nc, g, x_of):
    ctx = ExitStack()
    with ctx:
        sb = lambda n, s, d=F32: ctx.enter_context(nc.sbuf_tensor(n, s, d))
        sem = lambda n: ctx.enter_context(nc.semaphore(n))
        R = 3
        xt = sb("n_xt", [P, R, D])
        xn = sb("n_xn", [P, 2, D])
        sq = sb("n_sq", [P, D])
        ss = sb("n_ss", [P, TT])
        rt = sb("n_rt", [P, TT])
        rstd = sb("n_rstd", [P, TT])
        gm = sb("n_gm", [P, KD])
        tp = [ctx.enter_context(nc.psum_tensor(f"n_tp{j}", [P, KD, P], F32)) for j in range(2)]
        x_in = [sem(f"n_x_in{j}") for j in range(R)]
        gm_in, ssq, mean, root, inv, scaled, turned, stored = map(sem, (
            "n_gm_in", "n_ssq", "n_mean", "n_root", "n_inv", "n_scaled", "n_turned", "n_stored"))
        block = ctx.enter_context(nc.Block())

        @block.sync
        def _(sp):
            with nc.allow_non_contiguous_dma(reason="1024 gains, once"):
                sp.dma_start(gm[:, :], g["g_mix"].rearrange("a (k p) -> p (a k)", p=P)).then_inc(gm_in, 16)
            for t in range(TT):
                if t >= R:
                    sp.wait_ge(scaled, t - R + 1)
                sp.dma_start(xt[0:rows(t), t % R, :], x_of(t)).then_inc(x_in[t % R], 16)

        @block.scalar
        def _(act):
            for t in range(TT):
                r = rows(t)
                act.wait_ge(x_in[t % R], 16 * (t // R + 1))
                if t:
                    act.wait_ge(ssq, t)
                act.activation(sq[0:r, :], xt[0:r, t % R, :], ACT.Square,
                               accum_out=ss[0:r, t:t + 1]).then_inc(ssq, 1)
                act.wait_ge(mean, t + 1)
                act.activation(rt[0:r, t:t + 1], rt[0:r, t:t + 1], ACT.Sqrt).then_inc(root, 1)

        @block.vector
        def _(dve):
            dve.wait_ge(gm_in, 16)
            for t in range(TT + 1):
                if t < TT:
                    r = rows(t)
                    dve.wait_ge(ssq, t + 1)
                    dve.tensor_scalar(rt[0:r, t:t + 1], ss[0:r, t:t + 1], 1.0 / D, EPS, ALU.mult,
                                      ALU.add).then_inc(mean, 1)
                    dve.wait_ge(root, t + 1)
                    dve.reciprocal(rstd[0:r, t:t + 1], rt[0:r, t:t + 1]).then_inc(inv, 1)
                    dve.wait_ge(inv, t + 1)
                    if t >= 2:
                        dve.wait_ge(turned, t - 1)
                    dve.tensor_scalar(xn[0:r, t % 2, :], xt[0:r, t % R, :], rstd[0:r, t:t + 1], None,
                                      ALU.mult).then_inc(scaled, 1)
                if t >= 1:
                    u = t - 1
                    r = rows(u)
                    dve.wait_ge(turned, u + 1)
                    dve.tensor_tensor(g["u"][:, :, u * P:u * P + r], tp[u % 2][:, :, 0:r],
                                      gm[:, :].unsqueeze(2).to_broadcast([P, KD, r]),
                                      ALU.mult).then_inc(stored, 1)

        @block.tensor
        def _(pe):
            pe.wait_ge(g["ident_set"], 2)
            for t in range(TT):
                r = rows(t)
                pe.wait_ge(scaled, t + 1)
                if t >= 2:
                    pe.wait_ge(stored, t - 1)
                for k in range(KD):
                    last = pe.transpose(tp[t % 2][:, k, 0:r], xn[0:r, t % 2, k * P:(k + 1) * P],
                                        g["ident"][0:r, 0:r])
                last.then_inc(turned, 1)

        @block.gpsimd
        def _(pool):
            pool.memset(g["ident"][:, :], 0.0).then_inc(g["ident_set"], 1)
            pool.wait_ge(g["ident_set"], 1)
            pool.affine_select(out=g["ident"][:, :], in_=g["ident"][:, :], compare_op=ALU.not_equal, fill=1.0,
                               base=0, pattern=[[-1, P]], channel_multiplier=1).then_inc(g["ident_set"], 1)


def project(nc, g):
    ctx = ExitStack()
    with ctx:
        sb = lambda n, s, d=F32: ctx.enter_context(nc.sbuf_tensor(n, s, d))
        sem = lambda n: ctx.enter_context(nc.semaphore(n))
        w = sb("p_w", [P, 2, KD, P])
        wh = sb("p_wh", [P, 2, KD, P], F32R)
        wl = sb("p_wl", [P, 2, KD, P], F32R)
        ul = sb("p_ul", [P, KD, NT], F32R)
        zc = sb("p_zc", [P, 2, NT])
        zk = sb("p_zk", [P, 2, TT, P])
        acc = [ctx.enter_context(nc.psum_tensor(f"p_acc{j}", [P, 512], F32)) for j in range(6)]
        tp = [ctx.enter_context(nc.psum_tensor(f"p_tp{j}", [P, 4, P], F32)) for j in range(2)]
        w_in = [sem(f"p_w_in{j}") for j in range(2)]
        z_out = [sem(f"p_z_out{j}") for j in range(2)]
        k_out = g["pool_dma"][0:2]
        u_out = sem("p_u_out")
        acc_full, zc_full, tp_full, zk_full, wh_full, wl_full, uh_full, ul_full = map(sem, (
            "p_acc_full", "p_zc_full", "p_tp_full", "p_zk_full", "p_wh_full", "p_wl_full", "p_uh_full", "p_ul_full"))
        u, uh, ident, zT, ztok = g["u"], g["uh"], g["ident"], g["zT"], g["ztok"]
        win_v = g["w_in"].rearrange("a (k p) n -> p (a k) n", p=P)
        zt_v = ztok[0:SEQ, :].rearrange("(t p) n -> p t n", p=P)
        block = ctx.enter_context(nc.Block())
        PASSES = CHUNKS // 2
        GROUPS = [(0, 4), (4, 4), (8, 1)]
        NG_ = len(GROUPS)

        @block.sync
        def _(sp):
            def load(it, b):
                sp.dma_start(w[:, b, :, :], win_v[:, :, bass.ds((it * 2 + b) * P, P)]).then_inc(w_in[b], 16)

            load(0, 0)
            load(0, 1)
            sp.dma_start(g["u_kept"][:, :], u[:, :, :].rearrange("p k n -> p (k n)")).then_inc(u_out, 16)
            with sp.Fori(0, PASSES - 1) as it:
                for b in range(2):
                    sp.wait_ge(wl_full, it * 2 + b + 1)
                    load(it + 1, b)
            sp.wait_ge(u_out, 16)

        @block.tensor
        def _(pe):
            def turn(it, b):
                pe.wait_ge(zc_full, it * 2 * NSPLIT + (b + 1) * NSPLIT)
                for n, (t0, m) in enumerate(GROUPS):
                    j = b * NG_ + n
                    need(pe, zk_full, it * 2 * NG_ + (j - 1))
                    for t in range(t0, t0 + m):
                        last = pe.transpose(tp[j % 2][0:rows(t), t - t0, :],
                                            zc[:, b, t * P:t * P + rows(t)], ident[:, :])
                    last.then_inc(tp_full, 1)

            def step(it):
                for b in range(2):
                    need(pe, zc_full, (it - 1) * 2 * NSPLIT + (b + 1) * NSPLIT)
                    pe.wait_ge(wl_full, it * 2 + b + 1)
                    for s in range(NSPLIT):
                        t = slice(s * NS, (s + 1) * NS)
                        for k in range(KD):
                            if isinstance(it, int) and b == 0 and s == 0:
                                pe.wait_ge(ul_full, k + 1)
                            last = products(pe, acc[b * NSPLIT + s][:, 0:NS], wh[:, b, k, :], wl[:, b, k, :],
                                            uh[:, k, t], ul[:, k, t], k == 0, k == KD - 1)
                        last.then_inc(acc_full, 1)
                    if b == 1:
                        turn(it, 0)
                    elif not isinstance(it, int):
                        turn(it - 1, 1)

            looped(pe, PASSES, step)
            turn(PASSES - 1, 1)

        @block.scalar
        def _(act):
            def cut(it, b):
                act.wait_ge(w_in[b], it * 16 + 16)
                need(act, acc_full, (it - 1) * 2 * NSPLIT + (b + 1) * NSPLIT)
                act.activation(wh[:, b, :, :], w[:, b, :, :], ACT.Copy).then_inc(wh_full, 1)

            cut(0, 0)
            for k in range(KD):
                act.activation(uh[:, k, :], u[:, k, :], ACT.Copy).then_inc(uh_full, 1)
            cut(0, 1)

            def step(it, more=True):
                for b in range(2):
                    need(act, tp_full, it * 2 * NG_ + (b - 1) * NG_)
                    need(act, z_out[b], it * 16)
                    for s in range(NSPLIT):
                        act.wait_ge(acc_full, it * 2 * NSPLIT + b * NSPLIT + s + 1)
                        act.activation(zc[:, b, s * NS:(s + 1) * NS], acc[b * NSPLIT + s][:, 0:NS],
                                       ACT.Copy).then_inc(zc_full, 1)
                    if more:
                        cut(it + 1, b)
                for b in range(2):
                    act.wait_ge(zc_full, it * 2 * NSPLIT + (b + 1) * NSPLIT)
                    act.dma_start(zT[bass.ds(it * 2 + b, 1), :, :].rearrange("a p n -> (a p) n"),
                                  zc[:, b, :]).then_inc(z_out[b], 16)

            looped(act, PASSES - 1, step)
            step(PASSES - 1, more=False)
            for b in range(2):
                act.wait_ge(z_out[b], PASSES * 16)

        @block.vector
        def _(dve):
            def cut(it, b):
                dve.wait_ge(wh_full, it * 2 + b + 1)
                dve.tensor_tensor(wl[:, b, :, :], w[:, b, :, :], wh[:, b, :, :], ALU.subtract).then_inc(wl_full, 1)

            cut(0, 0)
            for k in range(KD):
                dve.wait_ge(uh_full, k + 1)
                dve.tensor_tensor(ul[:, k, :], u[:, k, :], uh[:, k, :], ALU.subtract).then_inc(ul_full, 1)
            cut(0, 1)

            def step(it, more=True):
                for b in range(2):
                    if more:
                        cut(it + 1, b)
                    need(dve, k_out[b], it * 32)
                    for n, (t0, m) in enumerate(GROUPS):
                        j = b * NG_ + n
                        dve.wait_ge(tp_full, it * 2 * NG_ + j + 1)
                        r = rows(t0)
                        dve.tensor_copy(zk[0:r, b, t0:t0 + m, :], tp[j % 2][0:r, 0:m, :]).then_inc(zk_full, 1)

            looped(dve, PASSES - 1, step)
            step(PASSES - 1, more=False)

        @block.gpsimd
        def _(pool):
            def step(it):
                for b in range(2):
                    c = it * 2 + b
                    pool.wait_ge(zk_full, it * 2 * NG_ + (b + 1) * NG_)
                    pool.dma_start(zt_v[:, :, bass.ds(c * P, P)], zk[:, b, 0:QT, :]).then_inc(k_out[b], 16)
                    pool.dma_start(ztok[SEQ:NT, bass.ds(c * P, P)], zk[0:DEC, b, QT, :]).then_inc(k_out[b], 16)

            looped(pool, PASSES, step)
            for b in range(2):
                pool.wait_ge(k_out[b], PASSES * 32)


def turn_groups(n):
    return [(a, min(4, n - a)) for a in range(0, n, 4)]


def pipeline(n, size):
    def unit(it, j, lag):
        p_, x = (it, j - lag) if j >= lag else (it - 1, j - lag + size)
        return p_, x // QT, x % QT, it * size + (j - lag)

    def there(it, j, lag):
        return not isinstance(it, int) or 0 <= it * size + j - lag < n * size

    def passes(eng, step, lag):
        for j in range(size):
            step(0, j)
        with eng.Fori(1, n) as it:
            for j in range(size):
                step(it, j)
        for j in range(lag):
            step(n, j)

    return unit, passes, there


def window_rows(eng, g, kept):
    n = 0
    ztok = g["ztok"]
    GW = H_G * HD
    jobs = [(f"win{x + 1}", min(DIL[x][0], SEQ), A_W + x * GW, 2 * A_W + x * GW, GW) for x in range(N_DIL)]
    jobs.append(("sb", SEQ, 3 * A_W + B_W, 3 * A_W + 2 * B_W, B_W))
    for name, m, kc, vc, width in jobs:
        for group, lo, hi in (("prompt", SEQ - m, SEQ), ("sample", SEQ, NT)):
            dst = g["out_" + name + "_" + group]
            for x, c in enumerate((kc, vc)):
                eng.dma_start(dst[:, x, :], ztok[lo:hi, c:c + width]).then_inc(kept, 16)
                n += 16
    return n


def stick(nc, g):
    ctx = ExitStack()
    with ctx:
        sb = lambda n, s, d=F32: ctx.enter_context(nc.sbuf_tensor(n, s, d))
        sem = lambda n: ctx.enter_context(nc.semaphore(n))
        ps = lambda n, s: ctx.enter_context(nc.psum_tensor(n, s, F32))
        PAIRS = H_B // 2
        U = 2 * QT
        BUF = 4
        q = sb("s_q", [HD, 2, SEQ])
        k = sb("s_k", [HD, 2, SEQ])
        v = sb("s_v", [P, 2, QT, HD])
        bias = sb("s_bias", [P, 2])
        causal = sb("s_causal", [P, P])
        const, kept = sem("s_const"), sem("s_kept")
        z = sb("s_z", [P, BUF, SEQ])
        w = sb("s_w", [P, 2, SEQ])
        r = sb("s_r", [P, 2, SEQ])
        cum = sb("s_cum", [P, 2, SEQ])
        a = sb("s_a", [P, BUF, SEQ])
        aT = sb("s_aT", [P, 2, SEQ])
        o = sb("s_o", [P, QT, P])
        S = [ps(f"s_S{j}", [P, SEQ]) for j in range(2)]
        tp = [ps(f"s_tp{j}", [P, 512]) for j in range(2)]
        oT = ps("s_oT", [P, 512])
        O = [ps("s_O", [P, HD]), oT[:, 0:HD]]
        s_full, z_full, masked, r_full, w_full, e_full, t_full, cum_full, al_full, a_full = map(sem, (
            "s_s_full", "s_z_full", "s_masked", "s_r_full", "s_w_full", "s_e_full", "s_t_full",
            "s_cum_full", "s_al_full", "s_a_full"))
        tp_full, aT_full, o_full, o_read, oT_full, oT_read = map(sem, (
            "s_tp_full", "s_aT_full", "s_o_full", "s_o_read", "s_oT_full", "s_oT_read"))
        qkv_in = [sem(f"s_qkv_in{b}") for b in range(2)]
        ident, zT, ztok, obT = g["ident"], g["zT"], g["ztok"], g["obT"]
        CQ, CK, COLV = 3 * CA, 3 * CA + CB, 3 * A_W + 2 * B_W
        BASE = [0]
        for i in range(QT):
            BASE.append(BASE[-1] + len(turn_groups(i + 1)))
        GH = BASE[QT]
        ztv = ztok[0:SEQ, :].rearrange("(t p) n -> p t n", p=P)
        block = ctx.enter_context(nc.Block())

        def group(it, b, i, n):
            return it * (2 * GH) + (b * GH + BASE[i] + n)

        unit, passes, there = pipeline(PAIRS, U)

        def late(x):
            p_, y = divmod(x, U)
            return p_ * 2 * GH + (y // QT) * GH + BASE[y % QT + 1]
        LATE = [late(j - 1 - BUF) for j in range(U)]

        @block.sync
        def _(sp):
            def load(it, b):
                half = b * HD
                need(sp, o_full, (it - 1) * U + (b + 1) * QT)
                sp.dma_start(q[:, b, :], zT[bass.ds(it + CQ, 1), half:half + HD, 0:SEQ]
                             .rearrange("a p n -> (a p) n")).then_inc(qkv_in[b], 16)
                sp.dma_start(k[:, b, :], zT[bass.ds(it + CK, 1), half:half + HD, 0:SEQ]
                             .rearrange("a p n -> (a p) n")).then_inc(qkv_in[b], 16)
                sp.dma_start(v[:, b, :, :], ztv[:, :, bass.ds(it * P + (COLV + half), HD)]).then_inc(qkv_in[b], 16)
                sp.dma_start(bias[:, b:b + 1], g["b_sb"][:, bass.ds(it * 2 + b, 1)].broadcast_to([P, 1]))\
                    .then_inc(qkv_in[b], 16)

            for b in range(2):
                load(0, b)
            n_kept = window_rows(sp, g, kept)
            with sp.Fori(1, PAIRS) as it:
                for b in range(2):
                    load(it, b)
            sp.wait_ge(kept, n_kept)

        @block.tensor
        def _(pe):
            def scores(it, j):
                _, b, i, u = unit(it, j, 0)
                if i == 0:
                    pe.wait_ge(qkv_in[b], it * 64 + 64)
                need(pe, z_full, u - 1)
                for c in range(0, (i + 1) * P, 512):
                    n = min(512, (i + 1) * P - c)
                    last = pe.matmul(S[j % 2][:, c:c + n], q[:, b, i * P:(i + 1) * P], k[:, b, c:c + n],
                                     start=True, stop=True)
                last.then_inc(s_full, 1)

            def turn(it, j):
                p_, b, i, u = unit(it, j, 3)
                pe.wait_ge(a_full, u + 1)
                for n, (t0, m) in enumerate(turn_groups(i + 1)):
                    x = b * GH + BASE[i] + n
                    need(pe, aT_full, group(p_, b, i, n) - 1)
                    for t in range(m):
                        last = pe.transpose(tp[x % 2][:, t * P:(t + 1) * P],
                                            a[:, (j - 3) % BUF, (t0 + t) * P:(t0 + t + 1) * P], ident[:, :])
                    last.then_inc(tp_full, 1)

            def values(it, j):
                p_, b, i, u = unit(it, j, 4)
                pe.wait_ge(aT_full, group(p_, b, i, len(turn_groups(i + 1)) - 1) + 1)
                need(pe, o_read, u - 1)
                if j == 5:
                    need(pe, oT_read, it * 2)
                for t in range(i + 1):
                    last = pe.matmul(O[j % 2][:, :], aT[:, j % 2, t * P:(t + 1) * P], v[:, b, t, :],
                                     start=(t == 0), stop=(t == i))
                last.then_inc(o_full, 1)

            def out(it, j):
                pe.wait_ge(o_read, it * U)
                for h in range(2):
                    if h:
                        pe.wait_ge(oT_read, (it - 1) * 2 + h)
                    for t in range(4):
                        last = pe.transpose(oT[:, t * P:(t + 1) * P], o[:, h * 4 + t, :], ident[:, :])
                    last.then_inc(oT_full, 1)

            def step(it, j):
                if there(it, j, 0):
                    scores(it, j)
                if there(it, j, 3):
                    turn(it, j)
                if there(it, j, 4):
                    values(it, j)
                if j == 4 and (not isinstance(it, int) or it):
                    out(it, j)

            passes(pe, step, 6)

        @block.scalar
        def _(act):
            act.preload_act_table_set("natural_log_exp_and_others")

            def step(it, j):
                if there(it, j, 0):
                    _, b, i, u = unit(it, j, 0)
                    n = (i + 1) * P
                    act.wait_ge(s_full, u + 1)
                    need(act, al_full, u - BUF + 1)
                    act.activation(z[:, j % BUF, 0:n], S[j % 2][:, 0:n], ACT.Identity, scale=SCALE,
                                   bias=bias[:, b:b + 1]).then_inc(z_full, 1)
                if there(it, j, 1):
                    p_, b, i, u = unit(it, j, 1)
                    n = (i + 1) * P
                    x = (j - 1) % 2
                    act.wait_ge(w_full, u + 1)
                    act.activation(w[:, x, 0:n], w[:, x, 0:n], ACT.Exp, scale=-1.0).then_inc(e_full, 1)
                    act.wait_ge(e_full, u + 1)
                    act.activation(w[:, x, 0:n], w[:, x, 0:n], ACT.Ln, bias=1.0).then_inc(t_full, 1)
                if there(it, j, 2):
                    p_, b, i, u = unit(it, j, 2)
                    n = (i + 1) * P
                    act.wait_ge(al_full, u + 1)
                    act.activation(a[:, (j - 2) % BUF, 0:n], a[:, (j - 2) % BUF, 0:n], ACT.Exp).then_inc(a_full, 1)
                if there(it, j, 5):
                    p_, b, i, u = unit(it, j, 5)
                    act.wait_ge(o_full, u + 1)
                    if b == i == 0:
                        need(act, oT_full, p_ * 2)
                    act.activation(o[:, i, b * HD:(b + 1) * HD], O[(j - 1) % 2][:, :], ACT.Copy).then_inc(o_read, 1)

            passes(act, step, 5)

        @block.gpsimd
        def _(pool):
            pool.memset(causal[:, :], 0.0).then_inc(const, 1)
            pool.wait_ge(const, 1)
            pool.affine_select(out=causal[:, :], in_=causal[:, :], compare_op=ALU.is_gt, fill=NEG, base=0,
                               pattern=[[-1, P]], channel_multiplier=1).then_inc(const, 1)
            pool.wait_ge(const, 2)

            def step(it, j):
                if there(it, j, 0):
                    _, b, i, u = unit(it, j, 0)
                    pool.wait_ge(z_full, u + 1)
                    diag = z[:, j % BUF, i * P:(i + 1) * P]
                    pool.tensor_tensor(diag, diag, causal[:, :], ALU.add).then_inc(masked, 1)
                if there(it, j, 1):
                    p_, b, i, u = unit(it, j, 1)
                    n = (i + 1) * P
                    pool.wait_ge(cum_full, u + 1)
                    need(pool, tp_full, it * (2 * GH) + LATE[j])
                    pool.tensor_tensor(a[:, (j - 1) % BUF, 0:n], z[:, (j - 1) % BUF, 0:n], cum[:, j % 2, 0:n],
                                       ALU.subtract).then_inc(al_full, 1)

            passes(pool, step, 1)

        @block.vector
        def _(dve):
            def step(it, j):
                if there(it, j, 0):
                    _, b, i, u = unit(it, j, 0)
                    n = (i + 1) * P
                    dve.wait_ge(masked, u + 1)
                    dve.tensor_scalar(w[:, j % 2, 0:n].bitcast(I32), z[:, j % BUF, 0:n].bitcast(I32),
                                      0x7FFFFFFF, None, ALU.bitwise_and).then_inc(w_full, 1)
                    dve.tensor_scalar(r[:, j % 2, 0:n], z[:, j % BUF, 0:n], 0.0, None, ALU.max).then_inc(r_full, 1)
                if there(it, j, 1):
                    p_, b, i, u = unit(it, j, 1)
                    n = (i + 1) * P
                    x = (j - 1) % 2
                    dve.wait_ge(t_full, u + 1)
                    dve.wait_ge(r_full, u + 1)
                    need(dve, al_full, u - 1)
                    dve.tensor_tensor_scan(cum[:, j % 2, 0:n][:, ::-1], w[:, x, 0:n][:, ::-1],
                                           r[:, x, 0:n][:, ::-1], 0.0, ALU.add, ALU.add).then_inc(cum_full, 1)
                if there(it, j, 3):
                    p_, b, i, u = unit(it, j, 3)
                    need(dve, o_full, u - 1)
                    for n, (t0, m) in enumerate(turn_groups(i + 1)):
                        x = b * GH + BASE[i] + n
                        dve.wait_ge(tp_full, group(p_, b, i, n) + 1)
                        dve.tensor_copy(aT[:, (j - 3) % 2, t0 * P:(t0 + m) * P],
                                        tp[x % 2][:, 0:m * P]).then_inc(aT_full, 1)
                if j == 4 and (not isinstance(it, int) or it):
                    for h in range(2):
                        dve.wait_ge(oT_full, (it - 1) * 2 + h + 1)
                        dve.tensor_copy(obT[:, bass.ds(it - 1, 1), h * 512:(h + 1) * 512]
                                        .rearrange("p a n -> p (a n)"), oT[:, :]).then_inc(oT_read, 1)

            passes(dve, step, 6)


def dilated(nc, g):
    ctx = ExitStack()
    with ctx:
        sb = lambda n, s, d=F32: ctx.enter_context(nc.sbuf_tensor(n, s, d))
        sem = lambda n: ctx.enter_context(nc.semaphore(n))
        ps = lambda n, s: ctx.enter_context(nc.psum_tensor(n, s, F32))
        PAIRS = H_G // 2
        U = 2 * QT
        BUF = 4
        BACK = [min(QT - 1, win // P) for win, _ in DIL]
        W = [(n + 1) * P for n in BACK]
        SEGB = [0, 2 * P, 0]
        q = sb("d_q", [HD, 2, N_DIL, SEQ])
        k = sb("d_k", [HD, 2, N_DIL, SEQ])
        v = sb("d_v", [P, 2, N_DIL, QT, HD])
        md = [sb(f"d_md{x}", [P, W[x]]) for x in range(N_DIL)]
        slope = sb("d_slope", [P, N_DIL * H_G])
        row = sb("d_row", [P, BUF, sum(W)])
        pT = sb("d_pT", [P, 2, sum(W)])
        mx = sb("d_mx", [P, BUF])
        nmx = sb("d_nmx", [P, BUF])
        den = sb("d_den", [P, BUF])
        rden = sb("d_rden", [P, BUF])
        o = sb("d_o", [P, QT, P])
        S = [ps(f"d_S{j}", [P, SEQ]) for j in range(2)]
        tp = [ps(f"d_tp{j}", [P, 512]) for j in range(2)]
        oT = ps("d_oT", [P, 512])
        O = [ps("d_O", [P, HD]), oT[:, 0:HD]]
        const, dist_set, md_set, s01_full, s2_full, biased, mx_full, nmx_full, p_full, rden_full = map(sem, (
            "d_const", "d_dist_set", "d_md_set", "d_s01_full", "d_s2_full", "d_biased", "d_mx_full",
            "d_nmx_full", "d_p_full", "d_rden_full"))
        masked = sem("d_masked")
        tp_full, pT_full, o_full, o_read, oT_full, oT_read = map(sem, (
            "d_tp_full", "d_pT_full", "d_o_full", "d_o_read", "d_oT_full", "d_oT_read"))
        qkv_in = [sem(f"d_qkv_in{b}") for b in range(2)]
        ident, zT, ztok, oaT = g["ident"], g["zT"], g["ztok"], g["oaT"]
        unit, passes, there = pipeline(PAIRS, U)

        def keys(i):
            return [(x, t) for x in range(N_DIL) for t in range(max(0, i - BACK[x]), i + 1)]

        def span(i, x):
            m = [n for n, (y, _) in enumerate(keys(i)) if y == x]
            return m[0] * P, max(0, i - BACK[x]), len(m)

        BASE = [0]
        for i in range(QT):
            BASE.append(BASE[-1] + len(turn_groups(len(keys(i)))))
        GH = BASE[QT]

        def group(it, b, i, n):
            return it * (2 * GH) + (b * GH + BASE[i] + n)

        def late(x):
            p_, y = divmod(x, U)
            return p_ * 2 * GH + (y // QT) * GH + BASE[y % QT + 1]

        ztv = ztok[0:SEQ, :].rearrange("(t p) n -> p t n", p=P)
        block = ctx.enter_context(nc.Block())

        @block.sync
        def _(sp):
            def load(it, b):
                half = b * HD
                need(sp, o_full, (it - 1) * U + (b + 1) * QT)
                for x in range(N_DIL):
                    c = x * (H_G // 2) + it
                    sp.dma_start(q[:, b, x, :], zT[bass.ds(c, 1), half:half + HD, 0:SEQ]
                                 .rearrange("a p n -> (a p) n")).then_inc(qkv_in[b], 16)
                    sp.dma_start(k[:, b, x, :], zT[bass.ds(c + CA, 1), half:half + HD, 0:SEQ]
                                 .rearrange("a p n -> (a p) n")).then_inc(qkv_in[b], 16)
                    sp.dma_start(v[:, b, x, :, :], ztv[:, :, bass.ds(c * P + (2 * A_W + half), HD)])\
                        .then_inc(qkv_in[b], 16)

            for b in range(2):
                load(0, b)
            with sp.Fori(1, PAIRS) as it:
                for b in range(2):
                    load(it, b)

        @block.gpsimd
        def _(pool):
            for h in range(N_DIL * H_G):
                pool.memset(slope[:, h:h + 1], SLOPES[h]).then_inc(const, 1)
            for x in range(N_DIL):
                pool.iota(pT[:, 0, sum(W[:x]):sum(W[:x + 1])].bitcast(I32), pattern=[[-1, W[x]]],
                          base=BACK[x] * P, channel_multiplier=1).then_inc(dist_set, 1)
            for x, (win, _) in enumerate(DIL):
                pool.wait_ge(md_set, 2 * N_DIL)
                pool.affine_select(out=md[x][:, :], in_=md[x][:, :], compare_op=ALU.is_ge, fill=NEG,
                                   base=BACK[x] * P, pattern=[[-1, W[x]]], channel_multiplier=1).then_inc(const, 1)
                pool.wait_ge(const, N_DIL * H_G + 2 * x + 1)
                pool.affine_select(out=md[x][:, :], in_=md[x][:, :], compare_op=ALU.is_ge, fill=NEG,
                                   base=win - BACK[x] * P, pattern=[[1, W[x]]], channel_multiplier=-1)\
                    .then_inc(const, 1)

        @block.tensor
        def _(pe):
            def scores(it, j):
                _, b, i, u = unit(it, j, 0)
                if i == 0:
                    pe.wait_ge(qkv_in[b], it * (9 * 16) + 9 * 16)
                for x in range(N_DIL):
                    _, t0, m = span(i, x)
                    if x == 0:
                        need(pe, biased, u * 3 - 1)
                    if x == 2:
                        need(pe, biased, u * 3)
                    c = SEGB[x]
                    key, end = t0 * P, (t0 + m) * P
                    while key < end:
                        n = min(512 - c % 512, end - key)
                        last = pe.matmul(S[x // 2][:, c:c + n], q[:, b, x, i * P:(i + 1) * P],
                                         k[:, b, x, key:key + n], start=True, stop=True,
                                         skip_group_check=True)
                        key, c = key + n, c + n
                    if x:
                        last.then_inc(s01_full if x == 1 else s2_full, 1)

            def turn(it, j):
                p_, b, i, u = unit(it, j, 2)
                pe.wait_ge(p_full, u + 1)
                for n, (t0, m) in enumerate(turn_groups(len(keys(i)))):
                    x = b * GH + BASE[i] + n
                    need(pe, pT_full, group(p_, b, i, n) - 1)
                    for t in range(m):
                        last = pe.transpose(tp[x % 2][:, t * P:(t + 1) * P],
                                            row[:, (j - 2) % BUF, (t0 + t) * P:(t0 + t + 1) * P], ident[:, :])
                    last.then_inc(tp_full, 1)

            def values(it, j):
                p_, b, i, u = unit(it, j, 3)
                ks = keys(i)
                pe.wait_ge(pT_full, group(p_, b, i, len(turn_groups(len(ks))) - 1) + 1)
                need(pe, o_read, u - 1)
                if j == 4:
                    need(pe, oT_read, it * 2)
                for n, (x, t) in enumerate(ks):
                    last = pe.matmul(O[(j - 3) % 2][:, :], pT[:, (j - 3) % 2, n * P:(n + 1) * P], v[:, b, x, t, :],
                                     start=(n == 0), stop=(n == len(ks) - 1))
                last.then_inc(o_full, 1)

            def out(it, j):
                pe.wait_ge(o_read, it * U)
                for h in range(2):
                    if h:
                        pe.wait_ge(oT_read, (it - 1) * 2 + h)
                    for t in range(4):
                        last = pe.transpose(oT[:, t * P:(t + 1) * P], o[:, h * 4 + t, :], ident[:, :])
                    last.then_inc(oT_full, 1)

            def step(it, j):
                if there(it, j, 0):
                    scores(it, j)
                if there(it, j, 2):
                    turn(it, j)
                if there(it, j, 3):
                    values(it, j)
                if j == 3 and (not isinstance(it, int) or it):
                    out(it, j)

            passes(pe, step, 5)

        @block.scalar
        def _(act):
            def step(it, j):
                if there(it, j, 1):
                    p_, b, i, u = unit(it, j, 1)
                    n = len(keys(i)) * P
                    x = (j - 1) % BUF
                    act.wait_ge(nmx_full, u + 1)
                    need(act, rden_full, u - BUF + 1)
                    act.activation(row[:, x, 0:n], row[:, x, 0:n], ACT.Exp, scale=SCALE, bias=nmx[:, x:x + 1],
                                   accum_out=den[:, x:x + 1]).then_inc(p_full, 1)
                if there(it, j, 2):
                    p_, b, i, u = unit(it, j, 2)
                    need(act, o_full, u - 1)
                    for n, (t0, m) in enumerate(turn_groups(len(keys(i)))):
                        x = b * GH + BASE[i] + n
                        act.wait_ge(tp_full, group(p_, b, i, n) + 1)
                        act.activation(pT[:, (j - 2) % 2, t0 * P:(t0 + m) * P], tp[x % 2][:, 0:m * P],
                                       ACT.Copy).then_inc(pT_full, 1)
                if there(it, j, 4):
                    p_, b, i, u = unit(it, j, 4)
                    act.wait_ge(o_full, u + 1)
                    act.wait_ge(rden_full, u + 1)
                    if b == i == 0:
                        need(act, oT_full, p_ * 2)
                    act.activation(o[:, i, b * HD:(b + 1) * HD], O[(j - 4) % 2][:, :], ACT.Copy,
                                   scale=rden[:, (j - 4) % BUF:(j - 4) % BUF + 1]).then_inc(o_read, 1)

            passes(act, step, 4)

        @block.vector
        def _(dve):
            for x in range(N_DIL):
                dve.wait_ge(dist_set, N_DIL)
                d = pT[:, 0, sum(W[:x]):sum(W[:x + 1])].bitcast(I32)
                f = row[:, 0, sum(W[:x]):sum(W[:x + 1])]
                m = row[:, 1, sum(W[:x]):sum(W[:x + 1])].bitcast(I32)
                dve.tensor_scalar(m, d, DIL[x][1] - 1, None, ALU.bitwise_and).then_inc(md_set, 1)
                dve.wait_ge(md_set, 2 * x + 1)
                dve.tensor_scalar(f, m, 0.0, NEG, ALU.is_gt, ALU.mult).then_inc(masked, 1)
                dve.wait_ge(masked, x + 1)
                dve.scalar_tensor_tensor(out=md[x][:, :], in0=d, scalar=-8.0, in1=f, op0=ALU.mult,
                                         op1=ALU.add).then_inc(md_set, 1)
                dve.wait_ge(md_set, 2 * x + 2)
            dve.wait_ge(const, N_DIL * H_G + 2 * N_DIL)

            def step(it, j):
                if there(it, j, 0):
                    _, b, i, u = unit(it, j, 0)
                    r = row[:, j % BUF, :]
                    need(dve, tp_full, it * (2 * GH) + LATE[j])
                    for x in range(N_DIL):
                        c, t0, m = span(i, x)
                        dve.wait_ge(s01_full if x < 2 else s2_full, u + 1)
                        y = W[x] - m * P
                        if not isinstance(it, int):
                            h = bass.ds(it * 2 + (x * H_G + b), 1)
                        else:
                            h = slice(it * 2 + x * H_G + b, it * 2 + x * H_G + b + 1)
                        dve.scalar_tensor_tensor(out=r[:, c:c + m * P], in0=md[x][:, y:W[x]], scalar=slope[:, h],
                                                 in1=S[x // 2][:, SEGB[x]:SEGB[x] + m * P], op0=ALU.mult,
                                                 op1=ALU.add).then_inc(biased, 1)
                    dve.wait_ge(biased, u * 3 + 3)
                    y = slice(j % BUF, j % BUF + 1)
                    need(dve, p_full, u - BUF + 1)
                    dve.reduce_max(mx[:, y], r[:, 0:len(keys(i)) * P], AX).then_inc(mx_full, 1)
                    dve.wait_ge(mx_full, u + 1)
                    dve.tensor_scalar(nmx[:, y], mx[:, y], -SCALE, None, ALU.mult).then_inc(nmx_full, 1)
                if there(it, j, 1):
                    _, b, i, u = unit(it, j, 1)
                    y = slice((j - 1) % BUF, (j - 1) % BUF + 1)
                    dve.wait_ge(p_full, u + 1)
                    need(dve, o_read, u - BUF + 1)
                    dve.reciprocal(rden[:, y], den[:, y]).then_inc(rden_full, 1)
                if j == 3 and (not isinstance(it, int) or it):
                    for h in range(2):
                        dve.wait_ge(oT_full, (it - 1) * 2 + h + 1)
                        dve.tensor_copy(oaT[:, bass.ds(it - 1, 1), h * 512:(h + 1) * 512]
                                        .rearrange("p a n -> p (a n)"), oT[:, :]).then_inc(oT_read, 1)

            LATE = [late(j - BUF) for j in range(U)]
            passes(dve, step, 5)


def gates_and_decode(nc, g):
    ctx = ExitStack()
    with ctx:
        sb = lambda n, s, d=F32: ctx.enter_context(nc.sbuf_tensor(n, s, d))
        sem = lambda n: ctx.enter_context(nc.semaphore(n))
        ps = lambda n, s: ctx.enter_context(nc.psum_tensor(n, s, F32))
        CH = 2 * KD
        GW = H_G * HD
        BHD, BHS = DEC * H_G, DEC * H_B
        N1, N2 = PAST // DIL[1][1], PAST // DIL[2][1]
        OWN = N1 + N2
        PG = PAST // PAGE
        D_SCORES_T, D_PROBS_T, D_VALUES, D_OUT_T = 3, 4, 5, 7
        S_SCORES_T, S_WEIGHTS_T, S_VALUES, S_OUT_T = 9, 11, 12, 15

        w = sb("g_w", [P, 2, KD, P])
        wh = sb("g_wh", [P, 2, KD, P], F32R)
        wl = sb("g_wl", [P, 2, KD, P], F32R)
        ul = sb("g_ul", [P, KD, NT], F32R)
        gate = g["spare"]
        acc = [ps(f"g_acc{s}", [P, 512]) for s in range(NSPLIT)]
        w_in = [sem(f"g_w_in{j}") for j in range(2)]
        g_out = [sem(f"g_g_out{j}") for j in range(2)]
        u_in = [sem(f"g_u_in{j}") for j in range(2)]
        wh_full, wl_full, ul_full, acc_full, gate_full = map(sem, (
            "g_wh_full", "g_wl_full", "g_ul_full", "g_acc_full", "g_gate_full"))
        uh, gT = g["uh"], g["gT"]
        win_v = g["w_in"].rearrange("a (k p) n -> p (a k) n", p=P)

        big = sb("g_big", [P, DEC, PG, B_W])
        big_flat = big[:, :, :, :].rearrange("p b x n -> p (b x n)")
        HALF = 2 * DEC * GW
        K = big_flat[:, 0:HALF].rearrange("p (x b n) -> p x b n", x=2, b=DEC)
        Q = big_flat[:, HALF:2 * HALF].rearrange("p (x b n) -> p x b n", x=2, b=DEC)
        V = sb("c_v", [P, 2, DEC, GW])
        dist = sb("c_dist", [P, 3])
        sl = sb("c_sl", [P, 2, H_G])
        bias = sb("c_bias", [P, 2, H_G])
        s = sb("c_s", [P, 2, BHD])
        st = g["spare_small"][0:BHD, 0:2 * P].rearrange("p (x n) -> p x n", x=2)
        mx = sb("c_mx", [BHD, 4])
        pT = sb("c_pT", [P, 2, BHD])
        head = g["spare_small"][0:H_B, 2 * P:2 * P + B_W].rearrange("p (h d) -> p h d", h=H_B)
        ones = sb("c_ones", [H_B, 1])
        om = sb("c_om", [H_G, DEC, GW])
        d_bank = ps("c_bank", [P, 512])
        s_ps = d_bank[0:BHD, 0:2 * P].rearrange("p (x n) -> p x n", x=2)
        pT_ps = d_bank[:, 2 * P:2 * P + 2 * BHD].rearrange("p (x n) -> p x n", x=2)
        oT_ps = d_bank[:, 384:384 + 2 * DEC].rearrange("p (x n) -> p x n", x=2)
        cleared, kq_in, v_in, pool_step, bias_set, dve_step, scored, s_full, sT_full, row_full, p_full, pn_full, \
            pT_full, pT_read, om_full, oT_full, done = map(sem, (
                "c_cleared", "c_kq_in", "c_v_in", "c_pool_step", "c_bias_set", "c_dve_step", "c_scored",
                "c_s_full", "c_sT_full", "c_row_full", "c_p_full", "c_pn_full", "c_pT_full", "c_pT_read",
                "c_om_full", "c_oT_full", "c_done"))

        KV = big
        wide = sb("e_wide", [P, DEC, B_W])
        Qs = wide
        table = sb("e_table", [1, DEC * PG], I32)
        es = sb("e_s", [P, PG, DEC, H_B])
        e_bias = sb("e_bias", [BHS, 1])
        z, ew, er, cum = (wide[0:BHS, n, 0:PAST] for n in range(4))
        aT = sb("e_aT", [P, PG, BHS])
        eom = wide[0:H_B, :, :]
        e_bank = ps("e_bank", [P, 512])
        es_ps = e_bank[0:BHS, 0:PG * P].rearrange("p (x n) -> p x n", x=PG)
        aT_ps = e_bank[:, 256:256 + PG * BHS].rearrange("p (x n) -> p x n", x=PG)
        eoT_ps = e_bank[:, 384:384 + CB * DEC].rearrange("p (x n) -> p x n", x=CB)
        table_in, ek_in, ev_in, eq_in, ebias_in, multiplied, e_step, es_full, esT_full, z_full, w_full, t_full, \
            al_full, a_full, aT_full, aT_read, eom_full, eoT_full = map(sem, (
                "e_table_in", "e_k_in", "e_v_in", "e_q_in", "e_bias_in", "e_multiplied", "e_step", "e_s_full",
                "e_sT_full", "e_z_full", "e_w_full", "e_t_full", "e_al_full", "e_a_full", "e_aT_full",
                "e_aT_read", "e_om_full", "e_oT_full"))
        pages = g["cache_sb"].rearrange("a n k c h d -> (a n) k c (h d)")
        n_pool = pages.shape[0]

        o_bank = [ps(f"o_bank{j}", [P, 512]) for j in range(3)]
        fill_full, fill_read = sem("o_fill_full"), sem("o_fill_read")
        D_FILLS, S_FILLS = DEC // 2, DEC
        FILLS = {D_VALUES: (0, 3), D_VALUES + 1: (3, D_FILLS), S_VALUES: (D_FILLS, D_FILLS + 3),
                 S_VALUES + 1: (D_FILLS + 3, D_FILLS + 6), S_VALUES + 2: (D_FILLS + 6, D_FILLS + S_FILLS)}
        ident, ztok, oaT, obT = g["ident"], g["ztok"], g["oaT"], g["obT"]
        tok = ztok[SEQ:NT, :]
        block = ctx.enter_context(nc.Block())

        def keys_or_values(eng, dst, cache_at, own_at, done_sem):
            for x, (p0, n, step) in enumerate(((0, P, 1), (0, N1, DIL[1][1]), (N1, N2, DIL[2][1]))):
                c = g[f"cache_win{x + 1}"]
                src = c[0, :, 0:n * step:step, cache_at, :, :].rearrange("b n h d -> n b (h d)")
                eng.dma_start(dst[p0:p0 + n, min(x, 1), :, :], src).then_inc(done_sem, 16)
            for x in range(N_DIL):
                eng.dma_start(dst[OWN + x:OWN + x + 1, 1, :, :],
                              tok[:, own_at + x * GW:own_at + (x + 1) * GW].unsqueeze(0)).then_inc(done_sem, 16)

        @block.sync
        def _(sp):
            def load(c):
                sp.dma_start(w[:, c % 2, :, :], win_v[:, :, QKV + c * P:QKV + (c + 1) * P]).then_inc(w_in[c % 2], 16)

            def load_pages(at, done_sem):
                for b in range(DEC):
                    for x in range(PG):
                        page = sp.value_load(table[0:1, b * PG + x:b * PG + x + 1], min_val=0, max_val=n_pool - 1)
                        sp.dma_start(KV[:, b, x, :], pages[bass.ds(page, 1), :, at, :]
                                     .rearrange("a k n -> (a k) n")).then_inc(done_sem, 16)

            load(0)
            load(1)
            for k in range(KD):
                need(sp, ul_full, k - 1)
                sp.dma_start(gate[:, k % 2, :], g["u_kept"][:, k * NT:(k + 1) * NT]).then_inc(u_in[k % 2], 16)
            sp.wait_ge(cleared, 3)
            keys_or_values(sp, K, 0, A_W, kq_in)
            for x, (p0, n) in enumerate(((0, P), (0, N1), (N1, N2))):
                q = tok[:, x * GW:(x + 1) * GW].unsqueeze(0)
                sp.dma_start(Q[p0:p0 + n, min(x, 1), :, :], q.broadcast_to([n, DEC, GW])).then_inc(kq_in, 16)
                sp.dma_start(Q[OWN + x:OWN + x + 1, 1, :, :], q).then_inc(kq_in, 16)
            keys_or_values(sp, V, 1, 2 * A_W, v_in)
            sp.dma_start(table[:, :], g["page_table"].rearrange("(a b) p -> a (b p)", a=1)).then_inc(table_in, 16)
            sp.dma_start(Qs[:, :, :], ztok[SEQ:NT, 3 * A_W:3 * A_W + B_W].unsqueeze(0)
                         .broadcast_to([P, DEC, B_W])).then_inc(eq_in, 16)
            for b in range(DEC):
                sp.dma_start(e_bias[b * H_B:(b + 1) * H_B, :], g["b_sb"].rearrange("a (h x) -> (a h) x", x=1))\
                    .then_inc(ebias_in, 16)
            sp.wait_ge(table_in, 16)
            for c in range(CH):
                if c + 2 < CH:
                    sp.wait_ge(wl_full, c + 1)
                    load(c + 2)
                if c == D_SCORES_T - 1:
                    sp.wait_ge(scored, 2)
                    load_pages(0, ek_in)
                if c == S_SCORES_T:
                    sp.wait_ge(es_full, DEC * PG)
                    load_pages(1, ev_in)
                sp.wait_ge(gate_full, (c + 1) * NSPLIT)
                sp.dma_start(gT[c, :, :], gate[:, c % 2, :]).then_inc(g_out[c % 2], 16)
            for b in range(2):
                sp.wait_ge(g_out[b], 16 * CH // 2)

        @block.gpsimd
        def _(pool):
            n = [0]

            def then(ins):
                n[0] += 1
                ins.then_inc(pool_step, 1)
                pool.wait_ge(pool_step, n[0])

            for t in (K, V, Q):
                pool.memset(t[:, 1, :, :], 0.0).then_inc(cleared, 1)
            nc_iota = dict(allow_small_or_imprecise_dtypes=True)
            then(pool.iota(dist[:, 0:1], pattern=[[0, 1]], base=P, channel_multiplier=-1, **nc_iota))
            then(pool.iota(dist[:, 1:2], pattern=[[0, 1]], base=PAST, channel_multiplier=-DIL[1][1], **nc_iota))
            then(pool.iota(dist[:, 2:3], pattern=[[0, 1]], base=PAST + N1 * DIL[2][1],
                           channel_multiplier=-DIL[2][1], **nc_iota))

            def keep(t, below, edge, fill):
                sign = -1 if below else 1
                then(pool.affine_select(out=t, in_=t, compare_op=ALU.is_ge, fill=fill,
                                        base=-sign * edge + (-1 if below else 0), pattern=[[0, 1]],
                                        channel_multiplier=sign))

            keep(dist[:, 1:2], True, N1, 0.0)
            keep(dist[:, 2:3], False, N1, 0.0)
            keep(dist[:, 2:3], True, OWN, 0.0)
            for h in range(H_G):
                then(pool.memset(sl[:, 0, h:h + 1], SLOPES[h]))
                then(pool.memset(sl[:, 1, h:h + 1], SLOPES[H_G + h]))
                keep(sl[:, 1, h:h + 1], True, N1, SLOPES[2 * H_G + h])
            then(pool.tensor_tensor(dist[:, 1:2], dist[:, 1:2], dist[:, 2:3], ALU.add))
            for x in range(2):
                then(pool.tensor_tensor(bias[:, x, :], sl[:, x, :], dist[:, x:x + 1].to_broadcast([P, H_G]),
                                        ALU.mult))
            for h in range(H_G):
                keep(bias[:, 1, h:h + 1], True, OWN + N_DIL, -NEG)
            then(pool.memset(ones[:, :], 1.0))
            then(pool.memset(head[:, :, :], 0.0))
            then(pool.affine_select(out=head[:, :, :], in_=head[:, :, :], compare_op=ALU.not_equal, fill=1.0,
                                    base=0, pattern=[[-1, H_B], [0, HD]], channel_multiplier=1))
            pool.memset(mx[:, :], 0.0).then_inc(bias_set, 1)

        @block.vector
        def _(dve):
            steps = [0]

            def then(ins):
                steps[0] += 1
                ins.then_inc(dve_step, 1)
                dve.wait_ge(dve_step, steps[0])

            def cut(c):
                dve.wait_ge(wh_full, c + 1)
                dve.tensor_tensor(wl[:, c % 2, :, :], w[:, c % 2, :, :], wh[:, c % 2, :, :], ALU.subtract)\
                    .then_inc(wl_full, 1)

            def dilated_scores(x):
                if x == 0:
                    dve.wait_ge(kq_in, 12 * 16)
                then(dve.tensor_tensor(K[:, x, :, :], K[:, x, :, :], Q[:, x, :, :], ALU.mult))
                dve.tensor_reduce(s[:, x, :], K[:, x, :, :].rearrange("p b (h d) -> p (b h) d", d=HD), AX,
                                  ALU.add).then_inc(scored, 1)
                dve.wait_ge(scored, x + 1)
                if x == 0:
                    dve.wait_ge(bias_set, 1)
                sv = s[:, x, :].rearrange("p (b h) -> p b h", h=H_G)
                dve.scalar_tensor_tensor(out=sv, in0=sv, scalar=SCALE,
                                         in1=bias[:, x, :].unsqueeze(1).to_broadcast([P, DEC, H_G]),
                                         op0=ALU.mult, op1=ALU.subtract).then_inc(s_full, 1)

            def dilated_softmax():
                dve.wait_ge(sT_full, 1)
                then(dve.tensor_copy(st[:, :, :], s_ps))
                then(dve.reduce_max(mx[:, 0:1], st[:, :, :].rearrange("p a b -> p (a b)"), AX))
                dve.tensor_scalar(mx[:, 1:2], mx[:, 0:1], -1.0, None, ALU.mult).then_inc(row_full, 1)
                dve.wait_ge(p_full, 1)
                then(dve.reciprocal(mx[:, 3:4], mx[:, 2:3]))
                dve.tensor_scalar(st[:, :, :], st[:, :, :], mx[:, 3:4], None, ALU.mult).then_inc(pn_full, 1)

            def stick_scores(b):
                if b == 0:
                    dve.wait_ge(eq_in, 16)
                    dve.wait_ge(ek_in, 16 * DEC * PG)
                dve.tensor_tensor(KV[:, b, :, :], KV[:, b, :, :], Qs[:, b, :].unsqueeze(1).to_broadcast([P, PG, B_W]),
                                  ALU.mult).then_inc(multiplied, 1)
                dve.wait_ge(multiplied, b + 1)
                for x in range(PG):
                    dve.tensor_reduce(es[:, x, b, :], KV[:, b, x, :].rearrange("p (h d) -> p h d", d=HD), AX,
                                      ALU.add).then_inc(es_full, 1)

            def stick_chain():
                dve.wait_ge(z_full, 1)
                dve.tensor_scalar(ew.bitcast(I32), z.bitcast(I32), 0x7FFFFFFF, None, ALU.bitwise_and)\
                    .then_inc(w_full, 1)
                then(dve.tensor_scalar(er, z, 0.0, None, ALU.max))
                dve.wait_ge(t_full, 2)
                then(dve.tensor_tensor_scan(cum[:, ::-1], ew[:, ::-1], er[:, ::-1], 0.0, ALU.add, ALU.add))
                dve.tensor_tensor(z, z, cum, ALU.subtract).then_inc(al_full, 1)

            def masked_outputs(f0, f1):
                for f in range(f0, f1):
                    dve.wait_ge(fill_full, f + 1)
                    if f < D_FILLS:
                        hm = head[0:H_G, 0:H_G, :].rearrange("p h d -> p (h d)").unsqueeze(1)
                        dve.tensor_tensor(om[:, 2 * f:2 * f + 2, :],
                                          o_bank[f % 3][0:H_G, :].rearrange("p (b n) -> p b n", b=2),
                                          hm.to_broadcast([H_G, 2, GW]), ALU.mult).then_inc(fill_read, 1)
                    else:
                        dve.tensor_tensor(eom[:, f - D_FILLS, :], o_bank[f % 3][0:H_B, :],
                                          head[:, :, :].rearrange("p h d -> p (h d)"), ALU.mult).then_inc(fill_read, 1)

            cut(0)
            for k in range(KD):
                dve.wait_ge(u_in[k % 2], 16 * (k // 2 + 1))
                dve.tensor_tensor(ul[:, k, :], gate[:, k % 2, :], uh[:, k, :], ALU.subtract).then_inc(ul_full, 1)
            for c in range(CH):
                if c + 1 < CH:
                    cut(c + 1)
                if c in (D_SCORES_T - 2, D_SCORES_T - 1):
                    dilated_scores(c - D_SCORES_T + 2)
                if c == D_SCORES_T:
                    dilated_softmax()
                if c == D_PROBS_T:
                    dve.wait_ge(pT_full, 1)
                    dve.tensor_copy(pT[:, :, :], pT_ps).then_inc(pT_read, 1)
                if c in FILLS:
                    masked_outputs(*FILLS[c])
                if c == D_OUT_T:
                    dve.wait_ge(oT_full, 1)
                    dve.tensor_copy(oaT[:, :, SEQ:NT], oT_ps).then_inc(done, 1)
                if S_SCORES_T - 4 <= c < S_SCORES_T:
                    for b in range(2):
                        stick_scores(2 * (c - S_SCORES_T + 4) + b)
                if c == S_SCORES_T:
                    stick_chain()
                if c == S_WEIGHTS_T:
                    dve.wait_ge(aT_full, 1)
                    dve.tensor_copy(aT[:, :, :], aT_ps).then_inc(aT_read, 1)
                if c == S_OUT_T:
                    dve.wait_ge(eoT_full, 1)
                    dve.tensor_copy(obT[:, :, SEQ:NT], eoT_ps).then_inc(done, 1)

        @block.scalar
        def _(act):
            def cut(c):
                act.wait_ge(w_in[c % 2], 16 * (c // 2 + 1))
                need(act, acc_full, (c - 1) * NSPLIT)
                act.activation(wh[:, c % 2, :, :], w[:, c % 2, :, :], ACT.Copy).then_inc(wh_full, 1)

            cut(0)
            for c in range(CH):
                if c + 1 < CH:
                    cut(c + 1)
                if c == D_SCORES_T:
                    act.wait_ge(row_full, 1)
                    act.activation(st[:, :, :], st[:, :, :], ACT.Exp, bias=mx[:, 1:2], accum_out=mx[:, 2:3])\
                        .then_inc(p_full, 1)
                if c == S_SCORES_T:
                    act.wait_ge(esT_full, 1)
                    act.wait_ge(ebias_in, 16 * DEC)
                    act.activation(z, es_ps.rearrange("p a b -> p (a b)"), ACT.Identity, scale=SCALE,
                                   bias=e_bias[:, :]).then_inc(z_full, 1)
                    act.wait_ge(w_full, 1)
                    act.activation(ew, ew, ACT.Exp, scale=-1.0).then_inc(t_full, 1)
                    act.wait_ge(t_full, 1)
                    act.activation(ew, ew, ACT.Ln, bias=1.0).then_inc(t_full, 1)
                if c == S_SCORES_T + 1:
                    act.wait_ge(al_full, 1)
                    act.activation(z, z, ACT.Exp).then_inc(a_full, 1)
                need(act, g_out[c % 2], 16 * (c // 2))
                for n in range(NSPLIT):
                    act.wait_ge(acc_full, c * NSPLIT + n + 1)
                    act.activation(gate[:, c % 2, n * NS:(n + 1) * NS], acc[n][:, 0:NS], ACT.Sigmoid)\
                        .then_inc(gate_full, 1)

        @block.tensor
        def _(pe):
            def values(f0, f1):
                for f in range(f0, f1):
                    need(pe, fill_read, f - 2)
                    if f < D_FILLS:
                        for b in (2 * f, 2 * f + 1):
                            for x in range(2):
                                last = pe.matmul(o_bank[f % 3][0:H_G, (b % 2) * GW:(b % 2 + 1) * GW],
                                                 pT[:, x, b * H_G:(b + 1) * H_G], V[:, x, b, :],
                                                 start=(x == 0), stop=(x == 1), skip_group_check=True)
                    else:
                        b = f - D_FILLS
                        for x in range(PG):
                            last = pe.matmul(o_bank[f % 3][0:H_B, :], aT[:, x, b * H_B:(b + 1) * H_B],
                                             KV[:, b, x, :], start=(x == 0), stop=(x == PG - 1))
                    last.then_inc(fill_full, 1)

            def outputs_T(o, masked, width, out_sem):
                for b in range(DEC):
                    for x in range(width // P):
                        last = pe.matmul(o[:, x, b:b + 1], masked[:, b, x * P:(x + 1) * P],
                                         ones[0:masked.shape[0], :], start=True, stop=True, skip_group_check=True)
                last.then_inc(out_sem, 1)

            for c in range(CH):
                if c == D_SCORES_T:
                    pe.wait_ge(s_full, 2)
                    for x in range(2):
                        last = pe.transpose(s_ps[:, x, :], s[:, x, :], ident[:, :])
                    last.then_inc(sT_full, 1)
                if c == D_PROBS_T:
                    pe.wait_ge(pn_full, 1)
                    for x in range(2):
                        last = pe.transpose(pT_ps[:, x, :], st[:, x, :], ident[0:BHD, 0:BHD])
                    last.then_inc(pT_full, 1)
                if c == D_VALUES:
                    pe.wait_ge(pT_read, 1)
                    pe.wait_ge(v_in, 6 * 16)
                if c == D_OUT_T:
                    pe.wait_ge(fill_read, D_FILLS)
                    outputs_T(oT_ps, om, GW, oT_full)
                if c == S_SCORES_T:
                    pe.wait_ge(es_full, DEC * PG)
                    for x in range(PG):
                        last = pe.transpose(es_ps[:, x, :], es[:, x, :, :].rearrange("p b h -> p (b h)"), ident[:, :])
                    last.then_inc(esT_full, 1)
                if c == S_WEIGHTS_T:
                    pe.wait_ge(a_full, 1)
                    for x in range(PG):
                        last = pe.transpose(aT_ps[:, x, :], z[:, x * P:(x + 1) * P], ident[0:BHS, 0:BHS])
                    last.then_inc(aT_full, 1)
                if c == S_VALUES:
                    pe.wait_ge(aT_read, 1)
                    pe.wait_ge(ev_in, 16 * DEC * PG)
                if c in FILLS:
                    values(*FILLS[c])
                if c == S_OUT_T:
                    pe.wait_ge(fill_read, D_FILLS + S_FILLS)
                    outputs_T(eoT_ps, eom, B_W, eoT_full)
                pe.wait_ge(wl_full, c + 1)
                for n in range(NSPLIT):
                    need(pe, gate_full, (c - 1) * NSPLIT + n + 1)
                    t = slice(n * NS, (n + 1) * NS)
                    for k in range(KD):
                        if c == 0 and n == 0:
                            pe.wait_ge(ul_full, k + 1)
                        last = products(pe, acc[n][:, 0:NS], wh[:, c % 2, k, :], wl[:, c % 2, k, :],
                                        uh[:, k, t], ul[:, k, t], k == 0, k == KD - 1)
                    last.then_inc(acc_full, 1)


def merge(nc, g):
    ctx = ExitStack()
    with ctx:
        sb = lambda n, s, d=F32: ctx.enter_context(nc.sbuf_tensor(n, s, d))
        sem = lambda n: ctx.enter_context(nc.semaphore(n))
        KA, KB = 2, CB
        KO = KA + KB
        PASSES = KD // 2
        U = 2 * NSPLIT
        w = sb("m_w", [P, 2, KO, P])
        wh = sb("m_wh", [P, 2, KO, P], F32R)
        wl = sb("m_wl", [P, 2, KO, P], F32R)
        oh = sb("m_oh", [P, KO, NT], F32R)
        ol = sb("m_ol", [P, KO, NT], F32R)
        gate = sb("m_gate", [P, 2, 2, NT])
        part = sb("m_part", [P, 2, 2, NS])
        bank = [[ctx.enter_context(nc.psum_tensor(f"m_{n}{j}", [P, 512], F32)) for n in ("ya", "yb")]
                for j in range(3)]
        w_in = [sem(f"m_w_in{j}") for j in range(2)]
        g_in = [sem(f"m_g_in{j}") for j in range(2)]
        full, wh_full, wl_full, oh_full, ol_full, part_full, merged = map(sem, (
            "m_full", "m_wh_full", "m_wl_full", "m_oh_full", "m_ol_full", "m_part_full", "m_merged"))
        oaT, obT, mT, gT = g["oaT"], g["obT"], g["mT"], g["gT"]
        o_of = lambda k: oaT[:, k, :] if k < KA else obT[:, k - KA, :]
        kp = lambda t: g[t].rearrange("a (k p) n -> p (a k) n", p=P)
        block = ctx.enter_context(nc.Block())

        @block.sync
        def _(sp):
            def load(it, b):
                f = it * 2 + b
                need(sp, wl_full, (it - 1) * 2 + b + 1)
                for lo, hi, t in ((0, KA, "w_oa"), (KA, KO, "w_ob")):
                    sp.dma_start(w[:, b, lo:hi, :], kp(t)[:, :, bass.ds(f * P, P)]).then_inc(w_in[b], 16)
                need(sp, part_full, ((it - 1) * U + (b + 1) * NSPLIT) * 2)
                for x in range(2):
                    sp.dma_start(gate[:, b, x, :], gT[bass.ds(f + x * KD, 1), :, :]
                                 .rearrange("a p n -> (a p) n")).then_inc(g_in[b], 16)

            for b in range(2):
                load(0, b)
            with sp.Fori(1, PASSES) as it:
                for b in range(2):
                    load(it, b)

        @block.tensor
        def _(pe):
            def step(it):
                for b in range(2):
                    pe.wait_ge(wl_full, it * 2 + b + 1)
                    for s in range(NSPLIT):
                        j = b * NSPLIT + s
                        need(pe, part_full, it * (2 * U) + (2 * j - 4))
                        t = slice(s * NS, (s + 1) * NS)
                        for k in range(KO):
                            if isinstance(it, int) and j == 0:
                                pe.wait_ge(ol_full, k + 1)
                            last = products(pe, bank[j % 3][k >= KA][:, 0:NS], wh[:, b, k, :], wl[:, b, k, :],
                                            oh[:, k, t], ol[:, k, t], k in (0, KA), k in (KA - 1, KO - 1))
                        last.then_inc(full, 1)

            looped(pe, PASSES, step)

        @block.scalar
        def _(act):
            def cut(it, b):
                act.wait_ge(w_in[b], it * 32 + 32)
                need(act, full, (it - 1) * U + (b + 1) * NSPLIT)
                act.activation(wh[:, b, :, :], w[:, b, :, :], ACT.Copy).then_inc(wh_full, 1)

            cut(0, 0)
            for k in range(KO):
                act.activation(oh[:, k, :], o_of(k), ACT.Copy).then_inc(oh_full, 1)
            cut(0, 1)
            with act.Fori(1, PASSES) as it:
                for b in range(2):
                    cut(it, b)

        @block.vector
        def _(dve):
            def cut(it, b):
                dve.wait_ge(wh_full, it * 2 + b + 1)
                dve.tensor_tensor(wl[:, b, :, :], w[:, b, :, :], wh[:, b, :, :], ALU.subtract).then_inc(wl_full, 1)

            cut(0, 0)
            for k in range(KO):
                dve.wait_ge(oh_full, k + 1)
                dve.tensor_tensor(ol[:, k, :], o_of(k), oh[:, k, :], ALU.subtract).then_inc(ol_full, 1)
            cut(0, 1)

            def step(it, more=True):
                for b in range(2):
                    dve.wait_ge(g_in[b], it * 32 + 32)
                    for s in range(NSPLIT):
                        j = b * NSPLIT + s
                        dve.wait_ge(full, it * U + j + 1)
                        need(dve, merged, it * U + (j - 1))
                        for x in range(2):
                            dve.tensor_tensor(part[:, j % 2, x, :], gate[:, b, x, s * NS:(s + 1) * NS],
                                              bank[j % 3][x][:, 0:NS], ALU.mult).then_inc(part_full, 1)
                    if more:
                        cut(it + 1, b)

            looped(dve, PASSES - 1, step)
            step(PASSES - 1, more=False)

        @block.gpsimd
        def _(pool):
            def step(it):
                for j in range(U):
                    pool.wait_ge(part_full, it * (2 * U) + (2 * j + 2))
                    s = j % NSPLIT
                    pool.tensor_tensor(mT[:, bass.ds(it * 2 + j // NSPLIT, 1), s * NS:(s + 1) * NS]
                                       .rearrange("p a n -> p (a n)"), part[:, j % 2, 0, :], part[:, j % 2, 1, :],
                                       ALU.add).then_inc(merged, 1)

            looped(pool, PASSES, step)


def residual(nc, g, x_of):
    ctx = ExitStack()
    with ctx:
        sb = lambda n, s, d=F32: ctx.enter_context(nc.sbuf_tensor(n, s, d))
        sem = lambda n: ctx.enter_context(nc.semaphore(n))
        ps = lambda n, s: ctx.enter_context(nc.psum_tensor(n, s, F32))
        w = sb("r_w", [P, KD, D])
        wr = sb("r_wr", [P, KD, NR])
        br = sb("r_br", [P, NR])
        gm = sb("r_gm", [P, KD])
        xt = sb("r_xt", [P, 2, D])
        sq = sb("r_sq", [P, D])
        st = sb("r_st", [P, 3, TT])
        u2T = sb("r_u2T", [P, 2, KD, P])
        acc = [ps(f"r_acc{j}", [P, D]) for j in range(2)]
        tp = ps("r_tp", [P, KD, P])
        lg = ps("r_lg", [P, 64])
        w_in = [sem(f"r_w_in{j}") for j in range(2)]
        x_in = [sem(f"r_x_in{j}") for j in range(2)]
        small_in, acc_full, h_full, ssq, mean, root, inv, u2_full, tp_full, u2T_full, lg_full, lg_read, cleared = \
            map(sem, ("r_small_in", "r_acc_full", "r_h_full", "r_ssq", "r_mean", "r_root", "r_inv", "r_u2_full",
                      "r_tp_full", "r_u2T_full", "r_lg_full", "r_lg_read", "r_cleared"))
        h, u2, logit, mT, ident = g["h"], g["u2"], g["logit"], g["mT"], g["ident"]
        kp = lambda t: g[t].rearrange("a (k p) n -> p (a k) n", p=P)
        block = ctx.enter_context(nc.Block())

        @block.sync
        def _(sp):
            for c in range(2):
                sp.dma_start(w[:, :, c * 512:(c + 1) * 512], kp("w_out")[:, :, c * 512:(c + 1) * 512])\
                    .then_inc(w_in[c], 16)
            with nc.allow_non_contiguous_dma(reason="1024 gains, once"):
                sp.dma_start(gm[:, :], g["g_moe"].rearrange("a (k p) -> p (a k)", p=P)).then_inc(small_in, 16)
            sp.dma_start(wr[:, :, 0:NG], kp("w_rg")).then_inc(small_in, 16)
            sp.dma_start(wr[:, :, NG:NR], kp("w_re")).then_inc(small_in, 16)
            sp.dma_start(br[:, 0:NG], g["b_rg"].broadcast_to([P, NG])).then_inc(small_in, 16)
            sp.dma_start(br[:, NG:NR], g["b_re"].broadcast_to([P, NE])).then_inc(small_in, 16)
            for t in range(TT):
                need(sp, h_full, t - 1)
                sp.dma_start(xt[0:rows(t), t % 2, :], x_of(t)).then_inc(x_in[t % 2], 16)

        @block.tensor
        def _(pe):
            for t in range(TT + 2):
                if t < TT:
                    r = rows(t)
                    need(pe, h_full, t - 1)
                    for c in range(2):
                        if t == 0:
                            pe.wait_ge(w_in[c], 16)
                        for k in range(KD):
                            last = pe.matmul(acc[t % 2][0:r, c * 512:(c + 1) * 512], mT[:, k, t * P:t * P + r],
                                             w[:, k, c * 512:(c + 1) * 512], start=(k == 0), stop=(k == KD - 1))
                    last.then_inc(acc_full, 1)
                if 1 <= t <= TT:
                    v, r = t - 1, rows(t - 1)
                    pe.wait_ge(u2_full, v + 1)
                    need(pe, u2T_full, v)
                    for k in range(KD):
                        last = pe.transpose(tp[:, k, 0:r], u2[0:r, v, k * P:(k + 1) * P], ident[0:r, 0:r])
                    last.then_inc(tp_full, 1)
                if t >= 2:
                    v, r = t - 2, rows(t - 2)
                    if v == 0:
                        pe.wait_ge(small_in, 16 * 5)
                    pe.wait_ge(u2T_full, v + 1)
                    need(pe, lg_read, v)
                    for k in range(KD):
                        last = pe.matmul(lg[0:r, 0:NR], u2T[:, v % 2, k, 0:r], wr[:, k, :],
                                         start=(k == 0), stop=(k == KD - 1))
                    last.then_inc(lg_full, 1)

        @block.scalar
        def _(act):
            for t in range(TT):
                r = rows(t)
                act.wait_ge(h_full, t + 1)
                need(act, ssq, t)
                act.activation(sq[0:r, :], h[0:r, t, :], ACT.Square, accum_out=st[0:r, 0, t:t + 1]).then_inc(ssq, 1)
                act.wait_ge(mean, t + 1)
                act.activation(st[0:r, 1, t:t + 1], st[0:r, 1, t:t + 1], ACT.Sqrt).then_inc(root, 1)

        @block.vector
        def _(dve):
            dve.wait_ge(small_in, 16 * 5)
            dve.wait_ge(cleared, 1)
            for t in range(TT + 2):
                if t < TT:
                    r = rows(t)
                    dve.wait_ge(x_in[t % 2], 16 * (t // 2 + 1))
                    dve.wait_ge(acc_full, t + 1)
                    dve.tensor_tensor(h[0:r, t, :], xt[0:r, t % 2, :], acc[t % 2][0:r, :], ALU.add).then_inc(h_full, 1)
                    dve.wait_ge(ssq, t + 1)
                    dve.tensor_scalar(st[0:r, 1, t:t + 1], st[0:r, 0, t:t + 1], 1.0 / D, EPS, ALU.mult,
                                      ALU.add).then_inc(mean, 1)
                    dve.wait_ge(root, t + 1)
                    dve.reciprocal(st[0:r, 2, t:t + 1], st[0:r, 1, t:t + 1]).then_inc(inv, 1)
                    dve.wait_ge(inv, t + 1)
                    dve.tensor_scalar(u2[0:r, t, :], h[0:r, t, :], st[0:r, 2, t:t + 1], None, ALU.mult)\
                        .then_inc(u2_full, 1)
                if 1 <= t <= TT:
                    v, r = t - 1, rows(t - 1)
                    dve.wait_ge(tp_full, v + 1)
                    need(dve, lg_full, v - 1)
                    dve.tensor_tensor(u2T[:, v % 2, :, 0:r], tp[:, :, 0:r],
                                      gm[:, :].unsqueeze(2).to_broadcast([P, KD, r]), ALU.mult).then_inc(u2T_full, 1)
                if t >= 2:
                    v, r = t - 2, rows(t - 2)
                    dve.wait_ge(lg_full, v + 1)
                    dve.tensor_tensor(logit[0:r, v, :], lg[0:r, 0:NR], br[0:r, :], ALU.add).then_inc(lg_read, 1)

        @block.gpsimd
        def _(pool):
            pool.memset(logit[:, QT, :], 0.0).then_inc(cleared, 1)


def route(nc, g):
    ctx = ExitStack()
    with ctx:
        sb = lambda n, s, d=F32: ctx.enter_context(nc.sbuf_tensor("t_" + n, s, d))
        sem = lambda n: ctx.enter_context(nc.semaphore("t_" + n))
        T4, T32 = [P, TT, NG], [P, TT, NE]
        gmax, ghit, gden, gprob, m1, m2, hit, e2 = (sb(n, [P, TT]) for n in (
            "gmax", "ghit", "gden", "gprob", "m1", "m2", "hit", "e2"))
        a4, oh4 = sb("a4", T4), sb("oh4", T4)
        el, a32, oh1, oh2, both, pos = (sb(n, T32) for n in ("el", "a32", "oh1", "oh2", "both", "pos"))
        desc = sb("desc", [P, NE])
        real = sb("real", [P, TT])
        tri = sb("tri", [P, P])
        ones = sb("ones", [P, P])
        zero = sb("zero", [P, NE])
        run = sb("run", [P, TT + 1, NE])
        tot = sb("tot", T32)
        cnt, start, nblk, nbi, nbe, c32, o32 = (sb(n, [P, NE]) for n in (
            "cnt", "start", "nblk", "nbi", "nbe", "c32", "o32"))
        thr = sb("thr", [P, 64])
        cmp9 = sb("cmp9", [P, NE, TT])
        cmpm = sb("cmpm", [P, MAXBLK // 2 + 2])
        me = sb("me", [P, 1])
        metaf = sb("metaf", [P, 4])
        metai = sb("metai", [P, 4], I32)
        destf = sb("destf", [P, 2, TT])
        fill = sb("fill", [P, D])
        rank_ps = ctx.enter_context(nc.psum_tensor("t_rank_ps", [P, 512], F32))
        tot_ps = ctx.enter_context(nc.psum_tensor("t_tot_ps", [P, 512], F32))
        const, step_, gexp_in, gexp, eexp_in, eexp, both_full, sums, dest_set, meta_set, meta_out = map(sem, (
            "const", "step", "gexp_in", "gexp", "eexp_in", "eexp", "both_full", "sums", "dest_set", "meta_set",
            "meta_out"))
        moved = g["pool_dma"][2]
        logit, u2, dest, wt, xs, ys, meta, meta_row = (g[n] for n in (
            "logit", "u2", "dest", "wt", "xs", "ys", "meta", "meta_row"))
        block = ctx.enter_context(nc.Block())
        NTHR = max(TT, MAXBLK // 2 + 2)

        @block.gpsimd
        def _(pool):
            n = [0]

            def then(ins):
                n[0] += 1
                ins.then_inc(const, 1)
                pool.wait_ge(const, n[0])

            kw = dict(allow_small_or_imprecise_dtypes=True)
            then(pool.iota(desc[:, :], pattern=[[-1, NE]], base=NE, channel_multiplier=0, **kw))
            then(pool.iota(thr[:, 0:NTHR], pattern=[[P, NTHR]], base=0, channel_multiplier=0, **kw))
            then(pool.iota(me[:, :], pattern=[[0, 1]], base=0, channel_multiplier=1, **kw))
            then(pool.memset(zero[:, :], 0.0))
            then(pool.memset(real[:, :], 1.0))
            then(pool.affine_select(out=real[:, QT:TT], in_=real[:, QT:TT], compare_op=ALU.is_ge, fill=0.0,
                                    base=DEC - 1, pattern=[[0, 1]], channel_multiplier=-1))
            then(pool.memset(ones[:, :], 1.0))
            then(pool.memset(tri[:, :], 1.0))
            then(pool.affine_select(out=tri[:, :], in_=tri[:, :], compare_op=ALU.is_gt, fill=0.0, base=0,
                                    pattern=[[1, P]], channel_multiplier=-1))
            then(pool.memset(fill[:, :], 0.0))
            pool.dma_start(xs[ASG:SLOTS, :], fill[:, :]).then_inc(moved, 16)
            for b in range(2):
                pool.dma_start(ys[ASG + b * 64:ASG + b * 64 + 64, :], fill[0:64, :])\
                    .then_inc(g["pool_dma"][3 + b], 16)
            pool.wait_ge(dest_set, 2)
            for t in range(TT):
                for c in range(2):
                    pool.indirect_dma_start(xs[:, :], bass.IndirectOffsetOnAxis(ap=dest[0:rows(t), c, t:t + 1], axis=0),
                                            u2[0:rows(t), t, :], None).then_inc(moved, 16)
            pool.wait_ge(moved, 16 * (2 * TT + 1))
            for b in range(2):
                pool.wait_ge(g["pool_dma"][3 + b], 16)

        @block.sync
        def _(sp):
            sp.wait_ge(meta_set, 1)
            sp.dma_start(meta, metai[:, :]).then_inc(meta_out, 16)
            sp.wait_ge(meta_out, 16)
            sp.dma_start(meta_row[:, :], meta.rearrange("(a p) c -> a (p c)", a=1)).then_inc(meta_out, 16)
            sp.wait_ge(meta_out, 32)

        @block.scalar
        def _(act):
            act.wait_ge(gexp_in, 1)
            act.activation(a4[:, :, :], a4[:, :, :], ACT.Exp).then_inc(gexp, 1)
            act.wait_ge(eexp_in, 1)
            act.activation(e2[:, :], e2[:, :], ACT.Exp).then_inc(eexp, 1)

        @block.tensor
        def _(pe):
            pe.wait_ge(both_full, 1)
            b = both[:, :, :].rearrange("p t e -> p (t e)")
            pe.matmul(rank_ps[:, 0:TT * NE], tri[:, :], b, start=True, stop=True)
            pe.matmul(tot_ps[:, 0:TT * NE], ones[:, :], b, start=True, stop=True).then_inc(sums, 1)

        @block.vector
        def _(dve):
            n = [0]

            def then(ins):
                n[0] += 1
                ins.then_inc(step_, 1)
                dve.wait_ge(step_, n[0])

            wide = lambda t, w: t.unsqueeze(2).to_broadcast([P, TT, w])
            over_t = lambda t, w: t.unsqueeze(1).to_broadcast([P, TT, w])
            g4, e32 = logit[:, :, 0:NG], logit[:, :, NG:NR]

            def first_max(src, width, mx, tmp, out):
                then(dve.tensor_reduce(mx[:, :], src, AX, ALU.max))
                then(dve.tensor_tensor(tmp, src, wide(mx[:, :], width), ALU.is_equal))
                then(dve.tensor_tensor(tmp, tmp, over_t(desc[:, 0:width], width), ALU.mult))
                then(dve.tensor_reduce(hit[:, :], tmp, AX, ALU.max))
                then(dve.tensor_tensor(out, tmp, wide(hit[:, :], width), ALU.is_equal))

            dve.wait_ge(const, 10)
            first_max(g4, NG, gmax, a4[:, :, :], oh4[:, :, :])
            dve.tensor_tensor(a4[:, :, :], g4, wide(gmax[:, :], NG), ALU.subtract).then_inc(gexp_in, 1)
            ohe = oh4[:, :, :].unsqueeze(3).to_broadcast([P, TT, NG, EPG])
            four = lambda t: t.rearrange("p t (a b) -> p t a b", b=EPG)
            then(dve.tensor_copy(four(a32[:, :, :]), ohe))
            then(dve.tensor_tensor(el[:, :, :], e32, a32[:, :, :], ALU.mult))
            then(dve.tensor_scalar(a32[:, :, :], a32[:, :, :], -NEG, NEG, ALU.mult, ALU.add))
            then(dve.tensor_tensor(el[:, :, :], el[:, :, :], a32[:, :, :], ALU.add))
            first_max(el[:, :, :], NE, m1, a32[:, :, :], oh1[:, :, :])
            then(dve.scalar_tensor_tensor(out=el[:, :, :], in0=oh1[:, :, :], scalar=3 * NEG, in1=el[:, :, :],
                                          op0=ALU.mult, op1=ALU.add))
            first_max(el[:, :, :], NE, m2, a32[:, :, :], oh2[:, :, :])
            dve.tensor_tensor(e2[:, :], m2[:, :], m1[:, :], ALU.subtract).then_inc(eexp_in, 1)
            then(dve.tensor_tensor(both[:, :, :], oh1[:, :, :], oh2[:, :, :], ALU.add))
            dve.tensor_tensor(both[:, :, :], both[:, :, :], wide(real[:, :], NE), ALU.mult).then_inc(both_full, 1)
            dve.wait_ge(gexp, 1)
            then(dve.tensor_reduce(gden[:, :], a4[:, :, :], AX, ALU.add))
            dve.wait_ge(eexp, 1)
            then(dve.tensor_scalar(m1[:, :], e2[:, :], 1.0, None, ALU.add))
            then(dve.tensor_tensor(gden[:, :], gden[:, :], m1[:, :], ALU.mult))
            then(dve.reciprocal(wt[:, 0, :], gden[:, :]))
            then(dve.tensor_tensor(wt[:, 1, :], wt[:, 0, :], e2[:, :], ALU.mult))
            dve.wait_ge(sums, 1)
            flat = lambda t: t[:, :, :].rearrange("p t e -> p (t e)")
            then(dve.tensor_copy(flat(tot), tot_ps[:, 0:TT * NE]))
            then(dve.tensor_reduce(cnt[:, :], tot[:, :, :].rearrange("p t e -> p e t"), AX, ALU.add))
            then(dve.tensor_tensor_scan(start[:, :], cnt[:, :], zero[:, :], 0.0, ALU.add, ALU.add))
            then(dve.tensor_tensor(start[:, :], start[:, :], cnt[:, :], ALU.subtract))
            then(dve.tensor_copy(run[:, 0, :], start[:, :]))
            for t in range(TT):
                then(dve.tensor_tensor(run[:, t + 1, :], run[:, t, :], tot[:, t, :], ALU.add))
            then(dve.tensor_tensor(flat(pos), run[:, 0:TT, :].rearrange("p t e -> p (t e)"), rank_ps[:, 0:TT * NE],
                                   ALU.add))
            for c, oh in enumerate((oh1, oh2)):
                then(dve.tensor_tensor(a32[:, :, :], oh[:, :, :], pos[:, :, :], ALU.mult))
                then(dve.tensor_reduce(destf[:, c, :], a32[:, :, :], AX, ALU.add))
                dve.tensor_copy(dest[:, c, :], destf[:, c, :]).then_inc(dest_set, 1)
            then(dve.tensor_tensor(cmp9[:, :, :], cnt[:, :].unsqueeze(2).to_broadcast([P, NE, TT]),
                                   thr[:, 0:TT].unsqueeze(1).to_broadcast([P, NE, TT]), ALU.is_gt))
            then(dve.tensor_reduce(nblk[:, :], cmp9[:, :, :], AX, ALU.add))
            then(dve.tensor_tensor_scan(nbi[:, :], nblk[:, :], zero[:, :], 0.0, ALU.add, ALU.add))
            then(dve.tensor_tensor(nbe[:, :], nbi[:, :], nblk[:, :], ALU.subtract))
            then(dve.tensor_scalar(c32[:, :], nbi[:, :], me[:, :], None, ALU.is_le))
            then(dve.tensor_reduce(metaf[:, 0:1], c32[:, :], AX, ALU.add))
            then(dve.tensor_scalar(metaf[:, 0:1], metaf[:, 0:1], float(NE - 1), None, ALU.min))
            then(dve.tensor_scalar(o32[:, :], nbe[:, :], me[:, :], None, ALU.is_le))
            then(dve.tensor_tensor(o32[:, :], o32[:, :], c32[:, :], ALU.subtract))
            then(dve.scalar_tensor_tensor(out=c32[:, :], in0=nbe[:, :], scalar=-float(P), in1=start[:, :],
                                          op0=ALU.mult, op1=ALU.add))
            then(dve.tensor_tensor(c32[:, :], c32[:, :], o32[:, :], ALU.mult))
            then(dve.tensor_reduce(metaf[:, 1:2], c32[:, :], AX, ALU.add))
            then(dve.scalar_tensor_tensor(out=metaf[:, 1:2], in0=me[:, :], scalar=float(P), in1=metaf[:, 1:2],
                                          op0=ALU.mult, op1=ALU.add))
            then(dve.tensor_scalar(metaf[:, 1:2], metaf[:, 1:2], float(ASG), None, ALU.min))
            then(dve.tensor_scalar(metaf[:, 3:4], nbi[:, NE - 1:NE], float(P // 2), None, ALU.mult))
            then(dve.tensor_scalar(cmpm[:, :], thr[:, 0:MAXBLK // 2 + 2], metaf[:, 3:4], None, ALU.is_lt))
            then(dve.tensor_reduce(metaf[:, 2:3], cmpm[:, :], AX, ALU.add))
            then(dve.tensor_scalar(metaf[:, 2:3], metaf[:, 2:3], -1.0, None, ALU.add))
            dve.tensor_copy(metai[:, :], metaf[:, :]).then_inc(meta_set, 1)


def experts(nc, g):
    ctx = ExitStack()
    with ctx:
        sb = lambda n, s, d=F32: ctx.enter_context(nc.sbuf_tensor("x_" + n, s, d))
        sem = lambda n: ctx.enter_context(nc.semaphore("x_" + n))
        ps = lambda n, s: ctx.enter_context(nc.psum_tensor("x_" + n, s, F32))
        wg, wu = (sb(n, [P, KD, FE]) for n in ("wg", "wu"))
        wgh, wgl, wuh, wul = (sb(n, [P, KD, FE], F32R) for n in ("wgh", "wgl", "wuh", "wul"))
        wd = sb("wd", [P, 2, KF, D])
        gm = sb("gm", [P, KD])
        x = sb("x", [P, 2, D])
        xT = sb("xT", [P, KD, P])
        xh, xl = (sb(n, [P, KD, P], F32R) for n in ("xh", "xl"))
        sg, gs, hm = (sb(n, [P, FE]) for n in ("sg", "gs", "hm"))
        hT = sb("hT", [P, KF, P])
        y = sb("y", [P, 2, D])
        tpx = [ps(f"tpx{j}", [P, 4, P]) for j in range(2)]
        G, U_ = ps("G", [P, FE]), ps("U", [P, FE])
        tph = ps("tph", [P, KF, P])
        Y = [ps(f"Y{j}", [P, 512]) for j in range(2)]
        x_in, d_in = ([sem(f"{n}{b}") for b in range(2)] for n in ("x_in", "d_in"))
        wg_in, wu_in = ([sem(f"{n}{b}") for b in range(2)] for n in ("wg_in", "wu_in"))
        gh_full, gl_full, uh_full, ul_full, xh_full, xl_full = map(sem, (
            "gh_full", "gl_full", "uh_full", "ul_full", "xh_full", "xl_full"))
        HALVES = [slice(0, KD // 2), slice(KD // 2, KD)]
        y_out = g["pool_dma"][3:5]
        gm_in, tpx_full, xT_full, g_full, u_full, sg_full, gs_full, hm_full, tph_full, hT_full, y_full, y_read = map(
            sem, ("gm_in", "tpx_full", "xT_full", "g_full", "u_full", "sg_full", "gs_full", "hm_full", "tph_full",
                  "hT_full", "y_full", "y_read"))
        xs, ys, meta_row, ident = g["xs"], g["ys"], g["meta_row"], g["ident"]
        Wg = g["w_gate"].rearrange("a e (k p) f -> (a e) p k f", p=P)
        Wu = g["w_up"].rearrange("a e (k p) f -> (a e) p k f", p=P)
        Wd = g["w_down"].rearrange("a e (k p) f -> (a e) p k f", p=P)
        block = ctx.enter_context(nc.Block())

        def pairs(eng):
            return eng.value_load(meta_row[0:1, 2:3], min_val=(-(-ASG // P) + 1) // 2 - 1,
                                  max_val=(MAXBLK + 1) // 2 - 1) + 1

        def passes(eng, step, end):
            n = pairs(eng)
            for j in range(2):
                step(0, j)
            with eng.Fori(1, n) as it:
                for j in range(2):
                    step(it, j)
            if end:
                end(n)

        @block.sync
        def _(sp):
            with nc.allow_non_contiguous_dma(reason="1024 gains, once"):
                sp.dma_start(gm[:, :], g["g_moe"].rearrange("a (k p) -> p (a k)", p=P)).then_inc(gm_in, 16)

            def step(it, b):
                n = it * 2 + b
                col = n * 4
                e = sp.value_load(meta_row[0:1, bass.ds(col, 1)], min_val=0, max_val=NE - 1)
                row = sp.value_load(meta_row[0:1, bass.ds(col + 1, 1)], min_val=0, max_val=ASG)
                w = lambda W: W[bass.ds(e, 1), :, :, :].rearrange("a p k f -> (a p) k f")
                need(sp, tpx_full, it * 4 + (2 * b - 2))
                sp.dma_start(x[:, b, :], xs[bass.ds(row, P), :]).then_inc(x_in[b], 16)
                for dst, src, cut, done in ((wg, Wg, gl_full, wg_in), (wu, Wu, ul_full, wu_in)):
                    for half in range(2):
                        need(sp, cut, it * 4 + (2 * b - 1 + half))
                        sp.dma_start(dst[:, HALVES[half], :], w(src)[:, HALVES[half], :]).then_inc(done[half], 16)
                need(sp, y_full, it * 4 + (2 * b - 2))
                sp.dma_start(wd[:, b, :, :], w(Wd)).then_inc(d_in[b], 16)

            passes(sp, step, None)

        @block.tensor
        def _(pe):
            def turn(it, b):
                pe.wait_ge(x_in[b], it * 16 + 16)
                for c in range(2):
                    need(pe, xT_full, it * 4 + (2 * b + c - 1))
                    for k in range(4):
                        last = pe.transpose(tpx[c][:, k, :], x[:, b, (c * 4 + k) * P:(c * 4 + k + 1) * P], ident[:, :])
                    last.then_inc(tpx_full, 1)

            def gate_up(n):
                pe.wait_ge(xl_full, n + 1)
                need(pe, hm_full, n)
                for bank, wh, wl, cut, s in ((G, wgh, wgl, gl_full, g_full), (U_, wuh, wul, ul_full, u_full)):
                    pe.wait_ge(cut, n * 2 + 2)
                    for k in range(KD):
                        last = products(pe, bank[:, :], xh[:, k, :], xl[:, k, :], wh[:, k, :], wl[:, k, :],
                                        k == 0, k == KD - 1)
                    last.then_inc(s, 1)

            def down(p_, b, n):
                pe.wait_ge(hm_full, n + 1)
                need(pe, hT_full, n)
                for k in range(KF):
                    last = pe.transpose(tph[:, k, :], hm[:, k * P:(k + 1) * P], ident[:, :])
                last.then_inc(tph_full, 1)
                pe.wait_ge(d_in[b], p_ * 16 + 16)
                pe.wait_ge(hT_full, n + 1)
                for c in range(2):
                    need(pe, y_read, n * 2 - 1 + c)
                    for k in range(KF):
                        last = pe.matmul(Y[c][:, :], hT[:, k, :], wd[:, b, k, c * 512:(c + 1) * 512],
                                         start=(k == 0), stop=(k == KF - 1))
                    last.then_inc(y_full, 1)

            def step(it, j):
                behind = j or not isinstance(it, int)
                p_, b, n = (it, 0, it * 2) if j else (it - 1, 1, it * 2 - 1)
                if behind:
                    gate_up(n)
                turn(it, j)
                if behind:
                    down(p_, b, n)

            def end(np_):
                gate_up(np_ * 2 - 1)
                down(np_ - 1, 1, np_ * 2 - 1)

            passes(pe, step, end)

        @block.scalar
        def _(act):
            def sigmoid(n):
                act.wait_ge(g_full, n + 1)
                need(act, gs_full, n)
                act.activation(sg[:, :], G[:, :], ACT.Sigmoid).then_inc(sg_full, 1)

            def high(n, w, wh, w_in, used, full):
                need(act, used, n)
                for half in range(2):
                    act.wait_ge(w_in[half], n * 16 + 16)
                    act.activation(wh[:, HALVES[half], :], w[:, HALVES[half], :], ACT.Copy).then_inc(full, 1)

            def output(p_, b, n):
                act.wait_ge(y_out[b], p_ * 16 + 16)
                for c in range(2):
                    act.wait_ge(y_full, n * 2 + c + 1)
                    act.activation(y[:, b, c * 512:(c + 1) * 512], Y[c][:, :], ACT.Copy).then_inc(y_read, 1)

            def step(it, j):
                behind = j or not isinstance(it, int)
                p_, b, n = (it, 0, it * 2) if j else (it - 1, 1, it * 2 - 1)
                new = it * 2 + j
                if behind:
                    sigmoid(n)
                high(new, wg, wgh, wg_in, g_full, gh_full)
                act.wait_ge(xT_full, new * 2 + 2)
                act.activation(xh[:, :, :], xT[:, :, :], ACT.Copy).then_inc(xh_full, 1)
                high(new, wu, wuh, wu_in, u_full, uh_full)
                if behind:
                    output(p_, b, n)

            def end(np_):
                sigmoid(np_ * 2 - 1)
                output(np_ - 1, 1, np_ * 2 - 1)

            passes(act, step, end)

        @block.vector
        def _(dve):
            dve.wait_ge(gm_in, 16)

            def turn(n):
                need(dve, u_full, n)
                for c in range(2):
                    dve.wait_ge(tpx_full, n * 2 + c + 1)
                    dve.tensor_tensor(xT[:, c * 4:(c + 1) * 4, :], tpx[c][:, :, :],
                                      gm[:, c * 4:(c + 1) * 4].unsqueeze(2).to_broadcast([P, 4, P]),
                                      ALU.mult).then_inc(xT_full, 1)

            def low_x(n):
                dve.wait_ge(xh_full, n + 1)
                dve.tensor_tensor(xl[:, :, :], xT[:, :, :], xh[:, :, :], ALU.subtract).then_inc(xl_full, 1)

            def low(n, half, w, wh, wl, high_full, full):
                dve.wait_ge(high_full, n * 2 + half + 1)
                s = HALVES[half]
                dve.tensor_tensor(wl[:, s, :], w[:, s, :], wh[:, s, :], ALU.subtract).then_inc(full, 1)

            def gated(n):
                dve.wait_ge(sg_full, n + 1)
                dve.tensor_tensor(gs[:, :], sg[:, :], G[:, :], ALU.mult).then_inc(gs_full, 1)

            def hidden(n):
                dve.wait_ge(u_full, n + 1)
                dve.wait_ge(gs_full, n + 1)
                need(dve, tph_full, n)
                dve.tensor_tensor(hm[:, :], gs[:, :], U_[:, :], ALU.mult).then_inc(hm_full, 1)

            def hidden_T(n):
                dve.wait_ge(tph_full, n + 1)
                need(dve, y_full, n * 2)
                dve.tensor_copy(hT[:, :, :], tph[:, :, :]).then_inc(hT_full, 1)

            def step(it, j):
                behind = j or not isinstance(it, int)
                n, new = it * 2 - 1 + j, it * 2 + j
                if behind:
                    gated(n)
                low(new, 0, wg, wgh, wgl, gh_full, gl_full)
                if behind:
                    hidden(n)
                    hidden_T(n)
                turn(new)
                low(new, 1, wg, wgh, wgl, gh_full, gl_full)
                low_x(new)
                for half in range(2):
                    low(new, half, wu, wuh, wul, uh_full, ul_full)

            def end(np_):
                gated(np_ * 2 - 1)
                hidden(np_ * 2 - 1)
                hidden_T(np_ * 2 - 1)

            passes(dve, step, end)

        @block.gpsimd
        def _(pool):
            def step(it, b):
                n = it * 2 + b
                row = pool.value_load(meta_row[0:1, bass.ds(n * 4 + 1, 1)], min_val=0, max_val=ASG)
                pool.wait_ge(y_read, n * 2 + 2)
                if b:
                    pool.wait_ge(y_out[0], it * 16 + 32)
                else:
                    pool.wait_ge(y_out[1], it * 16 + 16)
                pool.dma_start(ys[bass.ds(row, P), :], y[:, b, :]).then_inc(y_out[b], 16)

            def end(np_):
                for b in range(2):
                    pool.wait_ge(y_out[b], np_ * 16 + 16)
                pool.wait_ge(gm_in, 16)

            passes(pool, step, end)


def finish(nc, g, p_of, y_of):
    ctx = ExitStack()
    with ctx:
        sb = lambda n, s, d=F32: ctx.enter_context(nc.sbuf_tensor("f_" + n, s, d))
        sem = lambda n: ctx.enter_context(nc.semaphore("f_" + n))
        ps = lambda n, s: ctx.enter_context(nc.psum_tensor("f_" + n, s, F32))
        KP = PLE // P
        C = D // 2
        wpgh, wpgl = (sb(n, [P, KD, D], F32R) for n in ("wpgh", "wpgl"))
        wpph, wppl = (sb(n, [P, KP, D], F32R) for n in ("wpph", "wppl"))
        gp = sb("gp", [P, KD])
        gf = sb("gf", [P, D])
        y2 = sb("y2", [P, 2, 2, D])
        pt = sb("pt", [P, 2, PLE])
        pTh, pTl = (sb(n, [P, 2, KP, P], F32R) for n in ("pTh", "pTl"))
        sq = sb("sq", [P, D])
        st = sb("st", [P, 6, TT])
        un = sb("un", [P, 2, D])
        uT = sb("uT", [P, KD, P])
        uTh, uTl = (sb(n, [P, 2, KD, P], F32R) for n in ("uTh", "uTl"))
        sig = sb("sig", [P, 2, D])
        pps = sb("pps", [P, 2, D])
        yo = sb("yo", [P, 2, D])
        tp = ps("tp", [P, KD, P])
        gate = ps("gate", [P, D])
        pp = ps("pp", [P, D])
        tpp = ps("tpp", [P, KP, P])
        gp_in, gf_in, ssq, mean, root, inv, un_full, tp_full, uT_full, uTh_full, uTl_full, tpp_full, \
            pTh_full, pTl_full, wh_full, wl_full, gate_full, pp_full, sig_full, pps_full, mix, h_full, ssq2, mean2, \
            root2, inv2, yo_full = map(sem, (
                "gp_in", "gf_in", "ssq", "mean", "root", "inv", "un_full", "tp_full", "uT_full", "uTh_full",
                "uTl_full", "tpp_full", "pTh_full", "pTl_full", "wh_full", "wl_full", "gate_full", "pp_full",
                "sig_full", "pps_full", "mix", "h_full", "ssq2", "mean2", "root2", "inv2", "yo_full"))
        p_in, y_out = ([sem(f"{n}{b}") for b in range(2)] for n in ("p_in", "y_out"))
        piece_in = [sem(f"piece_in{n}") for n in range(5)]
        y_in = g["pool_dma"][5:7]
        h, wt, dest, ys, ident = (g[n] for n in ("h", "wt", "dest", "ys", "ident"))
        kp = lambda t: g[t].rearrange("a (k p) n -> p (a k) n", p=P)
        PC = 2 * D // KD
        place = [t[:, :, :].rearrange("p b n -> p (b n)") for t in (pps, yo, sig, pps, yo)]
        pieces = [(place[n].rearrange("p (k n) -> p k n", k=KD), kp("w_pg")[:, :, n * PC:(n + 1) * PC],
                   wpgh[:, :, n * PC:(n + 1) * PC], wpgl[:, :, n * PC:(n + 1) * PC]) for n in range(D // PC)]
        pieces.append((place[-1].rearrange("p (k n) -> p k n", k=KP), kp("w_pp"), wpph[:, :, :], wppl[:, :, :]))
        NP = len(pieces)
        block = ctx.enter_context(nc.Block())

        @block.sync
        def _(sp):
            with nc.allow_non_contiguous_dma(reason="1024 gains, once"):
                sp.dma_start(gp[:, :], g["g_ple"].rearrange("a (k p) -> p (a k)", p=P)).then_inc(gp_in, 16)
            for t in range(2):
                sp.dma_start(pt[0:rows(t), t % 2, :], p_of(t)).then_inc(p_in[t % 2], 16)
            for n, (raw, w, _, _) in enumerate(pieces):
                need(sp, wl_full, n - 2)
                sp.dma_start(raw, w).then_inc(piece_in[n], 16)
            sp.dma_start(gf[:, :], g["g_final"].unsqueeze(0).broadcast_to([P, D])).then_inc(gf_in, 16)
            for t in range(2, TT + 3):
                if t < TT:
                    sp.wait_ge(tpp_full, t - 1)
                    sp.dma_start(pt[0:rows(t), t % 2, :], p_of(t)).then_inc(p_in[t % 2], 16)
                v = t - 3
                if v >= 0:
                    sp.wait_ge(yo_full, v + 1)
                    sp.dma_start(y_of(v), yo[0:rows(v), v % 2, :]).then_inc(y_out[v % 2], 16)
            for b in range(2):
                sp.wait_ge(y_out[b], 16 * len(range(b, TT, 2)))

        @block.gpsimd
        def _(pool):
            for t in range(TT):
                need(pool, mix, 2 * (t - 1))
                for c in range(2):
                    pool.indirect_dma_start(y2[0:rows(t), t % 2, c, :], None, ys[:, :],
                                            bass.IndirectOffsetOnAxis(ap=dest[0:rows(t), c, t:t + 1], axis=0))\
                        .then_inc(y_in[t % 2], 16)

        @block.tensor
        def _(pe):
            for t in range(TT + 1):
                if t < TT:
                    r = rows(t)
                    pe.wait_ge(p_in[t % 2], 16 * (t // 2 + 1))
                    need(pe, pTl_full, t)
                    for k in range(KP):
                        last = pe.transpose(tpp[:, k, 0:r], pt[0:r, t % 2, k * P:(k + 1) * P], ident[0:r, 0:r])
                    last.then_inc(tpp_full, 1)
                    pe.wait_ge(un_full, t + 1)
                    need(pe, uT_full, t)
                    for k in range(KD):
                        last = pe.transpose(tp[:, k, 0:r], un[0:r, t % 2, k * P:(k + 1) * P], ident[0:r, 0:r])
                    last.then_inc(tp_full, 1)
                if t >= 1:
                    v, r = t - 1, rows(t - 1)
                    pe.wait_ge(pTl_full, v + 1)
                    pe.wait_ge(uTl_full, v + 1)
                    for c in range(2):
                        if v == 0:
                            pe.wait_ge(wl_full, 3 + c)
                        need(pe, sig_full, (v - 1) * 2 + c + 1)
                        cols = slice(c * C, (c + 1) * C)
                        for k in range(KD):
                            last = products(pe, gate[0:r, cols], uTh[:, v % 2, k, 0:r], uTl[:, v % 2, k, 0:r],
                                            wpgh[:, k, cols], wpgl[:, k, cols], k == 0, k == KD - 1)
                        last.then_inc(gate_full, 1)
                    if v == 0:
                        pe.wait_ge(wl_full, NP)
                    need(pe, pps_full, v)
                    for c in range(2):
                        cols = slice(c * C, (c + 1) * C)
                        for k in range(KP):
                            last = products(pe, pp[0:r, cols], pTh[:, v % 2, k, 0:r], pTl[:, v % 2, k, 0:r],
                                            wpph[:, k, cols], wppl[:, k, cols], k == 0, k == KP - 1)
                    last.then_inc(pp_full, 1)

        @block.scalar
        def _(act):
            def norm_root(t):
                r = rows(t)
                act.wait_ge(mix, 2 * t + 2)
                need(act, ssq2, t - 3)
                act.activation(sq[0:r, :], h[0:r, t, :], ACT.Square, accum_out=st[0:r, 0, t:t + 1]).then_inc(ssq, 1)
                act.wait_ge(mean, t + 1)
                act.activation(st[0:r, 1, t:t + 1], st[0:r, 1, t:t + 1], ACT.Sqrt).then_inc(root, 1)

            def high_parts(t):
                r = rows(t)
                need(act, pp_full, t - 1)
                act.wait_ge(tpp_full, t + 1)
                act.activation(pTh[:, t % 2, :, 0:r], tpp[:, :, 0:r], ACT.Copy).then_inc(pTh_full, 1)
                act.wait_ge(uT_full, t + 1)
                act.activation(uTh[:, t % 2, :, 0:r], uT[:, :, 0:r], ACT.Copy).then_inc(uTh_full, 1)

            def gate_out(v):
                r = rows(v)
                need(act, h_full, 2 * (v - 1) - 1)
                for c in range(2):
                    act.wait_ge(gate_full, 2 * v + c + 1)
                    act.activation(sig[0:r, v % 2, c * C:(c + 1) * C], gate[0:r, c * C:(c + 1) * C], ACT.Sigmoid)\
                        .then_inc(sig_full, 1)
                act.wait_ge(pp_full, v + 1)
                act.activation(pps[0:r, v % 2, :], pp[0:r, :], ACT.Copy).then_inc(pps_full, 1)

            def last_root(v):
                r = rows(v)
                act.wait_ge(h_full, 2 * v + 2)
                act.wait_ge(ssq, min(v + 4, TT))
                act.activation(sq[0:r, :], h[0:r, v, :], ACT.Square, accum_out=st[0:r, 3, v:v + 1]).then_inc(ssq2, 1)
                act.wait_ge(mean2, v + 1)
                act.activation(st[0:r, 4, v:v + 1], st[0:r, 4, v:v + 1], ACT.Sqrt).then_inc(root2, 1)

            norm_root(0)
            high_parts(0)
            for n, (raw, _, high, _) in enumerate(pieces):
                act.wait_ge(piece_in[n], 16)
                act.activation(high, raw, ACT.Copy).then_inc(wh_full, 1)
                if n == 1:
                    norm_root(1)
            for t in range(1, TT + 2):
                if t < TT:
                    high_parts(t)
                if t + 1 < TT:
                    norm_root(t + 1)
                if t >= 2:
                    last_root(t - 2)
                if t <= TT:
                    gate_out(t - 1)

        @block.vector
        def _(dve):
            dve.wait_ge(gp_in, 16)

            def mixed(t):
                r = rows(t)
                dve.wait_ge(y_in[t % 2], 32 * (t // 2 + 1))
                for c in range(2):
                    dve.scalar_tensor_tensor(out=h[0:r, t, :], in0=y2[0:r, t % 2, c, :], scalar=wt[0:r, c, t:t + 1],
                                             in1=h[0:r, t, :], op0=ALU.mult, op1=ALU.add).then_inc(mix, 1)
                    dve.wait_ge(mix, 2 * t + c + 1)

            def normed(t):
                r = rows(t)
                dve.wait_ge(ssq, t + 1)
                dve.tensor_scalar(st[0:r, 1, t:t + 1], st[0:r, 0, t:t + 1], 1.0 / D, EPS, ALU.mult,
                                  ALU.add).then_inc(mean, 1)
                dve.wait_ge(root, t + 1)
                dve.reciprocal(st[0:r, 2, t:t + 1], st[0:r, 1, t:t + 1]).then_inc(inv, 1)
                dve.wait_ge(inv, t + 1)
                need(dve, tp_full, t - 1)
                dve.tensor_scalar(un[0:r, t % 2, :], h[0:r, t, :], st[0:r, 2, t:t + 1], None, ALU.mult)\
                    .then_inc(un_full, 1)

            def turned(t):
                r = rows(t)
                dve.wait_ge(tp_full, t + 1)
                need(dve, uTl_full, t)
                dve.tensor_tensor(uT[:, :, 0:r], tp[:, :, 0:r], gp[:, :].unsqueeze(2).to_broadcast([P, KD, r]),
                                  ALU.mult).then_inc(uT_full, 1)
                dve.wait_ge(pTh_full, t + 1)
                dve.tensor_tensor(pTl[:, t % 2, :, 0:r], tpp[:, :, 0:r], pTh[:, t % 2, :, 0:r], ALU.subtract)\
                    .then_inc(pTl_full, 1)
                dve.wait_ge(uTh_full, t + 1)
                dve.tensor_tensor(uTl[:, t % 2, :, 0:r], uT[:, :, 0:r], uTh[:, t % 2, :, 0:r], ALU.subtract)\
                    .then_inc(uTl_full, 1)

            def low_weights(n):
                raw, _, high, low = pieces[n]
                dve.wait_ge(wh_full, n + 1)
                dve.tensor_tensor(low, raw, high, ALU.subtract).then_inc(wl_full, 1)

            def gated(v):
                r = rows(v)
                dve.wait_ge(sig_full, 2 * v + 2)
                dve.wait_ge(pps_full, v + 1)
                need(dve, y_out[v % 2], 16 * (v // 2))
                dve.tensor_tensor(yo[0:r, v % 2, :], sig[0:r, v % 2, :], pps[0:r, v % 2, :], ALU.mult)\
                    .then_inc(h_full, 1)
                dve.wait_ge(h_full, 2 * v + 1)
                dve.tensor_tensor(h[0:r, v, :], h[0:r, v, :], yo[0:r, v % 2, :], ALU.add).then_inc(h_full, 1)

            def last_norm(v):
                r = rows(v)
                dve.wait_ge(ssq2, v + 1)
                dve.tensor_scalar(st[0:r, 4, v:v + 1], st[0:r, 3, v:v + 1], 1.0 / D, EPS, ALU.mult,
                                  ALU.add).then_inc(mean2, 1)
                dve.wait_ge(root2, v + 1)
                dve.reciprocal(st[0:r, 5, v:v + 1], st[0:r, 4, v:v + 1]).then_inc(inv2, 1)
                dve.wait_ge(inv2, v + 1)
                dve.scalar_tensor_tensor(out=yo[0:r, v % 2, :], in0=h[0:r, v, :], scalar=st[0:r, 5, v:v + 1],
                                         in1=gf[0:r, :], op0=ALU.mult, op1=ALU.mult).then_inc(yo_full, 1)

            mixed(0)
            normed(0)
            turned(0)
            mixed(1)
            low_weights(0)
            low_weights(1)
            normed(1)
            for n in range(2, NP):
                low_weights(n)
            dve.wait_ge(gf_in, 16)
            for t in range(1, TT + 2):
                if t < TT:
                    turned(t)
                if t + 1 < TT:
                    mixed(t + 1)
                if t >= 2:
                    gated(t - 2)
                if t + 1 < TT:
                    normed(t + 1)
                if t >= 2:
                    last_norm(t - 2)


def build(nc, g):
    ctx = ExitStack()
    with ctx:
        def dram(n, s, d=F32):
            return nc.dram_tensor(n, s, d, kind="Internal").ap()

        def sb(n, s, d=F32):
            return ctx.enter_context(nc.sbuf_tensor(n, s, d))

        g = dict(g)
        g["zT"] = dram("zT", (CHUNKS, P, NT))
        g["ztok"] = dram("ztok", (NT, QKV))
        g["u_kept"] = nc.dram_tensor("u_kept", (P, KD * NT), F32, kind="Internal").ap()
        g["gT"] = nc.dram_tensor("gT", (2 * KD, P, NT), F32, kind="Internal").ap()
        g["xs"] = nc.dram_tensor("xs", (SLOTS, D), F32, kind="Internal").ap()
        g["ys"] = nc.dram_tensor("ys", (SLOTS, D), F32, kind="Internal").ap()
        g["meta"] = nc.dram_tensor("meta", (P, 4), I32, kind="Internal").ap()
        g["ident"] = sb("ident", [P, P])
        g["ident_set"] = ctx.enter_context(nc.semaphore("ident_set"))
        g["pool_dma"] = [ctx.enter_context(nc.semaphore("pool_dma_" + n)) for n in (
            "ztok_out0", "ztok_out1", "rows_moved", "y_out0", "y_out1", "y_in0", "y_in1")]
        g["logit"] = sb("logit", [P, TT, NR])
        g["dest"] = sb("dest", [P, 2, TT], I32)
        g["wt"] = sb("wt", [P, 2, TT])
        g["meta_row"] = sb("meta_row", [1, 4 * P], I32)
        xp = g["x_prompt"].rearrange("b (t p) d -> (b t) p d", p=P)
        xs = g["x_sample"].rearrange("b s d -> (b s) d")
        x_of = lambda t: xp[t, :, :] if t < QT else xs
        pp = g["p_prompt"].rearrange("a b (t p) d -> (a b t) p d", p=P)
        psm = g["p_sample"].rearrange("a b s d -> (a b s) d")
        yp = g["out_y_prompt"].rearrange("b (t p) d -> (b t) p d", p=P)
        ysm = g["out_y_sample"].rearrange("b s d -> (b s) d")
        uh = nc.sbuf_tensor("uh", [P, KD, NT], F32R, side="right")
        g["uh"] = uh.__enter__()
        with nc.sbuf_tensor("u2", [P, TT, D], F32) as u2:
            g["u2"] = u2
            flat2 = u2[:, :, :].rearrange("p t d -> p (t d)")
            g["obT"] = flat2[:, 0:CB * NT].rearrange("p (k n) -> p k n", k=CB)
            g["oaT"] = flat2[:, CB * NT:(CB + 2) * NT].rearrange("p (k n) -> p k n", k=2)
            g["spare"] = flat2[:, (CB + 2) * NT:(CB + 4) * NT].rearrange("p (k n) -> p k n", k=2)
            g["spare_small"] = flat2[:, (CB + 4) * NT:TT * D]
            first = nc.free_semaphores[0]
            with nc.sbuf_tensor("u", [P, KD, NT], F32) as g["u"]:
                norm_in(nc, g, x_of)
                project(nc, g)
            stick(nc, g)
            second = nc.free_semaphores[0]
            clear(nc, range(first, second))
            dilated(nc, g)
            gates_and_decode(nc, g)
            clear(nc, range(second, nc.free_semaphores[0]))
            uh.__exit__(None, None, None)
            g["h"] = ctx.enter_context(nc.sbuf_tensor("h", [P, TT, D], F32, side="right"))
            with nc.sbuf_tensor("mT", [P, KD, NT], F32) as mT:
                g["mT"] = mT
                merge(nc, g)
                residual(nc, g, x_of)
            route(nc, g)
        experts(nc, g)
        finish(nc, g, lambda t: pp[t, :, :] if t < QT else psm, lambda t: yp[t, :, :] if t < QT else ysm)


_OUT = (("y_prompt", (1, SEQ, D)), ("y_sample", (DEC, 1, D)),
        ("win1_prompt", (1, 1, 128, 2, H_G, HD)), ("win1_sample", (1, DEC, 1, 2, H_G, HD)),
        ("win2_prompt", (1, 1, 512, 2, H_G, HD)), ("win2_sample", (1, DEC, 1, 2, H_G, HD)),
        ("win3_prompt", (1, 1, SEQ, 2, H_G, HD)), ("win3_sample", (1, DEC, 1, 2, H_G, HD)),
        ("sb_prompt", (1, 1, SEQ, 2, H_B, HD)), ("sb_sample", (1, DEC, 1, 2, H_B, HD)))


def kernel(**inputs):
    import numpy as _np
    import concourse.bacc as _bacc
    from concourse.bass_utils import run_bass_kernel_spmd as _run

    nc = _bacc.Bacc("TRN2", target_bir_lowering=False, num_devices=1)
    arrays, g = {}, {}
    for name, a in inputs.items():
        a = _np.ascontiguousarray(a)
        arrays[f"in_{name}"] = a
        g[name] = nc.dram_tensor(f"in_{name}", a.shape, mybir.dt.from_np(a.dtype), kind="ExternalInput").ap()
    outputs(nc, g)
    build(nc, g)
    r = _run(nc, [arrays], core_ids=[0])
    return tuple(r.results[0][f"out_{n}"] for n, _ in _OUT)


def outputs(nc, g):
    for n, shape in _OUT:
        ap = nc.dram_tensor(f"out_{n}", shape, F32, kind="ExternalOutput").ap()
        if n[0] == "y":
            g[f"out_{n}"] = ap
        else:
            g[f"out_{n}"] = ap.rearrange("a b s c h d -> (a b s) c (h d)")
```
